# Optimizing a Trainium2 kernel written in Bass

```python
import math
import jax, jax.numpy as jnp
from jax import lax
import numpy as np

D_MODEL = 1024
BATCH = 1
SEQ = 256
DEPTH = 1

MLA_HEADS = 16
MLA_Q_RANK = 256
MLA_KV_RANK = 256
MLA_NOPE_DIM = 64
MLA_ROPE_DIM = 32
MLA_QK_DIM = MLA_NOPE_DIM + MLA_ROPE_DIM
MLA_V_DIM = D_MODEL // MLA_HEADS
ROPE_THETA = 10000.0

DIFF_HEADS = 8
DIFF_QK_DIM = 64
DIFF_V_DIM = D_MODEL // DIFF_HEADS

N_EXPERTS = 16
CAPACITY_FACTOR = 2
EXPERT_FF = 2 * D_MODEL

Q_BLOCK = 128
EPS = 1e-6

IN_COLS = (
    MLA_Q_RANK,
    MLA_KV_RANK,
    MLA_ROPE_DIM,
    DIFF_HEADS * 2 * DIFF_QK_DIM,
    DIFF_HEADS * 2 * DIFF_QK_DIM,
    DIFF_HEADS * DIFF_V_DIM,
    D_MODEL,
    D_MODEL,
)
IN_WIDTH = sum(IN_COLS)


def _rms_norm(x, w):
    xf = x.astype(jnp.float32)
    y = xf * lax.rsqrt(jnp.mean(xf * xf, axis=-1, keepdims=True) + EPS)
    return (y * w.astype(jnp.float32)).astype(x.dtype)

def _split_columns(z):
    parts, start = [], 0
    for width in IN_COLS:
        parts.append(z[..., start:start + width])
        start += width
    return parts

def _rope_tables(positions):
    inv_freq = 1.0 / (ROPE_THETA ** (jnp.arange(0, MLA_ROPE_DIM, 2, dtype=jnp.float32) / MLA_ROPE_DIM))
    ang = positions.astype(jnp.float32)[..., None] * inv_freq
    return jnp.cos(ang)[:, :, None, :], jnp.sin(ang)[:, :, None, :]

def _apply_rope(x, cos, sin):
    half = x.shape[-1] // 2
    x1, x2 = x[..., :half], x[..., half:]
    c, s = cos.astype(x.dtype), sin.astype(x.dtype)
    return jnp.concatenate([x1 * c - x2 * s, x1 * s + x2 * c], axis=-1)

def _alibi_slopes(n_heads):
    return jnp.asarray([2.0 ** (-8.0 * (i + 1) / n_heads) for i in range(n_heads)], dtype=jnp.float32)

def _to_blocks(a, axis):
    t = a.shape[axis]
    new_shape = a.shape[:axis] + (t // Q_BLOCK, Q_BLOCK) + a.shape[axis + 1:]
    return jnp.moveaxis(a.reshape(new_shape), axis, 0)

def _from_blocks(o, axis):
    o = jnp.moveaxis(o, 0, axis)
    return o.reshape(o.shape[:axis] + (o.shape[axis] * o.shape[axis + 1],) + o.shape[axis + 2:])

def _mla_attention(q, k, v):
    scale = MLA_QK_DIM ** -0.5

    def block(qb):
        s = jnp.einsum('bhqd,bhkd->bhqk', qb, k).astype(jnp.float32) * scale
        p = jax.nn.softmax(s, axis=-1)
        return jnp.einsum('bhqk,bhkd->bhqd', p.astype(v.dtype), v)

    out = lax.map(block, _to_blocks(q, 2))
    return _from_blocks(out, 2)

def _diff_attention(q1, q2, k1, k2, v, lam, slopes, positions):
    scale = DIFF_QK_DIM ** -0.5

    def block(args):
        q1b, q2b, pb = args
        dist = jnp.abs(pb[:, :, None] - positions[:, None, :]).astype(jnp.float32)
        bias = -slopes[None, :, None, None] * dist[:, None, :, :]
        a1 = jax.nn.softmax(jnp.einsum('bhqd,bhkd->bhqk', q1b, k1).astype(jnp.float32) * scale + bias, axis=-1)
        a2 = jax.nn.softmax(jnp.einsum('bhqd,bhkd->bhqk', q2b, k2).astype(jnp.float32) * scale + bias, axis=-1)
        a = a1 - lam * a2
        return jnp.einsum('bhqk,bhkd->bhqd', a.astype(v.dtype), v)

    out = lax.map(block, (_to_blocks(q1, 2), _to_blocks(q2, 2), _to_blocks(positions, 1)))
    return _from_blocks(out, 2)

def _expert_choice_moe(h, router_w, w_gate, w_up, w_down):
    b, t, d = h.shape
    capacity = CAPACITY_FACTOR * t // N_EXPERTS
    logits = jnp.einsum('btd,de->bte', h, router_w).astype(jnp.float32)
    affinity = jax.nn.softmax(logits, axis=-1)
    gate, idx = lax.top_k(jnp.swapaxes(affinity, 1, 2), capacity)
    xe = jax.vmap(lambda hb, ib: hb[ib])(h, idx)
    hidden = jax.nn.silu(jnp.einsum('becd,edf->becf', xe, w_gate)) * jnp.einsum('becd,edf->becf', xe, w_up)
    ye = jnp.einsum('becf,efd->becd', hidden, w_down) * gate[..., None].astype(h.dtype)
    return jax.vmap(
        lambda ib, yb: jnp.zeros((t, d), yb.dtype).at[ib.reshape(-1)].add(yb.reshape(-1, d))
    )(idx, ye)

def _hybrid_layer(x, positions, layer_idx, attn_norm_w, w_in, b_gate,
                  mla_q_norm_w, mla_w_uq, mla_kv_norm_w, mla_w_ukv,
                  mla_q_hnorm_w, mla_k_hnorm_w,
                  diff_q_hnorm_w, diff_k_hnorm_w, diff_lambda, diff_subln_w,
                  w_out, ffn_norm_w, router_w, expert_w_gate, expert_w_up, expert_w_down):
    b, t, _ = x.shape

    h = _rms_norm(x, attn_norm_w)
    z = jnp.einsum('btd,dc->btc', h, w_in)
    c_q, c_kv, k_rope, dq, dk, dv, g_mla, g_diff = _split_columns(z)

    cos, sin = _rope_tables(positions)
    q = jnp.einsum('btr,rc->btc', _rms_norm(c_q, mla_q_norm_w), mla_w_uq).reshape(b, t, MLA_HEADS, MLA_QK_DIM)
    kv = jnp.einsum('btr,rc->btc', _rms_norm(c_kv, mla_kv_norm_w), mla_w_ukv).reshape(
        b, t, MLA_HEADS, MLA_NOPE_DIM + MLA_V_DIM)
    k_nope, v_mla = kv[..., :MLA_NOPE_DIM], kv[..., MLA_NOPE_DIM:]
    k_r = jnp.broadcast_to(k_rope[:, :, None, :], (b, t, MLA_HEADS, MLA_ROPE_DIM))
    k = jnp.concatenate([k_nope, k_r], axis=-1)
    q = _rms_norm(q, mla_q_hnorm_w)
    k = _rms_norm(k, mla_k_hnorm_w)
    q = jnp.concatenate([q[..., :MLA_NOPE_DIM], _apply_rope(q[..., MLA_NOPE_DIM:], cos, sin)], axis=-1)
    k = jnp.concatenate([k[..., :MLA_NOPE_DIM], _apply_rope(k[..., MLA_NOPE_DIM:], cos, sin)], axis=-1)
    o_mla = _mla_attention(q.transpose(0, 2, 1, 3), k.transpose(0, 2, 1, 3), v_mla.transpose(0, 2, 1, 3))
    o_mla = o_mla.transpose(0, 2, 1, 3).reshape(b, t, D_MODEL)

    qd = _rms_norm(dq.reshape(b, t, DIFF_HEADS, 2, DIFF_QK_DIM), diff_q_hnorm_w)
    kd = _rms_norm(dk.reshape(b, t, DIFF_HEADS, 2, DIFF_QK_DIM), diff_k_hnorm_w)
    qd = qd.transpose(0, 2, 3, 1, 4)
    kd = kd.transpose(0, 2, 3, 1, 4)
    vd = dv.reshape(b, t, DIFF_HEADS, DIFF_V_DIM).transpose(0, 2, 1, 3)
    lam_init = 0.8 - 0.6 * math.exp(-0.3 * layer_idx)
    lf = diff_lambda.astype(jnp.float32)
    lam = jnp.exp(jnp.sum(lf[0] * lf[1])) - jnp.exp(jnp.sum(lf[2] * lf[3])) + lam_init
    o_diff = _diff_attention(qd[:, :, 0], qd[:, :, 1], kd[:, :, 0], kd[:, :, 1], vd, lam,
                             _alibi_slopes(DIFF_HEADS), positions)
    o_diff = _rms_norm(o_diff, diff_subln_w) * (1.0 - lam_init)
    o_diff = o_diff.transpose(0, 2, 1, 3).reshape(b, t, D_MODEL)

    gate_a = jax.nn.sigmoid(g_mla + b_gate[:D_MODEL])
    gate_b = jax.nn.sigmoid(g_diff + b_gate[D_MODEL:])
    merged = gate_a * o_mla + gate_b * o_diff
    x = x + jnp.einsum('btc,cd->btd', merged, w_out)

    h2 = _rms_norm(x, ffn_norm_w)
    return x + _expert_choice_moe(h2, router_w, expert_w_gate, expert_w_up, expert_w_down)

def first_inputs(seed: int = 0) -> dict:
    key = jax.random.key(seed)
    ks = jax.random.split(key, 24)
    f32 = jnp.float32

    def normal(k, shape, fan_in):
        return jax.random.normal(k, shape, f32) * (fan_in ** -0.5)

    def gain(k, shape):
        return 1.0 + 0.02 * jax.random.normal(k, shape, f32)

    x = jax.random.normal(ks[0], (BATCH, SEQ, D_MODEL), f32)
    offsets = jax.random.randint(ks[1], (BATCH, 1), 0, 1024, dtype=jnp.int32)
    positions = offsets + jnp.arange(SEQ, dtype=jnp.int32)[None, :]
    return {
        "x": x,
        "positions": positions,
        "attn_norm_w": gain(ks[2], (DEPTH, D_MODEL)),
        "w_in": normal(ks[3], (DEPTH, D_MODEL, IN_WIDTH), D_MODEL),
        "b_gate": 0.02 * jax.random.normal(ks[4], (DEPTH, 2 * D_MODEL), f32),
        "mla_q_norm_w": gain(ks[5], (DEPTH, MLA_Q_RANK)),
        "mla_w_uq": normal(ks[6], (DEPTH, MLA_Q_RANK, MLA_HEADS * MLA_QK_DIM), MLA_Q_RANK),
        "mla_kv_norm_w": gain(ks[7], (DEPTH, MLA_KV_RANK)),
        "mla_w_ukv": normal(ks[8], (DEPTH, MLA_KV_RANK, MLA_HEADS * (MLA_NOPE_DIM + MLA_V_DIM)), MLA_KV_RANK),
        "mla_q_hnorm_w": gain(ks[9], (DEPTH, MLA_QK_DIM)),
        "mla_k_hnorm_w": gain(ks[10], (DEPTH, MLA_QK_DIM)),
        "diff_q_hnorm_w": gain(ks[11], (DEPTH, DIFF_QK_DIM)),
        "diff_k_hnorm_w": gain(ks[12], (DEPTH, DIFF_QK_DIM)),
        "diff_lambda": 0.1 * jax.random.normal(ks[13], (DEPTH, 4, DIFF_QK_DIM), f32),
        "diff_subln_w": gain(ks[14], (DEPTH, DIFF_V_DIM)),
        "w_out": normal(ks[15], (DEPTH, D_MODEL, D_MODEL), D_MODEL),
        "ffn_norm_w": gain(ks[16], (DEPTH, D_MODEL)),
        "router_w": normal(ks[17], (DEPTH, D_MODEL, N_EXPERTS), D_MODEL),
        "expert_w_gate": normal(ks[18], (DEPTH, N_EXPERTS, D_MODEL, EXPERT_FF), D_MODEL),
        "expert_w_up": normal(ks[19], (DEPTH, N_EXPERTS, D_MODEL, EXPERT_FF), D_MODEL),
        "expert_w_down": normal(ks[20], (DEPTH, N_EXPERTS, EXPERT_FF, D_MODEL), EXPERT_FF),
    }

def first_block(x, positions, attn_norm_w, w_in, b_gate, mla_q_norm_w, mla_w_uq, mla_kv_norm_w,
              mla_w_ukv, mla_q_hnorm_w, mla_k_hnorm_w, diff_q_hnorm_w, diff_k_hnorm_w,
              diff_lambda, diff_subln_w, w_out, ffn_norm_w, router_w,
              expert_w_gate, expert_w_up, expert_w_down):
    for l in range(DEPTH):
        x = _hybrid_layer(
            x, positions, l, attn_norm_w[l], w_in[l], b_gate[l],
            mla_q_norm_w[l], mla_w_uq[l], mla_kv_norm_w[l], mla_w_ukv[l],
            mla_q_hnorm_w[l], mla_k_hnorm_w[l],
            diff_q_hnorm_w[l], diff_k_hnorm_w[l], diff_lambda[l], diff_subln_w[l],
            w_out[l], ffn_norm_w[l], router_w[l],
            expert_w_gate[l], expert_w_up[l], expert_w_down[l])
    return x


HEAD_DIM = 64
CONV_HEADS = 4
ATTN_HEADS = 8
SGU_HEADS = 4
CONV_W = CONV_HEADS * HEAD_DIM
ATTN_W = ATTN_HEADS * HEAD_DIM
SGU_W = SGU_HEADS * HEAD_DIM
D_MIX = CONV_W + ATTN_W + SGU_W
D_IN_PROJ = 3 * CONV_W + 3 * ATTN_W + 2 * SGU_W
CONV_WIDTH = 3
CHUNK = 128
D_FF = 4 * D_MODEL
PLE_DIM = 256


def rms_norm(x, g):
    xf = x.astype(jnp.float32)
    y = xf * lax.rsqrt(jnp.mean(xf * xf, axis=-1, keepdims=True) + EPS)
    return (y * g.astype(jnp.float32)).astype(x.dtype)

def short_conv(x, w):
    s = x.shape[1]
    xp = jnp.pad(x, ((0, 0), (CONV_WIDTH - 1, 0), (0, 0)))
    out = w[0] * xp[:, 0:s]
    for j in range(1, CONV_WIDTH):
        out = out + w[j] * xp[:, j:j + s]
    return out

def stick_breaking_attention(q, k, v):
    s_len = q.shape[1]
    scale = HEAD_DIM ** -0.5
    outs = []
    for qb in range(s_len // Q_BLOCK):
        start = qb * Q_BLOCK
        end = start + Q_BLOCK
        qi = q[:, start:end].astype(jnp.float32)
        kj = k[:, :end].astype(jnp.float32)
        vj = v[:, :end].astype(jnp.float32)
        z = jnp.einsum('bqhd,bkhd->bhqk', qi, kj) * scale
        t_pos = start + jnp.arange(Q_BLOCK)[:, None]
        s_pos = jnp.arange(end)[None, :]
        causal = s_pos < t_pos
        log_beta = jax.nn.log_sigmoid(z)
        log_rem = jnp.where(causal, jax.nn.log_sigmoid(-z), 0.0)
        suffix = lax.cumsum(log_rem, axis=3, reverse=True) - log_rem
        weights = jnp.where(causal, jnp.exp(log_beta + suffix), 0.0)
        o = jnp.einsum('bhqk,bkhd->bqhd', weights, vj)
        outs.append(o.astype(v.dtype))
    return jnp.concatenate(outs, axis=1)

def spatial_gating(u, v, g_v, w_s, b_s):
    bsz, s_len, _ = u.shape
    v = v.reshape(bsz, s_len, SGU_HEADS, HEAD_DIM)
    v = rms_norm(v, g_v.reshape(SGU_HEADS, HEAD_DIM))
    v = v.reshape(bsz, s_len // CHUNK, CHUNK, SGU_HEADS, HEAD_DIM)
    mask = jnp.tril(jnp.ones((CHUNK, CHUNK), dtype=w_s.dtype))
    w = w_s * mask
    sv = jnp.einsum('gts,bcsge->bctge', w, v) + b_s.T[:, :, None]
    return u * sv.reshape(bsz, s_len, SGU_W)

def second_inputs(seed: int = 0) -> dict:
    key = jax.random.key(seed)
    ks = jax.random.split(key, 17)

    def nrm(k, shape, scale):
        return jax.random.normal(k, shape, jnp.float32) * scale

    def gain(k, shape):
        return 1.0 + 0.05 * jax.random.normal(k, shape, jnp.float32)

    return {
        "x": nrm(ks[0], (BATCH, SEQ, D_MODEL), 1.0),
        "p": nrm(ks[1], (DEPTH, BATCH, SEQ, PLE_DIM), 1.0),
        "norm1_g": gain(ks[2], (DEPTH, D_MODEL)),
        "w_in": nrm(ks[3], (DEPTH, D_MODEL, D_IN_PROJ), D_MODEL ** -0.5),
        "conv_w": nrm(ks[4], (DEPTH, CONV_WIDTH, CONV_W), CONV_WIDTH ** -0.5),
        "q_norm_g": gain(ks[5], (DEPTH, HEAD_DIM)),
        "k_norm_g": gain(ks[6], (DEPTH, HEAD_DIM)),
        "sgu_norm_g": gain(ks[7], (DEPTH, SGU_W)),
        "sgu_w": nrm(ks[8], (DEPTH, SGU_HEADS, CHUNK, CHUNK), CHUNK ** -0.5),
        "sgu_b": gain(ks[9], (DEPTH, SGU_HEADS, CHUNK)),
        "w_out": nrm(ks[10], (DEPTH, D_MIX, D_MODEL), D_MIX ** -0.5),
        "norm2_g": gain(ks[11], (DEPTH, D_MODEL)),
        "w_ff1": nrm(ks[12], (DEPTH, D_MODEL, D_FF), D_MODEL ** -0.5),
        "w_ff2": nrm(ks[13], (DEPTH, D_FF, D_MODEL), D_FF ** -0.5),
        "norm3_g": gain(ks[14], (DEPTH, D_MODEL)),
        "w_ple_gate": nrm(ks[15], (DEPTH, D_MODEL, D_MODEL), D_MODEL ** -0.5),
        "w_ple_proj": nrm(ks[16], (DEPTH, PLE_DIM, D_MODEL), PLE_DIM ** -0.5),
    }

def second_block(x, p, norm1_g, w_in, conv_w, q_norm_g, k_norm_g, sgu_norm_g, sgu_w, sgu_b,
              w_out, norm2_g, w_ff1, w_ff2, norm3_g, w_ple_gate, w_ple_proj):
    bsz, s_len, _ = x.shape
    split_idx = list(np.cumsum([CONV_W, CONV_W, CONV_W, ATTN_W, ATTN_W, ATTN_W, SGU_W]))
    h = x
    for i in range(DEPTH):
        hn = rms_norm(h, norm1_g[i])
        proj = hn @ w_in[i]
        a_b, a_c, a_h, q, k, v, c_u, c_v = jnp.split(proj, split_idx, axis=-1)
        y_a = a_b * short_conv(a_c * a_h, conv_w[i])
        q = rms_norm(q.reshape(bsz, s_len, ATTN_HEADS, HEAD_DIM), q_norm_g[i])
        k = rms_norm(k.reshape(bsz, s_len, ATTN_HEADS, HEAD_DIM), k_norm_g[i])
        v = v.reshape(bsz, s_len, ATTN_HEADS, HEAD_DIM)
        y_b = stick_breaking_attention(q, k, v).reshape(bsz, s_len, ATTN_W)
        y_c = spatial_gating(jax.nn.gelu(c_u, approximate=False),
                             jax.nn.gelu(c_v, approximate=False),
                             sgu_norm_g[i], sgu_w[i], sgu_b[i])
        h = h + jnp.concatenate([y_a, y_b, y_c], axis=-1) @ w_out[i]
        f = jnp.square(jax.nn.relu(rms_norm(h, norm2_g[i]) @ w_ff1[i]))
        h = h + f @ w_ff2[i]
        gate = jax.nn.sigmoid(rms_norm(h, norm3_g[i]) @ w_ple_gate[i])
        h = h + gate * (p[i] @ w_ple_proj[i])
    return h


def setup_inputs(seed=0):
    out = dict(first_inputs(seed))
    for name, value in second_inputs(seed + 1).items():
        if name != "x":
            out[name + "_2"] = value
    return out


def reference(
    x, positions, attn_norm_w, w_in, b_gate, mla_q_norm_w, mla_w_uq, mla_kv_norm_w, mla_w_ukv,
    mla_q_hnorm_w, mla_k_hnorm_w, diff_q_hnorm_w, diff_k_hnorm_w, diff_lambda, diff_subln_w,
    w_out, ffn_norm_w, router_w, expert_w_gate, expert_w_up, expert_w_down, p_2, norm1_g_2,
    w_in_2, conv_w_2, q_norm_g_2, k_norm_g_2, sgu_norm_g_2, sgu_w_2, sgu_b_2, w_out_2,
    norm2_g_2, w_ff1_2, w_ff2_2, norm3_g_2, w_ple_gate_2, w_ple_proj_2,
):
    x = first_block(
        x, positions, attn_norm_w, w_in, b_gate, mla_q_norm_w, mla_w_uq, mla_kv_norm_w,
        mla_w_ukv, mla_q_hnorm_w, mla_k_hnorm_w, diff_q_hnorm_w, diff_k_hnorm_w, diff_lambda,
        diff_subln_w, w_out, ffn_norm_w, router_w, expert_w_gate, expert_w_up, expert_w_down,
    )
    return second_block(
        x, p_2, norm1_g_2, w_in_2, conv_w_2, q_norm_g_2, k_norm_g_2, sgu_norm_g_2, sgu_w_2,
        sgu_b_2, w_out_2, norm2_g_2, w_ff1_2, w_ff2_2, norm3_g_2, w_ple_gate_2, w_ple_proj_2,
    )


_drawn_inputs = setup_inputs


def setup_inputs(seed=0):
    import zlib

    import numpy as np

    out = dict(_drawn_inputs(seed))
    spreads = {}
    factors = {'b_gate': 6.916,
     'mla_q_norm_w': 8.0,
     'mla_kv_norm_w': 8.0,
     'mla_q_hnorm_w': 8.0,
     'mla_k_hnorm_w': 8.0,
     'diff_q_hnorm_w': 3.999,
     'diff_k_hnorm_w': 4.744,
     'diff_lambda': 4.988,
     'diff_subln_w': 4.263,
     'ffn_norm_w': 3.595,
     'q_norm_g_2': 112.314,
     'k_norm_g_2': 200.0,
     'sgu_norm_g_2': 42.639,
     'sgu_b_2': 32.473,
     'norm3_g_2': 200.0,
     'norm2_g_2': 6.393,
     'p_2': 4.335,
     'w_ple_gate_2': 6.155,
     'w_ple_proj_2': 4.344}
    for name, (base, spread) in spreads.items():
        noise = np.random.default_rng([zlib.crc32(name.encode()), seed]).standard_normal(out[name].shape)
        drawn = base * np.exp(spread * noise) if base else spread * noise
        out[name] = __import__('jax').numpy.asarray(drawn.astype(out[name].dtype))
    for name, factor in factors.items():
        out[name] = (out[name] * factor).astype(out[name].dtype)
    return out
```

```python
from contextlib import ExitStack
import math

import concourse.bass as bass
import concourse.mybir as mybir

F32 = mybir.dt.float32
I32 = mybir.dt.int32
ALU = mybir.AluOpType
ACT = mybir.ActivationFunctionType
AX = mybir.AxisListType.X

P = 128
T = 256
HALVES = T // P
D = 1024
KT = D // P
EPS = 1e-6

HEADS, QK, NOPE, ROPE, VD = 16, 96, 64, 32, 64
HR = ROPE // 2
RANK = 256
RT = RANK // P
C_COLS = 2 * RANK + ROPE
THETA = 10000.0
DHEADS, DQK, DV = 8, 64, 128
LAM_INIT = 0.8 - 0.6 * math.exp(-0.3 * 0)

EXPERTS, CAP, FF = 16, 32, 2048
FCOL = FF // 4
DCOL = D // 4

CONV, CONVW = 256, 3
SHEADS, SHD = 8, 64
SATT = SHEADS * SHD
SGU, SG = 256, 4
DFF = 4096
PLE = 256

SLOTS, SLOT = 8, 2048
EXPERT_CHUNKS = 3 * KT
assert EXPERT_CHUNKS % SLOTS == 0

VEC_ROWS = [("attn_norm_w", 8), ("mla_q_norm_w", 2), ("mla_kv_norm_w", 2), ("ffn_norm_w", 8), ("norm1_g_2", 8),
            ("norm2_g_2", 8), ("norm3_g_2", 8), ("conv_w_2", 6), ("sgu_b_2", 4)]
VEC = {}
for _name, _rows in VEC_ROWS:
    VEC[_name] = sum(r for _, r in VEC_ROWS[:len(VEC)])
NVEC = sum(r for _, r in VEC_ROWS)

ROW_VECS = [("mla_q_hnorm_w", QK), ("mla_k_hnorm_w", QK), ("diff_q_hnorm_w", DQK), ("diff_k_hnorm_w", DQK),
            ("diff_subln_w", DV), ("q_norm_g_2", SHD), ("k_norm_g_2", SHD), ("sgu_norm_g_2", SGU),
            ("diff_lambda", 4 * DQK)]
ROW = {}
for _name, _n in ROW_VECS:
    ROW[_name] = sum(n for _, n in ROW_VECS[:len(ROW)])
NROW = sum(n for _, n in ROW_VECS)

INV_FREQ = [1.0 / THETA ** (2 * i / ROPE) for i in range(HR)]
TWO_PI_PARTS = (6.28125, 0.0019350051879882812, 3.0199157663446332e-07)
ROUND = 1.5 * 2.0 ** 23
PI_BELOW = 3.1415925
RSQRT_MAGIC = float(0x5F3759DF)


def hybrid_blocks(nc, t):
    ctx = ExitStack()
    with ctx:
        def sb(name, shape, dt=F32):
            return ctx.enter_context(nc.sbuf_tensor(name, shape, dt))

        def sem(name):
            return ctx.enter_context(nc.semaphore(name))

        ring = sb("ring", [P, SLOTS, SLOT])
        xs = sb("xs", [P, HALVES, D])
        xn = sb("xn", [P, HALVES, D])
        hT = sb("hT", [P, KT, T])
        ident = sb("ident", [P, P])
        ones = sb("ones", [P, P])
        later = sb("later", [P, P])
        tri = sb("tri", [P, P])
        tril = sb("tril", [P, P])
        slot_ids = sb("slot_ids", [P, P])
        vec_rows = sb("vec_rows", [NVEC, P])
        vec = sb("vec", [P, NVEC])
        row = sb("row", [P, NROW])
        wsT = sb("wsT", [P, SG, P])
        pT = sb("pT", [P, PLE // P, T])
        router = sb("router", [P, KT, EXPERTS])
        stat = sb("stat", [P, 384])
        arena = sb("arena", [P, 26 * 1024])
        ps = ctx.enter_context(nc.psum_tensor("ps", [P, 8, 512], F32))
        psf = ps[:, :, :].rearrange("p b n -> p (b n)")

        def at(off, *shape):
            n = math.prod(shape)
            v = arena[:, off:off + n]
            names = "abcd"[:len(shape)]
            if len(shape) > 1:
                v = v.rearrange(f"p ({' '.join(names)}) -> p {' '.join(names)}", **dict(zip(names, shape)))
            return v

        K = 1024
        dq = at(0, HALVES, D)
        dk = at(2 * K, HALVES, D)
        dv = at(4 * K, HALVES, D)
        q = at(6 * K, HALVES, HEADS * QK)
        kv = at(9 * K, HALVES, HEADS * 128)
        kf = at(13 * K, HALVES, HEADS * QK)
        ga = at(16 * K, HALVES, D)
        gb = at(18 * K, HALVES, D)
        c_sb = at(20 * K, HALVES, C_COLS)
        cT = at(20 * K + 1152, 2, RT, T)
        bgate = at(22 * K + 128, 2 * D)
        scores = [at(22 * K + 128 + i * K, 4, T) for i in range(2)]
        sgu_in = at(22 * K + 128, SG, P)
        p_in = at(22 * K + 640, HALVES, PLE)
        qkT = [at(20 * K + i * 512, 512) for i in range(2)]
        pt_sb = [at(21 * K + 128 + i * 512, 2, T) for i in range(2)]
        dist = at(24 * K + 256, HALVES, T)
        trig = at(24 * K + 768, 6, HALVES * HR)
        posb = at(24 * K + 960, 4, T)
        rope_t = [at(20 * K, HALVES, HEADS, HR), at(20 * K + 512, HALVES, HEADS, HR)]
        posi = at(6 * K, 3, T).bitcast(I32)
        kr = at(25 * K + 960, HALVES, ROPE)
        onehot = at(0, HALVES, EXPERTS * CAP)
        xT_all = at(1 * K, KT, EXPERTS * CAP)
        xe = at(5 * K, KT, CAP)
        hid_g = at(5 * K + 256, FCOL)
        hid = at(5 * K + 768, FCOL)
        hidT = at(6 * K + 256, 4, P)
        gated = at(6 * K + 768, HALVES, P)
        scat = at(7 * K, T)
        ye = at(7 * K + 256, DCOL)
        logit = at(7 * K + 512, HALVES, EXPERTS)
        aff = at(7 * K + 576, HALVES, EXPERTS)
        slot_t = at(7 * K + 640, HALVES, EXPERTS)
        routing = at(8 * K, 6, T)[0:EXPERTS]
        a_bT = at(0, 2, T)
        a_hT = at(512, 2, T)
        conv = at(1 * K, 2, T + CONVW - 1)
        conv_y = at(1 * K + 520, T)
        yT = at(2 * K, KT, T)
        qk2 = at(4 * K, HALVES, 2 * SATT)
        v2 = at(6 * K, HALVES, SATT)
        u2 = at(7 * K, HALVES, SGU)
        cv2 = at(7 * K + 512, HALVES, SGU)
        qkT2 = at(8 * K, SATT // P, 512)
        SC = 384
        na = [at(10 * K + i * SC, SC) for i in range(2)]
        spl = [at(11 * K + i * SC, SC) for i in range(2)]
        lb = [at(off, SC) for off in (12 * K, 12 * K + SC, 14 * K + 512)]
        lr = [at(13 * K + i * SC, SC) for i in range(2)]
        yc = at(14 * K, HALVES, SGU)
        fT = at(15 * K, DFF // P, T)
        gate2 = at(0, HALVES, D)
        out_sb = at(2 * K, HALVES, D)
        sq = xn[:, :, :].rearrange("p h d -> p (h d)")

        ss_x, rstd_x = stat[:, 0:2], stat[:, 2:4]
        ss_c, rstd_c = stat[:, 4:8], stat[:, 8:12]
        ss_h, rstd_h = stat[:, 16:48], stat[:, 48:80]
        mxn = [stat[:, 80 + 4 * i:84 + 4 * i] for i in range(2)]
        sums = [stat[:, 88 + 4 * i:92 + 4 * i] for i in range(2)]
        rec = [stat[:, 96 + 4 * i:100 + 4 * i] for i in range(2)]
        lam, lam_s = stat[:, 104:105], stat[:, 106:108]
        freq = stat[:, 108:124]
        posc_f = stat[:, 128:136]
        nw = [stat[:, 136 + 32 * i:168 + 32 * i] for i in range(3)]
        ss_kr = stat[:, 232:234]
        rstd_k = stat[:, 240:272]
        ss_o, rstd_o = stat[:, 272:288], stat[:, 288:304]
        rmax, rsum, rinv = stat[:, 304:306], stat[:, 306:308], stat[:, 308:310]
        rstd_0 = stat[:, 310:312]
        posc = sb("posc", [P, HALVES, 3], I32)
        top8 = sb("top8", [EXPERTS, 4, 8])
        rcount = sb("rcount", [EXPERTS, 2])

        slot_loaded = [sem(f"slot_loaded{i}") for i in range(SLOTS)]
        chunk_used = sem("chunk_used")
        x_loaded, small_loaded = sem("x_loaded"), sem("small_loaded")
        gate_bias_loaded = sem("gate_bias_loaded")
        masks_ready = sem("masks_ready")
        vec_done, vec_ready = sem("vec_done"), sem("vec_ready")
        pw_done, pw_ready = sem("pw_done"), sem("pw_ready")
        tr_done, tr_dve, tr_act = sem("tr_done"), sem("tr_dve"), sem("tr_act")
        sq_act, rstd_ready = sem("sq_act"), sem("rstd_ready")
        xn_dve, xn_act, x_ready = sem("xn_dve"), sem("xn_act"), sem("x_ready")
        block_dve, block_act = sem("block_dve"), sem("block_act")
        sq_ready, sq_read = sem("sq_ready"), sem("sq_read")
        c_sq, c_norm, cT_done, cT_dve = sem("c_sq"), sem("c_norm"), sem("cT_done"), sem("cT_dve")
        dqk_ready, qk_ready = sem("dqk_ready"), sem("qk_ready")
        lam_in, lam_exp = sem("lam_in"), sem("lam_exp")
        angle_ready, trig_ready = sem("angle_ready"), sem("trig_ready")
        gate_in, gate_ready = sem("gate_in"), sem("gate_ready")
        hT_done, hT_evac, hS_done, hS_read = sem("hT_done"), sem("hT_evac"), sem("hS_done"), sem("hS_read")
        max_ready, exp_done, prob_ready = sem("max_ready"), sem("exp_done"), sem("prob_ready")
        hP_done, hP_evac, hO_done, hO_evac = sem("hP_done"), sem("hP_evac"), sem("hO_done"), sem("hO_evac")
        od_sums, od_root, od_ready, merged_ready = sem("od_sums"), sem("od_root"), sem("od_ready"), sem("merged_ready")
        logit_done, rmax_ready, rexp_done, aff_ready = sem("logit_done"), sem("rmax_ready"), sem("rexp_done"), sem("aff_ready")
        affT_done, slot_done, slotT_done, onehot_ready = sem("affT_done"), sem("slot_done"), sem("slotT_done"), sem("onehot_ready")
        gather_done, gather_dve, gather_act = sem("gather_done"), sem("gather_dve"), sem("gather_act")
        xe_ready, silu_done, hid_ready = sem("xe_ready"), sem("silu_done"), sem("hid_ready")
        hidT_done, hidT_ready, ye_ready = sem("hidT_done"), sem("hidT_ready"), sem("ye_ready")
        gated_ready, scat_done, scat_ready = sem("gated_ready"), sem("scat_done"), sem("scat_ready")
        e_scatter, moe_added = sem("e_scatter"), sem("moe_added")
        a_act, a_dve, conv_ready = sem("a_act"), sem("a_dve"), sem("conv_ready")
        gelu_done, v_ready = sem("gelu_done"), sem("v_ready")
        qk2_ready, qkT2_done, qkT2_evac = sem("qk2_ready"), sem("qkT2_done"), sem("qkT2_evac")
        z_done, sp_ready, lr_ready = sem("z_done"), sem("sp_ready"), sem("lr_ready")
        suf_done, arg_ready, w_exp, w_ready = sem("suf_done"), sem("arg_ready"), sem("w_exp"), sem("w_ready")
        yb_done, yb_evac = sem("yb_done"), sem("yb_evac")
        cv_ready, sv_done, yc_ready, ycT_done, ycT_evac = sem("cv_ready"), sem("sv_done"), sem("yc_ready"), sem("ycT_done"), sem("ycT_evac")
        f_relu, f_ready = sem("f_relu"), sem("f_ready")
        gate2_ready, out_ready, out_stored = sem("gate2_ready"), sem("out_ready"), sem("out_stored")
        dve_step, act_step, pool_step = sem("dve_step"), sem("act_step"), sem("pool_step")

        def two_tiles(w, k0, c0, cols):
            return w[2 * k0 * P:(2 * k0 + 2) * P, c0:c0 + cols].rearrange("(k p) c -> p k c", p=P)

        def tiles(name, c0, cols, rows=D):
            return [two_tiles(t[name][0], k, c0, cols) for k in range(rows // (2 * P))]

        w_in_cols = [(0, C_COLS)] + [(C_COLS + i * D, D) for i in range(5)]
        first_blocks = ([tiles("w_in", *w_in_cols[i]) for i in range(4)]
                        + [tiles("mla_w_uq", i * 768, 768, RANK) for i in range(2)]
                        + [tiles("mla_w_ukv", i * 1024, 1024, RANK) for i in range(2)]
                        + [tiles("w_in", *w_in_cols[i]) for i in (4, 5)]
                        + [tiles("w_out", 0, D)])
        second_blocks = ([tiles("w_in_2", 0, 768), tiles("w_in_2", 768, 1024), tiles("w_in_2", 1792, 1024)]
                         + [tiles("w_out_2", 0, D)]
                         + [tiles("w_ff1_2", i * D, D) for i in range(4)]
                         + [tiles("w_ff2_2", 0, D, DFF)]
                         + [tiles("w_ple_proj_2", 0, D, PLE)]
                         + [tiles("w_ple_gate_2", 0, D)])
        n_first = sum(len(b) for b in first_blocks)
        second_base = n_first + EXPERTS * EXPERT_CHUNKS
        NAMES = ["c", "dq", "dk", "dv", "uq0", "uq1", "ukv0", "ukv1", "gate_a", "gate_b", "out",
                 "conv", "qk2", "vuv", "out2", "up0", "up1", "up2", "up3", "down", "proj", "gate2"]
        FIRST, DONE, n = {}, {}, 0
        for name, blk in zip(NAMES, first_blocks + second_blocks):
            if name == "conv":
                n = second_base
            FIRST[name], n = n, n + len(blk)
            DONE[name] = n
        SETS = dict(zip(NAMES, "BABABABABA" + "B" + "BABB" + "BABA" + "BAB"))

        def slot_view(i, cols):
            return ring[:, i % SLOTS, 0:2 * cols].rearrange("p (k c) -> p k c", k=2)

        def landed(i):
            return 16 * (i // SLOTS + 1)

        SET = {"A": 0, "B": 4}

        def pset(s, h, n=D):
            return psf[:, 512 * SET[s] + h * D:512 * SET[s] + h * D + n]

        block = ctx.enter_context(nc.Block())

        @block.sync
        def _(sp):
            x_dram = t["x"][0].rearrange("(h p) d -> p h d", p=P)
            sp.dma_start(xs[:, :, :], x_dram).then_inc(x_loaded, 16)

            def load(i, src):
                if i >= SLOTS:
                    sp.wait_ge(chunk_used, i - SLOTS + 1)
                sp.dma_start(slot_view(i, src.shape[2]), src).then_inc(slot_loaded[i % SLOTS], 16)

            i = 0
            for blk in first_blocks:
                for src in blk:
                    load(i, src)
                    i += 1
            with sp.Fori(0, EXPERTS) as e:
                for k in range(EXPERT_CHUNKS):
                    m, kt = k // KT, k % KT
                    if m < 2:
                        w = t["expert_w_gate" if m == 0 else "expert_w_up"]
                        src = w[0, e, kt * P:(kt + 1) * P, :]
                        dst = ring[:, (n_first + k) % SLOTS, :]
                    else:
                        src = t["expert_w_down"][0, e, 2 * kt * P:(2 * kt + 2) * P, :].rearrange("(k p) c -> p k c", p=P)
                        dst = slot_view(n_first + k, D)
                    sp.wait_ge(chunk_used, EXPERT_CHUNKS * e + n_first + k - SLOTS + 1)
                    sp.dma_start(dst, src).then_inc(slot_loaded[(n_first + k) % SLOTS], 16)
            i = second_base
            for blk in second_blocks:
                for src in blk:
                    load(i, src)
                    i += 1
            for h in range(HALVES):
                sp.wait_ge(out_ready, h + 1)
                sp.dma_start(t["out"][0, h * P:(h + 1) * P, :], out_sb[:, h, :]).then_inc(out_stored, 16)
            sp.wait_ge(out_stored, 16 * HALVES)

        N_SMALL = len(VEC_ROWS) + len(ROW_VECS) + 6
        N_MASKS = 7
        STAGES = ["attn", "merge", "ffn", "mix", "ff", "ple"]

        @block.gpsimd
        def _(pool):
            count = [0]

            def step(ins):
                count[0] += 1
                ins.then_inc(pool_step, 1)
                pool.wait_ge(pool_step, count[0])

            def mask(buf, fill_in, fill_out, op, pattern, mult):
                step(pool.memset(buf[:, :], fill_in))
                pool.affine_select(out=buf[:, :], in_=buf[:, :], compare_op=op, fill=fill_out, base=0,
                                   pattern=pattern, channel_multiplier=mult).then_inc(masks_ready, 1)

            mask(ident, 0.0, 1.0, ALU.not_equal, [[-1, P]], 1)
            mask(tril, 1.0, 0.0, ALU.is_ge, [[1, P]], -1)
            mask(tri, 1.0, 0.0, ALU.is_gt, [[1, P]], -1)
            mask(later, 1.0, 0.0, ALU.is_gt, [[-1, P]], 1)
            pool.memset(ones[:, :], 1.0).then_inc(masks_ready, 1)
            pool.iota(slot_ids[:, :].rearrange("p (j s) -> p j s", s=CAP), pattern=[[0, P // CAP], [1, CAP]], base=0,
                      channel_multiplier=0, allow_small_or_imprecise_dtypes=True).then_inc(masks_ready, 1)
            for i in range(HR):
                f = pool.memset(freq[:, i:i + 1], INV_FREQ[i])
            f.then_inc(masks_ready, 1)

            wl = row[:, ROW["diff_subln_w"]:ROW["diff_subln_w"] + DV]
            pool.wait_ge(small_loaded, 16 * N_SMALL)
            step(pool.tensor_scalar(wl, wl, 1.0 - LAM_INIT, None, ALU.mult))
            od = dq.rearrange("p h (n d) -> p (h n) d", d=DV)
            pool.wait_ge(hO_evac, DHEADS)
            pool.wait_ge(sq_read, 5)
            pool.tensor_tensor(sq.rearrange("p (n d) -> p n d", d=DV), od, od, ALU.mult).then_inc(od_sums, 1)
            pool.wait_ge(od_root, 1)
            step(pool.tensor_tensor(od, od, rstd_o.unsqueeze(2).to_broadcast([P, 2 * DHEADS, DV]), ALU.mult))
            step(pool.tensor_tensor(od, od, wl.unsqueeze(1).to_broadcast([P, 2 * DHEADS, DV]), ALU.mult))
            pool.wait_ge(gate_ready, 2)
            pool.tensor_tensor(dq, dq, gb, ALU.mult).then_inc(od_ready, 1)

        @block.scalar
        def _(act):
            for name, rows in VEC_ROWS:
                src = t[name]
                src = src[0].rearrange("w (r c) -> (w r) c", c=P) if name == "conv_w_2" else (
                    src[0] if name == "sgu_b_2" else src[0].rearrange("(r c) -> r c", c=P))
                act.dma_start(vec_rows[VEC[name]:VEC[name] + rows, :], src).then_inc(small_loaded, 16)
            act.dma_start(sgu_in, t["sgu_w_2"][0].rearrange("g a b -> a g b")).then_inc(small_loaded, 16)
            act.dma_start(p_in, t["p_2"][0, 0].rearrange("(h p) d -> p h d", p=P)).then_inc(small_loaded, 16)
            act.dma_start(posi[:, 0, :], t["positions"][0].partition_broadcast(P)).then_inc(small_loaded, 16)
            for h in range(HALVES):
                act.dma_start(posc[:, h, 0:1], t["positions"][0, h * P:(h + 1) * P].rearrange("(p o) -> p o", o=1)
                              ).then_inc(small_loaded, 16)
            for name, n in ROW_VECS:
                src = t[name][0]
                src = src.rearrange("a b -> (a b)") if name == "diff_lambda" else src
                act.dma_start(row[:, ROW[name]:ROW[name] + n], src.partition_broadcast(P)).then_inc(small_loaded, 16)
            act.dma_start(router[:, :, :], t["router_w"][0].rearrange("(k p) e -> p k e", p=P)).then_inc(small_loaded, 16)

            def square_half():
                act.activation(xn[:, 0, :], xs[:, 0, :], ACT.Square, accum_out=ss_x[:, 0:1]).then_inc(sq_act, 1)

            def scale_half(n):
                act.wait_ge(rstd_ready, n + 1)
                act.activation(xn[:, 0, :], xs[:, 0, :], ACT.Copy, scale=rstd_x[:, 0:1]).then_inc(xn_act, 1)

            def evac_stage(s, base, weight):
                for b in (1, 3):
                    act.wait_ge(tr_done, 4 * STAGES.index(s) + b + 1)
                    for kt in (2 * b, 2 * b + 1):
                        scale = vec[:, VEC[weight] + kt:VEC[weight] + kt + 1] if weight else 1.0
                        act.activation(hT[:, kt, :], ps[:, base + b, (kt % 2) * T:(kt % 2 + 1) * T], ACT.Copy,
                                       scale=scale).then_inc(tr_act, 1)

            def evac(name, dst, n=D):
                act.wait_ge(chunk_used, DONE[name])
                scale = rstd_0[:, 0:1] if name[0] in "cd" else 1.0
                act.activation(dst, pset(SETS[name], 0, n), ACT.Copy, scale=scale).then_inc(block_act, 1)

            def squares(n, src, dst):
                if n:
                    act.wait_ge(sq_read, n)
                act.activation(dst, src, ACT.Square).then_inc(sq_ready, 1)

            act.wait_ge(x_loaded, 16)
            square_half()
            act.wait_ge(vec_ready, 1)
            evac_stage("attn", 0, "attn_norm_w")
            act.wait_ge(pw_ready, 2)
            act.dma_start(bgate, t["b_gate"][0].partition_broadcast(P)).then_inc(gate_bias_loaded, 16)
            act.wait_ge(rstd_ready, 1)
            evac("c", c_sb[:, 0, :], C_COLS)
            act.wait_ge(block_act, 1)
            act.wait_ge(block_dve, 1)
            for j in range(2):
                for h in range(HALVES):
                    act.activation(sq[:, (2 * j + h) * RANK:(2 * j + h + 1) * RANK], c_sb[:, h, j * RANK:(j + 1) * RANK], ACT.Square,
                                   accum_out=ss_c[:, 2 * j + h:2 * j + h + 1]).then_inc(c_sq, 1)
            for h in range(HALVES):
                act.activation(sq[:, D + h * ROPE:D + (h + 1) * ROPE], c_sb[:, h, 2 * RANK:C_COLS], ACT.Square,
                               accum_out=ss_kr[:, h:h + 1]).then_inc(c_sq, 1)
            evac("dq", dq[:, 0, :])
            act.wait_ge(block_act, 2)
            act.wait_ge(block_dve, 2)
            squares(0, dq.rearrange("p h d -> p (h d)"), sq)
            evac("dk", dk[:, 0, :])
            act.wait_ge(block_act, 3)
            act.wait_ge(block_dve, 3)
            squares(1, dk.rearrange("p h d -> p (h d)"), sq)
            act.wait_ge(lam_in, 1)
            act.activation(lam_s, lam_s, ACT.Exp).then_inc(lam_exp, 1)
            evac("dv", dv[:, 0, :])
            act.wait_ge(angle_ready, 1)
            act.activation(trig[:, 4:6, :], trig[:, 4:6, :], ACT.Sin).then_inc(trig_ready, 1)
            evac("uq0", q[:, 0, 0:768], 768)
            evac("uq1", q[:, 0, 768:1536], 768)
            act.wait_ge(block_act, 6)
            act.wait_ge(block_dve, 6)
            squares(2, q[:, 0, :], sq[:, 0:HEADS * QK])
            evac("ukv0", kv[:, 0, 0:1024])
            evac("ukv1", kv[:, 0, 1024:2048])
            squares(3, q[:, 1, :], sq[:, 0:HEADS * QK])
            act.wait_ge(block_act, 8)
            act.wait_ge(block_dve, 8)
            squares(4, kv.rearrange("p h (n d) -> p (h n) d", d=128)[:, :, 0:NOPE],
                    sq.rearrange("p (n d) -> p n d", d=NOPE))
            for i, g in enumerate((ga, gb)):
                act.wait_ge(gate_in, 2 * i + 2)
                act.activation(g, g, ACT.Sigmoid).then_inc(gate_ready, 1)

            for i in range(DHEADS + 4):
                if i < DHEADS:
                    act.wait_ge(hT_done, i + 1)
                    if i >= 2:
                        act.wait_ge(hS_done, i - 1)
                    act.activation(qkT[i % 2], ps[:, i % 2, :], ACT.Copy).then_inc(hT_evac, 1)
                if 0 <= i - 1 < DHEADS:
                    u = i - 1
                    act.wait_ge(max_ready, u + 1)
                    for j in range(4):
                        e = act.activation(scores[u % 2][:, j, :], scores[u % 2][:, j, :], ACT.Exp,
                                           bias=mxn[u % 2][:, j:j + 1], accum_out=sums[u % 2][:, j:j + 1])
                    e.then_inc(exp_done, 1)
                if 0 <= i - 3 < DHEADS:
                    u = i - 3
                    act.wait_ge(hP_done, u + 1)
                    if u >= 2:
                        act.wait_ge(hO_done, u - 1)
                    act.activation(pt_sb[u % 2], ps[:, 6, :].rearrange("p (k t) -> p k t", k=2), ACT.Copy).then_inc(hP_evac, 1)
                if 0 <= i - 4 < DHEADS:
                    u = i - 4
                    act.wait_ge(hO_done, u + 1)
                    act.activation(dq[:, :, u * DV:(u + 1) * DV],
                                   ps[:, 7, 0:T].rearrange("p (h d) -> p h d", h=2),
                                   ACT.Copy).then_inc(hO_evac, 1)
            for i in range(HEADS + 1):
                if i < HEADS:
                    u = DHEADS + i
                    act.wait_ge(hT_done, u + 1)
                    act.wait_ge(hS_done, u - 1)
                    act.activation(qkT[u % 2][0:QK, :], ps[0:QK, u % 2, :], ACT.Copy).then_inc(hT_evac, 1)
                if i >= 1:
                    u = DHEADS + i - 1
                    act.wait_ge(max_ready, u + 1)
                    act.wait_ge(hP_done, u - 1)
                    for h in range(HALVES):
                        e = act.activation(scores[u % 2][:, h, :], ps[:, 2 + u % 2, h * T:(h + 1) * T], ACT.Exp,
                                           bias=mxn[u % 2][:, h:h + 1], scale=QK ** -0.5, accum_out=sums[u % 2][:, h:h + 1])
                    e.then_inc(exp_done, 1)

            evac_stage("merge", 0, None)
            act.wait_ge(x_ready, 1)
            square_half()
            scale_half(1)
            evac_stage("ffn", 0, "ffn_norm_w")
            act.wait_ge(rmax_ready, 1)
            for h in range(HALVES):
                e = act.activation(logit[:, h, :], logit[:, h, :], ACT.Exp, bias=rmax[:, h:h + 1],
                                   accum_out=rsum[:, h:h + 1])
            e.then_inc(rexp_done, 1)
            for kt in range(1, KT, 2):
                act.wait_ge(gather_done, kt + 1)
                act.activation(xT_all[:, kt, :], ps[:, kt, :], ACT.Copy,
                               scale=vec[:, VEC["ffn_norm_w"] + kt:VEC["ffn_norm_w"] + kt + 1]).then_inc(gather_act, 1)

            act.sem_inc(ye_ready, 1)
            with act.Fori(0, EXPERTS) as e:
                act.wait_ge(scat_done, e + 2)
                act.wait_ge(e_scatter, e + 1)
                act.activation(scat, ps[:, 3, 256:512], ACT.Copy).then_inc(scat_ready, 1)
                act.wait_ge(chunk_used, EXPERT_CHUNKS * e + n_first + KT)
                act.wait_ge(hid_ready, e + 1)
                act.activation(hid_g, ps[:, 0, :], ACT.Silu).then_inc(silu_done, 1)
                act.wait_ge(hidT_done, e + 2)
                act.activation(hidT, ps[:, 2, :].rearrange("p (c t) -> p c t", c=4), ACT.Copy).then_inc(hidT_ready, 1)
                act.wait_ge(chunk_used, EXPERT_CHUNKS * e + n_first + EXPERT_CHUNKS)
                act.activation(ye, ps[:, 3, 0:DCOL], ACT.Copy).then_inc(ye_ready, 1)

            act.wait_ge(moe_added, EXPERTS + 1)
            square_half()
            scale_half(2)
            evac_stage("mix", 0, "norm1_g_2")
            act.wait_ge(chunk_used, DONE["conv"])
            act.activation(a_hT, ps[:, 6, :].rearrange("p (c t) -> p c t", c=2), ACT.Copy).then_inc(a_act, 1)
            act.activation(a_bT, ps[:, 4, :].rearrange("p (c t) -> p c t", c=2), ACT.Copy).then_inc(a_act, 1)
            act.wait_ge(chunk_used, DONE["qk2"])
            act.activation(qk2[:, 0, :], pset("A", 0), ACT.Copy).then_inc(block_act, 1)
            act.wait_ge(block_act, 9)
            act.wait_ge(block_dve, 9)
            act.activation(sq, qk2.rearrange("p h d -> p (h d)"), ACT.Square).then_inc(sq_ready, 1)
            for j in range(SATT // P):
                act.wait_ge(qkT2_done, j + 1)
                act.activation(qkT2[:, j, :], ps[:, j, :], ACT.Copy).then_inc(qkT2_evac, 1)
            act.wait_ge(chunk_used, DONE["vuv"])
            for h in range(HALVES):
                act.activation(u2[:, h, :], pset("B", h)[:, 512:768], ACT.Gelu).then_inc(gelu_done, 1)
                act.activation(cv2[:, h, :], pset("B", h)[:, 768:1024], ACT.Gelu).then_inc(gelu_done, 1)
            act.wait_ge(gelu_done, 4)
            act.wait_ge(sq_read, 6)
            act.activation(sq[:, 0:HALVES * SGU], cv2.rearrange("p h d -> p (h d)"), ACT.Square).then_inc(sq_ready, 1)
            for i in range(SHEADS + 1):
                if i < SHEADS:
                    act.wait_ge(z_done, i + 1)
                    act.activation(na[i % 2], ps[:, 4 + i % 2, 0:SC], ACT.Abs).then_inc(act_step, 1)
                    act.wait_ge(act_step, 2 * i + 1)
                    act.activation(na[i % 2], na[i % 2], ACT.Exp, scale=-1.0).then_inc(act_step, 1)
                    act.wait_ge(act_step, 2 * i + 2)
                    if i >= 2:
                        act.wait_ge(lr_ready, i - 1)
                    act.activation(spl[i % 2], na[i % 2], ACT.Ln, bias=1.0).then_inc(sp_ready, 1)
                if i >= 1:
                    act.wait_ge(arg_ready, i)
                    act.activation(lb[(i - 1) % 3], lb[(i - 1) % 3], ACT.Exp).then_inc(w_exp, 1)
            act.wait_ge(ycT_done, 1)
            act.activation(yT[:, 6:8, :], ps[:, 3, :].rearrange("p (c t) -> p c t", c=2), ACT.Copy).then_inc(ycT_evac, 1)

            act.wait_ge(x_ready, 2)
            square_half()
            scale_half(3)
            evac_stage("ff", 0, "norm2_g_2")
            for b in range(4):
                act.wait_ge(chunk_used, DONE[f"up{b}"])
                for j in range(4):
                    act.activation(fT[:, 8 * b + 2 * j:8 * b + 2 * j + 2, :],
                                   ps[:, SET[SETS[f"up{b}"]] + j, :].rearrange("p (c t) -> p c t", c=2),
                                   ACT.Relu).then_inc(f_relu, 1)

            act.wait_ge(x_ready, 3)
            square_half()
            evac_stage("ple", 4, "norm3_g_2")
            act.wait_ge(rstd_ready, 5)
            act.wait_ge(chunk_used, DONE["gate2"])
            for h in range(HALVES):
                act.activation(gate2[:, h, :], pset("B", h), ACT.Sigmoid, scale=rstd_x[:, h:h + 1]).then_inc(gate2_ready, 1)

        @block.vector
        def _(dve):
            count = [0]

            def step(ins):
                count[0] += 1
                ins.then_inc(dve_step, 1)
                dve.wait_ge(dve_step, count[0])

            def roots(ss, out, n, dim, ready=None):
                v, a, y = nw[0][:, 0:n], nw[1][:, 0:n], nw[2][:, 0:n]
                step(dve.tensor_scalar(v, ss, 1.0 / dim, EPS, ALU.mult, ALU.add))
                step(dve.tensor_scalar(a.bitcast(I32), v.bitcast(I32), 1, None, ALU.logical_shift_right))
                step(dve.tensor_scalar(y.bitcast(I32), a.bitcast(I32), -1.0, RSQRT_MAGIC, ALU.mult, ALU.add))
                step(dve.tensor_scalar(v, v, -0.5, None, ALU.mult))
                for k in range(3):
                    step(dve.tensor_tensor(a, y, y, ALU.mult))
                    step(dve.tensor_tensor(a, a, v, ALU.mult))
                    last = dve.scalar_tensor_tensor(out if k == 2 else y, a, 1.5, y, ALU.add, ALU.mult)
                    if k < 2 or ready is None:
                        step(last)
                last.then_inc(ready, 1) if ready is not None else None

            def norm(n, scaled=True):
                step(dve.scalar_tensor_tensor(xn[:, 1, :], xs[:, 1, :], 1.0, xs[:, 1, :], ALU.mult, ALU.mult,
                                              accum_out=ss_x[:, 1:2]))
                dve.wait_ge(sq_act, n + 1)
                roots(ss_x, rstd_x, 2, D, rstd_ready)
                dve.wait_ge(rstd_ready, n + 1)
                if scaled:
                    dve.tensor_scalar(xn[:, 1, :], xs[:, 1, :], rstd_x[:, 1:2], None, ALU.mult).then_inc(xn_dve, 1)

            def evac_stage(s, base, weight):
                for b in (0, 2):
                    dve.wait_ge(tr_done, 4 * STAGES.index(s) + b + 1)
                    for kt in (2 * b, 2 * b + 1):
                        src = ps[:, base + b, (kt % 2) * T:(kt % 2 + 1) * T]
                        if weight is None:
                            ins = dve.tensor_copy(hT[:, kt, :], src)
                        else:
                            ins = dve.tensor_scalar(hT[:, kt, :], src, vec[:, VEC[weight] + kt:VEC[weight] + kt + 1], None, ALU.mult)
                        ins.then_inc(tr_dve, 1)

            def evac(name, dst, n=D):
                dve.wait_ge(chunk_used, DONE[name])
                src = pset(SETS[name], 1, n)
                if name[0] in "cd":
                    ins = dve.tensor_scalar(dst, src, rstd_0[:, 1:2], None, ALU.mult)
                else:
                    ins = dve.tensor_copy(dst, src)
                ins.then_inc(block_dve, 1)

            def rows(name):
                n = dict(ROW_VECS)[name]
                return row[:, ROW[name]:ROW[name] + n]

            dve.wait_ge(x_loaded, 16)
            norm(0, scaled=False)
            step(dve.tensor_copy(rstd_0, rstd_x))
            dve.wait_ge(vec_done, 1)
            dve.tensor_copy(vec[:, :], ps[:, 4, 0:NVEC]).then_inc(vec_ready, 1)
            dve.wait_ge(vec_ready, 1)
            evac_stage("attn", 0, "attn_norm_w")
            dve.wait_ge(pw_done, 1)
            dve.tensor_copy(pT[:, :, :], ps[:, 5, :].rearrange("p (k t) -> p k t", k=2)).then_inc(pw_ready, 1)
            dve.wait_ge(masks_ready, N_MASKS)
            dve.tensor_tensor(wsT[:, :, :], ps[:, 6, :].rearrange("p (g t) -> p g t", g=SG),
                              tril[:, :].unsqueeze(1).to_broadcast([P, SG, P]), ALU.mult).then_inc(pw_ready, 1)

            dve.wait_ge(small_loaded, 16 * N_SMALL)
            for i, (op, c) in enumerate(((ALU.arith_shift_right, 12), (ALU.bitwise_and, 4095))):
                step(dve.tensor_scalar(posi[:, 1 + i, :], posi[:, 0, :], c, None, op))
                step(dve.tensor_scalar(posc[:, :, 1 + i], posc[:, :, 0], c, None, op))
                step(dve.tensor_copy(posb[:, i, :], posi[:, 1 + i, :]))
                step(dve.tensor_copy(posc_f[:, 2 * i:2 * i + 2], posc[:, :, 1 + i]))
            step(dve.tensor_copy(posc_f[:, 4:6], posc[:, :, 0]))
            for h in range(HALVES):
                for i in range(2):
                    step(dve.tensor_scalar(posb[:, 2 + i, :], posb[:, i, :], posc_f[:, 2 * i + h:2 * i + h + 1], None,
                                           ALU.subtract))
                step(dve.scalar_tensor_tensor(posb[:, 2, :], posb[:, 2, :], 4096.0, posb[:, 3, :], ALU.mult, ALU.add))
                step(dve.scalar_tensor_tensor(dist[:, h, :], posb[:, 2, :], -1.0, posb[:, 2, :], ALU.mult, ALU.max))
            ang, turns, sin_a, cos_a, tmp = trig[:, 0, :], trig[:, 1, :], trig[:, 4, :], trig[:, 5, :], trig[:, 2, :]
            for h in range(HALVES):
                step(dve.tensor_scalar(trig[:, 0, h * HR:(h + 1) * HR], freq, posc_f[:, 4 + h:5 + h], None, ALU.mult))
            step(dve.tensor_scalar(turns, ang, 1.0 / (2 * math.pi), ROUND, ALU.mult, ALU.add))
            step(dve.tensor_scalar(turns, turns, -ROUND, None, ALU.add))
            for c in TWO_PI_PARTS:
                step(dve.scalar_tensor_tensor(ang, turns, -c, ang, ALU.mult, ALU.add))
            step(dve.tensor_scalar(sin_a, ang, PI_BELOW, -PI_BELOW, ALU.min, ALU.max))
            step(dve.tensor_scalar(ang, ang, math.pi / 2, None, ALU.add))
            step(dve.tensor_scalar(tmp, ang, math.pi, -2 * math.pi, ALU.is_gt, ALU.mult))
            step(dve.tensor_tensor(ang, ang, tmp, ALU.add))
            dve.tensor_scalar(cos_a, ang, PI_BELOW, -PI_BELOW, ALU.min, ALU.max).then_inc(angle_ready, 1)
            lam_v = rows("diff_lambda").rearrange("p (a b d) -> p a b d", a=2, b=2)
            lam_t = posb[:, 2, 0:2 * DQK].rearrange("p (a d) -> p a d", a=2)
            step(dve.tensor_tensor(lam_t, lam_v[:, :, 0, :], lam_v[:, :, 1, :], ALU.mult))
            dve.tensor_reduce(lam_s, lam_t, AX, ALU.add).then_inc(lam_in, 1)

            evac("c", c_sb[:, 1, :], C_COLS)
            dve.wait_ge(c_sq, 6)
            roots(ss_c, rstd_c, 4, RANK)
            for j in range(2):
                for h in range(HALVES):
                    c = c_sb[:, h, j * RANK:(j + 1) * RANK]
                    dve.tensor_scalar(c, c, rstd_c[:, 2 * j + h:2 * j + h + 1], None, ALU.mult).then_inc(c_norm, 1)

            def head_sums(n, src, out, ready=None):
                dve.wait_ge(sq_ready, n + 1)
                dve.tensor_reduce(out, src, AX, ALU.add).then_inc(sq_read, 1)
                dve.wait_ge(sq_read, n + 1)

            def diff_norm(n, buf, weight):
                v = buf.rearrange("p h (n d) -> p (h n) d", d=DQK)
                head_sums(n, sq.rearrange("p (n d) -> p n d", d=DQK), ss_h)
                roots(ss_h, rstd_h, 2 * HEADS, DQK)
                step(dve.tensor_tensor(v, v, rstd_h.unsqueeze(2).to_broadcast([P, 2 * HEADS, DQK]), ALU.mult))
                dve.tensor_tensor(v, v, weight.unsqueeze(1).to_broadcast([P, 2 * HEADS, DQK]), ALU.mult).then_inc(dqk_ready, 1)

            evac("dq", dq[:, 1, :])
            step(dve.tensor_scalar(rows("diff_q_hnorm_w"), rows("diff_q_hnorm_w"), DQK ** -0.5, None, ALU.mult))
            diff_norm(0, dq, rows("diff_q_hnorm_w"))
            evac("dk", dk[:, 1, :])
            diff_norm(1, dk, rows("diff_k_hnorm_w"))
            dve.wait_ge(lam_exp, 1)
            step(dve.tensor_scalar(lam, lam_s[:, 0:1], LAM_INIT, lam_s[:, 1:2], ALU.add, ALU.subtract))
            evac("dv", dv[:, 1, :])
            for j in range(2):
                for kt in range(RT):
                    dve.wait_ge(cT_done, j + 1)
                    w = VEC["mla_q_norm_w" if j == 0 else "mla_kv_norm_w"] + kt
                    dve.tensor_scalar(cT[:, j, kt, :], ps[:, 4 + j, kt * T:(kt + 1) * T], vec[:, w:w + 1], None,
                                      ALU.mult).then_inc(cT_dve, 1)
            dve.wait_ge(trig_ready, 1)
            evac("uq0", q[:, 1, 0:768], 768)
            evac("uq1", q[:, 1, 768:1536], 768)
            evac("ukv0", kv[:, 1, 0:1024])
            evac("ukv1", kv[:, 1, 1024:2048])
            dve.wait_ge(block_dve, 8)

            def rope(x1, x2, cos, sin, t1, t2):
                step(dve.tensor_tensor(t1, x1, sin, ALU.mult))
                step(dve.tensor_tensor(t2, x2, sin, ALU.mult))
                step(dve.tensor_tensor(x1, x1, cos, ALU.mult))
                step(dve.tensor_tensor(x1, x1, t2, ALU.subtract))
                step(dve.tensor_tensor(x2, x2, cos, ALU.mult))
                step(dve.tensor_tensor(x2, x2, t1, ALU.add))

            sin_t, cos_t = (trig[:, i, :].rearrange("p (h i) -> p h i", h=HALVES) for i in (4, 5))
            step(dve.tensor_tensor(kr, c_sb[:, :, 2 * RANK:C_COLS],
                                   rows("mla_k_hnorm_w")[:, NOPE:QK].unsqueeze(1).to_broadcast([P, HALVES, ROPE]), ALU.mult))
            rt = [trig[:, 0, :].rearrange("p (h i) -> p h i", h=HALVES), trig[:, 1, :].rearrange("p (h i) -> p h i", h=HALVES)]
            rope(kr[:, :, 0:HR], kr[:, :, HR:ROPE], cos_t, sin_t, *rt)
            for h in range(HALVES):
                head_sums(2 + h, sq[:, 0:HEADS * QK].rearrange("p (n d) -> p n d", d=QK), ss_h[:, h * HEADS:(h + 1) * HEADS])
            roots(ss_h, rstd_h, 2 * HEADS, QK)
            qh = q.rearrange("p h (n d) -> p (h n) d", d=QK)
            step(dve.tensor_tensor(qh, qh, rstd_h.unsqueeze(2).to_broadcast([P, 2 * HEADS, QK]), ALU.mult))
            step(dve.tensor_tensor(qh, qh, rows("mla_q_hnorm_w").unsqueeze(1).to_broadcast([P, 2 * HEADS, QK]), ALU.mult))
            q4 = q.rearrange("p h (n d) -> p h n d", d=QK)
            full = [P, HALVES, HEADS, HR]
            rope(q4[:, :, :, NOPE:NOPE + HR], q4[:, :, :, NOPE + HR:QK], cos_t.unsqueeze(2).to_broadcast(full),
                 sin_t.unsqueeze(2).to_broadcast(full), *rope_t)
            head_sums(4, sq.rearrange("p (n d) -> p n d", d=NOPE), ss_h)
            step(dve.tensor_tensor(ss_h.rearrange("p (h n) -> p h n", h=HALVES), ss_h.rearrange("p (h n) -> p h n", h=HALVES),
                                   ss_kr.unsqueeze(2).to_broadcast([P, HALVES, HEADS]), ALU.add))
            roots(ss_h, rstd_k, 2 * HEADS, QK)
            kh = kf.rearrange("p h (n d) -> p (h n) d", d=QK)
            kn = kv.rearrange("p h (n d) -> p (h n) d", d=128)[:, :, 0:NOPE]
            step(dve.tensor_tensor(kh[:, :, 0:NOPE], kn, rstd_k.unsqueeze(2).to_broadcast([P, 2 * HEADS, NOPE]), ALU.mult))
            step(dve.tensor_tensor(kh[:, :, 0:NOPE], kh[:, :, 0:NOPE],
                                   rows("mla_k_hnorm_w")[:, 0:NOPE].unsqueeze(1).to_broadcast([P, 2 * HEADS, NOPE]), ALU.mult))
            wide = [P, HALVES, HEADS, ROPE]
            dve.tensor_tensor(kf.rearrange("p h (n d) -> p h n d", d=QK)[:, :, :, NOPE:QK], kr.unsqueeze(2).to_broadcast(wide),
                              rstd_k.rearrange("p (h n) -> p h n", h=HALVES).unsqueeze(3).to_broadcast(wide),
                              ALU.mult).then_inc(qk_ready, 1)
            dve.wait_ge(gate_bias_loaded, 16)
            for i, (name, g) in enumerate((("gate_a", ga), ("gate_b", gb))):
                dve.wait_ge(chunk_used, DONE[name])
                for h in range(HALVES):
                    dve.scalar_tensor_tensor(g[:, h, :], pset(SETS[name], h), rstd_0[:, h:h + 1], bgate[:, i * D:(i + 1) * D],
                                             ALU.mult, ALU.add).then_inc(gate_in, 1)
            dve.wait_ge(gate_in, 4)

            for i in range(1, DHEADS + 2):
                if i - 1 < DHEADS:
                    u = i - 1
                    s = scores[u % 2]
                    dve.wait_ge(hS_done, u + 1)
                    if u >= 2:
                        dve.wait_ge(hP_done, u - 1)
                    for m in range(2):
                        dve.scalar_tensor_tensor(s[:, 2 * m:2 * m + 2, :].rearrange("p h k -> p (h k)"),
                                                 dist.rearrange("p h k -> p (h k)"), -2.0 ** (-8.0 * (u + 1) / DHEADS),
                                                 ps[:, 2 + 2 * (u % 2) + m, :], ALU.mult, ALU.add).then_inc(hS_read, 1)
                    dve.wait_ge(hS_read, 2 * u + 2)
                    step(dve.tensor_reduce(mxn[u % 2], s, AX, ALU.max))
                    dve.tensor_scalar(mxn[u % 2], mxn[u % 2], -1.0, None, ALU.mult).then_inc(max_ready, 1)
                if i >= 2:
                    u = i - 2
                    s, r = scores[u % 2], rec[u % 2]
                    dve.wait_ge(exp_done, u + 1)
                    step(dve.reciprocal(r, sums[u % 2]))
                    step(dve.tensor_scalar(r[:, 2:4], r[:, 2:4], lam, None, ALU.mult))
                    for h in range(HALVES):
                        dve.tensor_scalar(s[:, 2 + h, :], s[:, 2 + h, :], r[:, 2 + h:3 + h], None, ALU.mult).then_inc(dve_step, 1)
                        count[0] += 1
                    dve.wait_ge(dve_step, count[0])
                    for h in range(HALVES):
                        dve.scalar_tensor_tensor(s[:, h, :], s[:, h, :], r[:, h:h + 1], s[:, 2 + h, :], ALU.mult,
                                                 ALU.subtract).then_inc(prob_ready, 1)
            for i in range(1, HEADS + 3):
                if i >= 3:
                    step(dve.reciprocal(rec[(DHEADS + i - 3) % 2][:, 0:2], sums[(DHEADS + i - 3) % 2][:, 0:2]))
                if i - 1 < HEADS:
                    u = DHEADS + i - 1
                    dve.wait_ge(hS_done, u + 1)
                    if i >= 3:
                        dve.wait_ge(exp_done, u - 1)
                    step(dve.tensor_reduce(mxn[u % 2][:, 0:2], ps[:, 2 + u % 2, :].rearrange("p (h k) -> p h k", h=2), AX, ALU.max))
                    dve.tensor_scalar(mxn[u % 2][:, 0:2], mxn[u % 2][:, 0:2], -QK ** -0.5, None, ALU.mult).then_inc(max_ready, 1)
                if 0 <= i - 2 < HEADS:
                    u = DHEADS + i - 2
                    dve.wait_ge(hP_done, u + 1)
                    dve.wait_ge(hO_done, u - 1)
                    dve.tensor_copy(pt_sb[u % 2], ps[:, 4 + u % 2, :].rearrange("p (k t) -> p k t", k=2)).then_inc(hP_evac, 1)
                if 0 <= i - 3 < HEADS:
                    hd = i - 3
                    u = DHEADS + hd
                    r = rec[u % 2]
                    dve.wait_ge(hO_done, u + 1)
                    for h in range(HALVES):
                        g = ga[:, h, hd * VD:(hd + 1) * VD]
                        dve.wait_ge(gate_ready, 2)
                        o = dve.scalar_tensor_tensor(g, ps[:, 6 + u % 2, h * VD:(h + 1) * VD], r[:, h:h + 1], g, ALU.mult, ALU.mult)
                    o.then_inc(hO_evac, 1)
                if i == 8:
                    dve.wait_ge(od_sums, 1)
                    step(dve.tensor_reduce(ss_o, sq.rearrange("p (n d) -> p n d", d=DV), AX, ALU.add))
                    roots(ss_o, rstd_o, 2 * DHEADS, DV, od_root)
            dve.wait_ge(hO_evac, DHEADS + HEADS)
            dve.wait_ge(od_ready, 1)
            for h in range(HALVES):
                dve.tensor_tensor(ga[:, h, :], ga[:, h, :], dq[:, h, :], ALU.add).then_inc(merged_ready, 1)
            evac_stage("merge", 0, None)

            def add_product(name):
                dve.wait_ge(chunk_used, DONE[name])
                for h in range(HALVES):
                    a = dve.tensor_tensor(xs[:, h, :], pset(SETS[name], h), xs[:, h, :], ALU.add)
                a.then_inc(x_ready, 1)

            add_product("out")
            dve.wait_ge(x_ready, 1)
            norm(1)
            evac_stage("ffn", 0, "ffn_norm_w")
            dve.wait_ge(logit_done, 1)
            lp = ps[:, 4, 0:HALVES * EXPERTS].rearrange("p (h e) -> p h e", h=HALVES)
            step(dve.tensor_copy(logit, lp))
            step(dve.tensor_reduce(rmax, logit, AX, ALU.max))
            dve.tensor_scalar(rmax, rmax, -1.0, None, ALU.mult).then_inc(rmax_ready, 1)
            dve.wait_ge(rexp_done, 1)
            step(dve.reciprocal(rinv, rsum))
            for h in range(HALVES):
                dve.tensor_scalar(aff[:, h, :], logit[:, h, :], rinv[:, h:h + 1], None, ALU.mult).then_inc(aff_ready, 1)
            r0, work, sel, eq, cum, zero = (routing[:, i, :] for i in range(6))
            dve.wait_ge(affT_done, 1)
            step(dve.memset(zero, 0.0))
            step(dve.tensor_copy(r0, ps[0:EXPERTS, 5, 0:T]))
            src = r0
            for k in range(CAP // 8):
                step(dve.max(top8[:, k, :], src))
                if k + 1 < CAP // 8:
                    step(dve.match_replace(work, top8[:, k, :], src, -1.0))
                    src = work
            least = top8[:, CAP // 8 - 1, 7:8]
            step(dve.tensor_scalar(sel, r0, least, None, ALU.is_gt, ALU.add, accum_out=rcount[:, 0:1]))
            step(dve.tensor_scalar(rcount[:, 1:2], rcount[:, 0:1], -1.0, float(CAP), ALU.mult, ALU.add))
            step(dve.tensor_scalar(eq, r0, least, None, ALU.is_equal))
            step(dve.tensor_tensor_scan(cum, eq, zero, 0.0, ALU.add, ALU.add))
            step(dve.scalar_tensor_tensor(eq, cum, rcount[:, 1:2], eq, ALU.is_le, ALU.mult))
            step(dve.tensor_tensor(sel, sel, eq, ALU.add))
            step(dve.tensor_tensor_scan(cum, sel, zero, 0.0, ALU.add, ALU.add))
            step(dve.tensor_tensor(cum, cum, sel, ALU.mult))
            dve.tensor_scalar(cum, cum, -1.0, None, ALU.add).then_inc(slot_done, 1)
            dve.wait_ge(slotT_done, 1)
            step(dve.tensor_copy(slot_t, ps[:, 6, 0:HALVES * EXPERTS].rearrange("p (h e) -> p h e", h=HALVES)))
            grid = [P, EXPERTS, CAP]
            for h in range(HALVES):
                dve.tensor_tensor(onehot[:, h, :].rearrange("p (e s) -> p e s", e=EXPERTS),
                                  slot_t[:, h, :].unsqueeze(2).to_broadcast(grid),
                                  slot_ids[:, 0:CAP].unsqueeze(1).to_broadcast(grid), ALU.is_equal).then_inc(onehot_ready, 1)
            for kt in range(0, KT, 2):
                dve.wait_ge(gather_done, kt + 1)
                dve.tensor_scalar(xT_all[:, kt, :], ps[:, kt, :], vec[:, VEC["ffn_norm_w"] + kt:VEC["ffn_norm_w"] + kt + 1],
                                  None, ALU.mult).then_inc(gather_dve, 1)
            dve.wait_ge(gather_dve, KT // 2)
            dve.wait_ge(gather_act, KT // 2)

            dve.sem_inc(hid_ready, 1)
            dve.sem_inc(moe_added, 1)
            with dve.Fori(0, EXPERTS) as e:
                dve.wait_ge(chunk_used, EXPERT_CHUNKS * e + n_first - KT)
                dve.tensor_copy(xe, xT_all[:, :, bass.ds(e * CAP, CAP)]).then_inc(xe_ready, 1)
                dve.wait_ge(scat_done, e + 1)
                for h in range(HALVES):
                    dve.tensor_scalar(gated[:, h, :], slot_ids[:, :], slot_t[:, h, bass.ds(e, 1)], aff[:, h, bass.ds(e, 1)],
                                      ALU.is_equal, ALU.mult).then_inc(gated_ready, 1)
                dve.wait_ge(silu_done, e + 1)
                dve.wait_ge(chunk_used, EXPERT_CHUNKS * e + n_first + 2 * KT)
                dve.wait_ge(hidT_done, e + 1)
                dve.tensor_tensor(hid, hid_g, ps[:, 1, :], ALU.mult).then_inc(hid_ready, 1)
                dve.wait_ge(e_scatter, e + 2)
                for j in range(4):
                    xv = xs[:, :, j * DCOL:(j + 1) * DCOL]
                    a = dve.tensor_tensor(xv, ps[:, 4 + j, :].rearrange("p (h d) -> p h d", h=HALVES), xv, ALU.add)
                a.then_inc(moe_added, 1)

            dve.wait_ge(moe_added, EXPERTS + 1)
            norm(2)
            evac_stage("mix", 0, "norm1_g_2")
            step(dve.memset(conv[:, :, 0:CONVW - 1], 0.0))
            dve.wait_ge(chunk_used, DONE["conv"])
            dve.wait_ge(a_act, 1)
            dve.tensor_tensor(conv[:, :, CONVW - 1:], ps[:, 5, :].rearrange("p (c t) -> p c t", c=2), a_hT, ALU.mult).then_inc(a_dve, 1)
            dve.wait_ge(a_dve, 1)
            dve.wait_ge(a_act, 2)
            for ct in range(2):
                w = [vec[:, VEC["conv_w_2"] + 2 * j + ct:VEC["conv_w_2"] + 2 * j + ct + 1] for j in range(CONVW)]
                step(dve.tensor_scalar(conv_y, conv[:, ct, 0:T], w[0], None, ALU.mult))
                for j in range(1, CONVW):
                    step(dve.scalar_tensor_tensor(conv_y, conv[:, ct, j:j + T], w[j], conv_y, ALU.mult, ALU.add))
                dve.tensor_tensor(yT[:, ct, :], conv_y, a_bT[:, ct, :], ALU.mult).then_inc(conv_ready, 1)
                dve.wait_ge(conv_ready, ct + 1)
            evac("qk2", qk2[:, 1, :])
            step(dve.tensor_scalar(rows("q_norm_g_2"), rows("q_norm_g_2"), SHD ** -0.5, None, ALU.mult))
            head_sums(5, sq.rearrange("p (n d) -> p n d", d=SHD), ss_h)
            roots(ss_h, rstd_h, 4 * SHEADS, SHD)
            v = qk2.rearrange("p h (n d) -> p (h n) d", d=SHD)
            step(dve.tensor_tensor(v, v, rstd_h.unsqueeze(2).to_broadcast([P, 4 * SHEADS, SHD]), ALU.mult))
            for i, name in enumerate(("q_norm_g_2", "k_norm_g_2")):
                v = qk2.rearrange("p h (n d) -> p h n d", d=SHD)[:, :, i * SHEADS:(i + 1) * SHEADS, :]
                w = rows(name).unsqueeze(1).unsqueeze(1).to_broadcast([P, HALVES, SHEADS, SHD])
                dve.tensor_tensor(v, v, w, ALU.mult).then_inc(qk2_ready, 1)
            dve.wait_ge(chunk_used, DONE["vuv"])
            for h in range(HALVES):
                dve.tensor_copy(v2[:, h, :], pset("B", h)[:, 0:SATT]).then_inc(v_ready, 1)
            head_sums(6, sq[:, 0:HALVES * SGU].rearrange("p (n d) -> p n d", d=SGU // SG), ss_h[:, 0:2 * SG])
            roots(ss_h[:, 0:2 * SG], rstd_h[:, 0:2 * SG], 2 * SG, SGU // SG)
            v = cv2.rearrange("p h (n d) -> p (h n) d", d=SGU // SG)
            step(dve.tensor_tensor(v, v, rstd_h[:, 0:2 * SG].unsqueeze(2).to_broadcast([P, 2 * SG, SGU // SG]), ALU.mult))
            dve.tensor_tensor(cv2, cv2, rows("sgu_norm_g_2").unsqueeze(1).to_broadcast([P, HALVES, SGU]), ALU.mult).then_inc(cv_ready, 1)

            def diagonal(buf):
                return buf.rearrange("p (c t) -> p c t", t=P)[:, 0:3:2, :]

            for i in range(SHEADS + 2):
                if i < SHEADS:
                    z = ps[:, 4 + i % 2, 0:SC]
                    dve.wait_ge(sp_ready, i + 1)
                    if i >= 3:
                        dve.wait_ge(yb_done, i - 2)
                    step(dve.scalar_tensor_tensor(lb[i % 3], z, 0.0, spl[i % 2], ALU.min, ALU.subtract))
                    if i >= 2:
                        dve.wait_ge(suf_done, i - 1)
                    step(dve.tensor_tensor(lr[i % 2], lb[i % 3], z, ALU.subtract))
                    dve.tensor_tensor(diagonal(lr[i % 2]), diagonal(lr[i % 2]), tri[:, :].unsqueeze(1).to_broadcast([P, 2, P]),
                                      ALU.mult).then_inc(lr_ready, 1)
                if 0 <= i - 1 < SHEADS:
                    u = i - 1
                    dve.wait_ge(suf_done, u + 1)
                    dve.tensor_tensor(lb[u % 3], ps[:, 6 + u % 2, 0:SC], lb[u % 3], ALU.add).then_inc(arg_ready, 1)
                if i == 0:
                    dve.wait_ge(sv_done, 1)
                    for g in range(SG):
                        w = SGU // SG
                        s = ps[:, 2, :].rearrange("p (h d) -> p h d", h=HALVES)[:, :, g * w:(g + 1) * w]
                        b = vec[:, VEC["sgu_b_2"] + g:VEC["sgu_b_2"] + g + 1]
                        dve.scalar_tensor_tensor(yc[:, :, g * w:(g + 1) * w], s, b, u2[:, :, g * w:(g + 1) * w], ALU.add,
                                                 ALU.mult).then_inc(yc_ready, 1)
                if 0 <= i - 2 < SHEADS:
                    u = i - 2
                    dve.wait_ge(w_exp, u + 1)
                    dve.tensor_tensor(diagonal(lb[u % 3]), diagonal(lb[u % 3]), tri[:, :].unsqueeze(1).to_broadcast([P, 2, P]),
                                      ALU.mult).then_inc(w_ready, 1)
                    if u % 2:
                        pair = u // 2
                        dve.wait_ge(yb_done, u + 1)
                        dve.tensor_copy(yT[:, 2 + pair, :], ps[:, pair % 2, 0:T]).then_inc(yb_evac, 1)
            add_product("out2")
            dve.wait_ge(x_ready, 2)
            norm(3)
            evac_stage("ff", 0, "norm2_g_2")
            for b in range(4):
                for j in range(4):
                    f = fT[:, 8 * b + 2 * j:8 * b + 2 * j + 2, :]
                    dve.wait_ge(f_relu, 4 * b + j + 1)
                    dve.tensor_tensor(f, f, f, ALU.mult).then_inc(f_ready, 1)
            add_product("down")
            dve.wait_ge(x_ready, 3)
            norm(4, scaled=False)
            evac_stage("ple", 4, "norm3_g_2")
            for h in range(HALVES):
                dve.wait_ge(gate2_ready, h + 1)
                step(dve.tensor_tensor(gate2[:, h, :], pset(SETS["proj"], h), gate2[:, h, :], ALU.mult))
                dve.tensor_tensor(out_sb[:, h, :], xs[:, h, :], gate2[:, h, :], ALU.add).then_inc(out_ready, 1)

        @block.tensor
        def _(pe):
            def transposes(s, src, base):
                for b in range(4):
                    for kt in (2 * b, 2 * b + 1):
                        for h in range(HALVES):
                            m = pe.transpose(ps[:, base + b, (kt % 2) * T + h * P:(kt % 2) * T + (h + 1) * P],
                                             src[:, h, kt * P:(kt + 1) * P], ident[:, :])
                    m.then_inc(tr_done, 1)

            def stage_ready(s):
                pe.wait_ge(tr_dve, 4 * (STAGES.index(s) + 1))
                pe.wait_ge(tr_act, 4 * (STAGES.index(s) + 1))

            def product(name, left, cols, n_chunks, ready=None):
                for c in range(n_chunks):
                    i = FIRST[name] + c
                    pe.wait_ge(slot_loaded[i % SLOTS], landed(i))
                    w = slot_view(i, cols)
                    for k in range(2):
                        kt = 2 * c + k
                        if ready is not None:
                            ready(kt)
                        for h in range(HALVES):
                            for c0 in range(0, cols, 512):
                                n = min(512, cols - c0)
                                m = pe.matmul(pset(SETS[name], h)[:, c0:c0 + n], left(kt, h), w[:, k, c0:c0 + n],
                                              start=kt == 0, stop=kt == 2 * n_chunks - 1)
                    m.then_inc(chunk_used, 1)

            def product_T(name, cols, n_chunks):
                for c in range(n_chunks):
                    i = FIRST[name] + c
                    pe.wait_ge(slot_loaded[i % SLOTS], landed(i))
                    w = slot_view(i, cols)
                    for k in range(2):
                        kt = 2 * c + k
                        for ct in range(cols // P):
                            m = pe.matmul(ps[:, SET[SETS[name]] + ct // 2, (ct % 2) * T:(ct % 2 + 1) * T],
                                          w[:, k, ct * P:(ct + 1) * P], hT[:, kt, :], start=kt == 0 and ct % 2 == 0,
                                          stop=kt == 2 * n_chunks - 1, skip_group_check=True)
                    m.then_inc(chunk_used, 1)

            def left_h(kt, h):
                return hT[:, kt, h * P:(h + 1) * P]

            pe.wait_ge(masks_ready, 1)
            pe.wait_ge(x_loaded, 16)
            transposes("attn", xs, 0)
            pe.wait_ge(small_loaded, 16 * N_SMALL)
            pe.transpose(ps[:, 4, 0:NVEC], vec_rows[:, :], ident[0:NVEC, 0:NVEC]).then_inc(vec_done, 1)
            for kt in range(PLE // P):
                for h in range(HALVES):
                    pe.transpose(ps[:, 5, kt * T + h * P:kt * T + (h + 1) * P], p_in[:, h, kt * P:(kt + 1) * P], ident[:, :])
            for g in range(SG):
                m = pe.transpose(ps[:, 6, g * P:(g + 1) * P], sgu_in[:, g, :], ident[:, :])
            m.then_inc(pw_done, 1)

            stage_ready("attn")
            pe.wait_ge(pw_ready, 2)
            early = [("c", C_COLS, 4), ("dq", D, 4), ("dk", D, 4), ("dv", D, 4), ("uq0", 768, 1), ("uq1", 768, 1),
                     ("ukv0", 1024, 1), ("ukv1", 1024, 1), ("gate_a", D, 4), ("gate_b", D, 4)]
            for b, (name, cols, n) in enumerate(early):
                if name == "uq0":
                    pe.wait_ge(c_norm, 4)
                    pe.wait_ge(block_act, 3)
                    pe.wait_ge(block_dve, 3)
                    for j in range(2):
                        for kt in range(RT):
                            for h in range(HALVES):
                                c0 = j * RANK + kt * P
                                m = pe.transpose(ps[:, 4 + j, kt * T + h * P:kt * T + (h + 1) * P], c_sb[:, h, c0:c0 + P], ident[:, :])
                        m.then_inc(cT_done, 1)
                    pe.wait_ge(cT_dve, 4)
                if b >= 2:
                    pe.wait_ge(block_act, b - 1)
                    pe.wait_ge(block_dve, b - 1)
                if name[0] == "u":
                    j = 1 if name.startswith("ukv") else 0
                    product(name, lambda kt, h: cT[:, j, kt, h * P:(h + 1) * P], cols, n)
                else:
                    product(name, left_h, cols, n)

            pe.wait_ge(dqk_ready, 2)
            pe.wait_ge(gate_in, 4)
            pe.wait_ge(block_act, 8)
            for i in range(DHEADS + 4):
                if i < DHEADS:
                    if i >= 2:
                        pe.wait_ge(hT_evac, i - 1)
                    for j, buf in enumerate((dq, dk)):
                        for h in range(HALVES):
                            m = pe.transpose(ps[:, i % 2, j * T + h * P:j * T + (h + 1) * P], buf[:, h, i * P:(i + 1) * P], ident[:, :])
                    m.then_inc(hT_done, 1)
                if 0 <= i - 1 < DHEADS:
                    u = i - 1
                    pe.wait_ge(hT_evac, u + 1)
                    if u >= 2:
                        pe.wait_ge(hS_read, 2 * u - 2)
                    for h in range(HALVES):
                        for mp in range(2):
                            r = slice(DQK * mp, DQK * (mp + 1))
                            m = pe.matmul(ps[:, 2 + 2 * (u % 2) + mp, h * T:(h + 1) * T], qkT[u % 2][r, h * P:(h + 1) * P],
                                          qkT[u % 2][r, T:2 * T], start=True, stop=True)
                    m.then_inc(hS_done, 1)
                if 0 <= i - 3 < DHEADS:
                    u = i - 3
                    pe.wait_ge(prob_ready, 2 * u + 2)
                    if u >= 1:
                        pe.wait_ge(hP_evac, u)
                    for kb in range(2):
                        for h in range(HALVES):
                            m = pe.transpose(ps[:, 6, kb * T + h * P:kb * T + (h + 1) * P], scores[u % 2][:, h, kb * P:(kb + 1) * P], ident[:, :])
                    m.then_inc(hP_done, 1)
                if 0 <= i - 4 < DHEADS:
                    u = i - 4
                    pe.wait_ge(hP_evac, u + 1)
                    if u >= 1:
                        pe.wait_ge(hO_evac, u)
                    for h in range(HALVES):
                        for kb in range(2):
                            m = pe.matmul(ps[:, 7, h * P:(h + 1) * P], pt_sb[u % 2][:, kb, h * P:(h + 1) * P],
                                          dv[:, kb, u * DV:(u + 1) * DV], start=kb == 0, stop=kb == 1)
                    m.then_inc(hO_done, 1)
            pe.wait_ge(qk_ready, 1)
            pe.wait_ge(hO_evac, DHEADS)
            for i in range(HEADS + 3):
                if i < HEADS:
                    u = DHEADS + i
                    pe.wait_ge(hT_evac, u - 1)
                    for j, buf in enumerate((q, kf)):
                        for h in range(HALVES):
                            m = pe.transpose(ps[0:QK, u % 2, j * T + h * P:j * T + (h + 1) * P], buf[:, h, i * QK:(i + 1) * QK], ident[:, :])
                    m.then_inc(hT_done, 1)
                if 0 <= i - 1 < HEADS:
                    u = DHEADS + i - 1
                    pe.wait_ge(hT_evac, u + 1)
                    if i >= 3:
                        pe.wait_ge(exp_done, u - 1)
                    for h in range(HALVES):
                        m = pe.matmul(ps[:, 2 + u % 2, h * T:(h + 1) * T], qkT[u % 2][0:QK, h * P:(h + 1) * P],
                                      qkT[u % 2][0:QK, T:2 * T], start=True, stop=True)
                    m.then_inc(hS_done, 1)
                if 0 <= i - 2 < HEADS:
                    u = DHEADS + i - 2
                    pe.wait_ge(exp_done, u + 1)
                    pe.wait_ge(hP_evac, u - 1)
                    for kb in range(2):
                        for h in range(HALVES):
                            m = pe.transpose(ps[:, 4 + u % 2, kb * T + h * P:kb * T + (h + 1) * P], scores[u % 2][:, h, kb * P:(kb + 1) * P], ident[:, :])
                    m.then_inc(hP_done, 1)
                if 0 <= i - 3 < HEADS:
                    hd = i - 3
                    u = DHEADS + hd
                    pe.wait_ge(hP_evac, u + 1)
                    pe.wait_ge(hO_evac, u - 1)
                    for h in range(HALVES):
                        for kb in range(2):
                            m = pe.matmul(ps[:, 6 + u % 2, h * VD:(h + 1) * VD], pt_sb[u % 2][:, kb, h * P:(h + 1) * P],
                                          kv[:, kb, hd * 128 + NOPE:(hd + 1) * 128], start=kb == 0, stop=kb == 1)
                    m.then_inc(hO_done, 1)

            pe.wait_ge(merged_ready, 2)
            transposes("merge", ga, 0)
            stage_ready("merge")
            product("out", left_h, D, 4)
            pe.wait_ge(xn_act, 1)
            pe.wait_ge(xn_dve, 1)
            transposes("ffn", xn, 0)
            stage_ready("ffn")
            for h in range(HALVES):
                for kt in range(KT):
                    m = pe.matmul(ps[:, 4, h * EXPERTS:(h + 1) * EXPERTS], left_h(kt, h), router[:, kt, :], start=kt == 0, stop=kt == KT - 1)
            m.then_inc(logit_done, 1)
            pe.wait_ge(aff_ready, 2)
            for h in range(HALVES):
                m = pe.transpose(ps[0:EXPERTS, 5, h * P:(h + 1) * P], aff[:, h, :], ident[:, :])
            m.then_inc(affT_done, 1)
            pe.wait_ge(slot_done, 1)
            for h in range(HALVES):
                m = pe.transpose(ps[:, 6, h * EXPERTS:(h + 1) * EXPERTS], routing[:, 4, h * P:(h + 1) * P], ident[0:EXPERTS, 0:EXPERTS])
            m.then_inc(slotT_done, 1)
            pe.wait_ge(onehot_ready, 2)
            for kt in range(KT):
                for h in range(HALVES):
                    m = pe.matmul(ps[:, kt, :], xn[:, h, kt * P:(kt + 1) * P], onehot[:, h, :], start=h == 0, stop=h == HALVES - 1)
                m.then_inc(gather_done, 1)
            pe.wait_ge(gather_act, KT // 2)
            pe.wait_ge(gather_dve, KT // 2)

            for s in (scat_done, hidT_done, e_scatter):
                pe.sem_inc(s, 1)
            with pe.Fori(0, EXPERTS) as e:
                def chunk_wait(k):
                    i = n_first + k
                    pe.wait_ge(slot_loaded[i % SLOTS], 16 * (EXPERT_CHUNKS // SLOTS) * e + landed(i))

                pe.wait_ge(gated_ready, 2 * e + 2)
                pe.wait_ge(ye_ready, e + 1)
                for h in range(HALVES):
                    m = pe.transpose(ps[:, 3, 256 + h * P:256 + (h + 1) * P], gated[:, h, :], ident[:, :])
                m.then_inc(scat_done, 1)
                pe.wait_ge(xe_ready, e + 1)
                pe.wait_ge(hid_ready, e + 1)
                for bank in range(2):
                    for kt in range(KT):
                        chunk_wait(bank * KT + kt)
                        w = ring[:, (n_first + bank * KT + kt) % SLOTS, :]
                        for j in range(4):
                            m = pe.matmul(ps[j * CAP:(j + 1) * CAP, bank, :], xe[:, kt, :], w[:, j * FCOL:(j + 1) * FCOL],
                                          start=kt == 0, stop=kt == KT - 1, skip_group_check=True)
                        m.then_inc(chunk_used, 1)
                pe.wait_ge(hid_ready, e + 2)
                for c in range(4):
                    m = pe.transpose(ps[:, 2, c * P:(c + 1) * P], hid[:, c * P:(c + 1) * P], ident[:, :])
                m.then_inc(hidT_done, 1)
                pe.wait_ge(scat_ready, e + 1)
                pe.wait_ge(hidT_ready, e + 1)
                for c in range(KT):
                    chunk_wait(2 * KT + c)
                    w = slot_view(n_first + 2 * KT + c, D)
                    for k in range(2):
                        ft = 2 * c + k
                        for j in range(4):
                            m = pe.matmul(ps[j * CAP:(j + 1) * CAP, 3, 0:DCOL], hidT[:, ft % 4, (ft // 4) * CAP:(ft // 4 + 1) * CAP],
                                          w[:, k, j * DCOL:(j + 1) * DCOL], start=ft == 0, stop=ft == FF // P - 1, skip_group_check=True)
                    m.then_inc(chunk_used, 1)
                pe.wait_ge(ye_ready, e + 2)
                pe.wait_ge(moe_added, e + 1)
                for h in range(HALVES):
                    for j in range(4):
                        m = pe.matmul(ps[:, 4 + j, h * DCOL:(h + 1) * DCOL], scat[j * CAP:(j + 1) * CAP, h * P:(h + 1) * P],
                                      ye[j * CAP:(j + 1) * CAP, :], start=True, stop=True)
                m.then_inc(e_scatter, 1)

            pe.wait_ge(xn_act, 2)
            pe.wait_ge(xn_dve, 2)
            transposes("mix", xn, 0)
            stage_ready("mix")
            product_T("conv", 768, 4)
            product("qk2", left_h, D, 4)
            pe.wait_ge(a_act, 2)
            pe.wait_ge(a_dve, 1)
            product("vuv", left_h, D, 4)
            pe.wait_ge(qk2_ready, 2)
            for j in range(SATT // P):
                for i in range(2):
                    for h in range(HALVES):
                        m = pe.transpose(ps[:, j, i * T + h * P:i * T + (h + 1) * P],
                                         qk2[:, h, i * SATT + j * P:i * SATT + (j + 1) * P], ident[:, :])
                m.then_inc(qkT2_done, 1)
            pe.wait_ge(qkT2_evac, SATT // P)
            pe.wait_ge(gelu_done, 4)
            pe.wait_ge(v_ready, 2)
            for i in range(SHEADS + 2):
                if i < SHEADS:
                    r = slice(SHD * (i % 2), SHD * (i % 2 + 1))
                    if i >= 2:
                        pe.wait_ge(lr_ready, i - 1)
                    pe.matmul(ps[:, 4 + i % 2, 0:T], qkT2[r, i // 2, T:T + P], qkT2[r, i // 2, 0:T], start=True, stop=True)
                    pe.matmul(ps[:, 4 + i % 2, T:SC], qkT2[r, i // 2, T + P:2 * T], qkT2[r, i // 2, P:T], start=True,
                              stop=True).then_inc(z_done, 1)
                if i == 0:
                    pe.wait_ge(cv_ready, 1)
                    for h in range(HALVES):
                        for g in range(SG):
                            w = SGU // SG
                            m = pe.matmul(ps[:, 2, h * SGU + g * w:h * SGU + (g + 1) * w], wsT[:, g, :], cv2[:, h, g * w:(g + 1) * w],
                                          start=True, stop=True)
                    m.then_inc(sv_done, 1)
                if 0 <= i - 1 < SHEADS:
                    u = i - 1
                    pe.wait_ge(lr_ready, u + 1)
                    if u >= 2:
                        pe.wait_ge(arg_ready, u - 1)
                    pe.matmul(ps[:, 6 + u % 2, 0:SC], later[:, :], lr[u % 2], start=True, stop=False)
                    pe.matmul(ps[:, 6 + u % 2, P:T], ones[:, :], lr[u % 2][:, T:SC], start=False, stop=True).then_inc(suf_done, 1)
                if 0 <= i - 2 < SHEADS:
                    u = i - 2
                    r = slice(SHD * (u % 2), SHD * (u % 2 + 1))
                    pe.wait_ge(w_ready, u + 1)
                    if u >= 4:
                        pe.wait_ge(yb_evac, u // 2 - 1)
                    pe.matmul(ps[r, (u // 2) % 2, 0:T], v2[:, 0, u * SHD:(u + 1) * SHD], lb[u % 3][:, 0:T], start=True, stop=False,
                              skip_group_check=True)
                    pe.matmul(ps[r, (u // 2) % 2, P:T], v2[:, 1, u * SHD:(u + 1) * SHD], lb[u % 3][:, T:SC], start=False, stop=True,
                              skip_group_check=True).then_inc(yb_done, 1)
            pe.wait_ge(yc_ready, SG)
            for kt in range(SGU // P):
                for h in range(HALVES):
                    m = pe.transpose(ps[:, 3, kt * T + h * P:kt * T + (h + 1) * P], yc[:, h, kt * P:(kt + 1) * P], ident[:, :])
            m.then_inc(ycT_done, 1)
            pe.wait_ge(conv_ready, 2)
            pe.wait_ge(yb_evac, SHEADS // 2)
            pe.wait_ge(ycT_evac, 1)
            pe.wait_ge(arg_ready, SHEADS)
            product("out2", lambda kt, h: yT[:, kt, h * P:(h + 1) * P], D, 4)
            pe.wait_ge(xn_act, 3)
            pe.wait_ge(xn_dve, 3)
            transposes("ff", xn, 0)
            stage_ready("ff")
            for b in range(4):
                if b >= 2:
                    pe.wait_ge(f_relu, 4 * (b - 1))
                product_T(f"up{b}", D, 4)
            pe.wait_ge(f_relu, 12)
            product("down", lambda kt, h: fT[:, kt, h * P:(h + 1) * P], D, DFF // (2 * P),
                    ready=lambda kt: pe.wait_ge(f_ready, kt // 2 + 1))
            pe.wait_ge(f_relu, 16)
            product("proj", lambda kt, h: pT[:, kt, h * P:(h + 1) * P], D, 1)
            pe.wait_ge(x_ready, 3)
            transposes("ple", xs, 4)
            stage_ready("ple")
            product("gate2", left_h, D, 4)


INPUTS = ["x", "positions", "attn_norm_w", "w_in", "b_gate", "mla_q_norm_w", "mla_w_uq", "mla_kv_norm_w", "mla_w_ukv",
          "mla_q_hnorm_w", "mla_k_hnorm_w", "diff_q_hnorm_w", "diff_k_hnorm_w", "diff_lambda", "diff_subln_w", "w_out",
          "ffn_norm_w", "router_w", "expert_w_gate", "expert_w_up", "expert_w_down", "p_2", "norm1_g_2", "w_in_2",
          "conv_w_2", "q_norm_g_2", "k_norm_g_2", "sgu_norm_g_2", "sgu_w_2", "sgu_b_2", "w_out_2", "norm2_g_2",
          "w_ff1_2", "w_ff2_2", "norm3_g_2", "w_ple_gate_2", "w_ple_proj_2"]


def kernel(**inputs):
    import numpy as np
    import concourse.bacc as bacc
    from concourse.bass_utils import run_bass_kernel_spmd

    nc = bacc.Bacc("TRN2", target_bir_lowering=False, num_devices=1)
    arrays, t = {}, {}
    for name in INPUTS:
        a = np.ascontiguousarray(inputs[name])
        arrays[f"in_{name}"] = a
        t[name] = nc.dram_tensor(f"in_{name}", a.shape, mybir.dt.from_np(a.dtype), kind="ExternalInput").ap()
    t["out"] = nc.dram_tensor("out_x", (1, T, D), F32, kind="ExternalOutput").ap()
    hybrid_blocks(nc, t)
    result = run_bass_kernel_spmd(nc, [arrays], core_ids=[0])
    return result.results[0]["out_x"]
```

```python
from contextlib import ExitStack
import math

import concourse.bass as bass
import concourse.mybir as mybir

F32 = mybir.dt.float32
F32R = mybir.dt.float32r
I32 = mybir.dt.int32
ALU = mybir.AluOpType
ACT = mybir.ActivationFunctionType
AX = mybir.AxisListType.X

P = 128
T = 256
HALVES = T // P
D = 1024
KT = D // P
EPS = 1e-6

HEADS, QK, NOPE, ROPE, VD = 16, 96, 64, 32, 64
HR = ROPE // 2
RANK = 256
RT = RANK // P
C_COLS = 2 * RANK + ROPE
THETA = 10000.0
DHEADS, DQK, DV = 8, 64, 128
LAM_INIT = 0.8 - 0.6 * math.exp(-0.3 * 0)

EXPERTS, CAP, FF = 16, 32, 2048
FCOL = FF // 4
DCOL = D // 4

CONV, CONVW = 256, 3
SHEADS, SHD = 8, 64
SATT = SHEADS * SHD
SGU, SG = 256, 4
DFF = 4096
PLE = 256

SLOTS, SLOT = 8, 2048
EXPERT_CHUNKS = 3 * KT
assert EXPERT_CHUNKS % SLOTS == 0
DENSE_SLOTS = 5
WBUFS = SLOTS - DENSE_SLOTS
SBUF_BASE = 16512

VEC_ROWS = [("attn_norm_w", 8), ("mla_q_norm_w", 2), ("mla_kv_norm_w", 2), ("ffn_norm_w", 8), ("norm1_g_2", 8),
            ("norm2_g_2", 8), ("norm3_g_2", 8), ("conv_w_2", 6), ("sgu_b_2", 4), ("diff_q_hnorm_w", 1),
            ("diff_k_hnorm_w", 1)]
VEC = {}
for _name, _rows in VEC_ROWS:
    VEC[_name] = sum(r for _, r in VEC_ROWS[:len(VEC)])
NVEC = sum(r for _, r in VEC_ROWS)

ROW_VECS = [("mla_q_hnorm_w", QK), ("mla_k_hnorm_w", QK),
            ("diff_subln_w", DV), ("q_norm_g_2", SHD), ("k_norm_g_2", SHD), ("sgu_norm_g_2", SGU),
            ("diff_lambda", 4 * DQK)]
ROW = {}
for _name, _n in ROW_VECS:
    ROW[_name] = sum(n for _, n in ROW_VECS[:len(ROW)])
NROW = sum(n for _, n in ROW_VECS)

INV_FREQ = [1.0 / THETA ** (2 * i / ROPE) for i in range(HR)]
TWO_PI_PARTS = (6.28125, 0.0019350051879882812, 3.0199157663446332e-07)
ROUND = 1.5 * 2.0 ** 23
PI_BELOW = 3.1415925
RSQRT_MAGIC = float(0x5F3759DF)


def hybrid_blocks(nc, t):
    ctx = ExitStack()
    with ctx:
        used = [SBUF_BASE]

        def sb(name, shape, dt=F32):
            v = nc.alloc_sbuf_tensor_at(name, shape, dt, offset=used[0]).ap()
            used[0] += (math.prod(shape[1:]) * 4 + 31) // 32 * 32
            return v

        def sem(name):
            return ctx.enter_context(nc.semaphore(name))

        ring = sb("ring", [P, SLOTS, SLOT])
        w_split = nc.alloc_sbuf_tensor_at("w_split", [P, WBUFS, 2, SLOT // 2], F32R,
                                          offset=SBUF_BASE + DENSE_SLOTS * SLOT * 4).ap()
        xs = sb("xs", [P, HALVES, D])
        xn = sb("xn", [P, HALVES, D])
        hT_at = used[0]
        hT_hi, hT_lo = sb("hT_hi", [P, KT, T], F32R), sb("hT_lo", [P, KT, T], F32R)
        xn_hi, xn_lo = (nc.alloc_sbuf_tensor_at(n, [P, HALVES, D], F32R, offset=hT_at + i * HALVES * D * 4).ap()
                        for i, n in enumerate(("xn_hi", "xn_lo")))
        ident = sb("ident", [P, P])
        ones = sb("ones", [P, P])
        later = sb("later", [P, P])
        tri = sb("tri", [P, P])
        tril = sb("tril", [P, P])
        slot_ids = sb("slot_ids", [P, P])
        vec_rows = sb("vec_rows", [NVEC, P])
        vec = sb("vec", [P, NVEC])
        row = sb("row", [P, NROW])
        router = sb("router", [P, KT, EXPERTS])
        stat = sb("stat", [P, 640])
        arena_at = used[0]
        arena = sb("arena", [P, 25 * 1024])
        ps = ctx.enter_context(nc.psum_tensor("ps", [P, 8, 512], F32))
        psf = ps[:, :, :].rearrange("p b n -> p (b n)")

        def at(off, *shape):
            n = math.prod(shape)
            v = arena[:, off:off + n]
            names = "abcd"[:len(shape)]
            if len(shape) > 1:
                v = v.rearrange(f"p ({' '.join(names)}) -> p {' '.join(names)}", **dict(zip(names, shape)))
            return v

        def split_at(name, off, *shape):
            return nc.alloc_sbuf_tensor_at(name, [P, *shape], F32R, offset=arena_at + off * 4).ap()

        K = 1024
        dq = at(0, HALVES, D)
        dk = at(2 * K, HALVES, D)
        dv = at(4 * K, HALVES, D)
        q = at(6 * K, HALVES, HEADS * QK)
        v1 = at(9 * K, HALVES, HEADS * VD)
        kf = at(11 * K, HALVES, HEADS * QK)
        ga = at(14 * K, HALVES, D)
        gb = at(16 * K, HALVES, D)
        c_sb = at(18 * K, HALVES, C_COLS)
        cT = [split_at(n, 18 * K + 1152 + i * K, 2, RT, T) for i, n in enumerate(("cT_hi", "cT_lo"))]
        qkT = [at(18 * K + i * 512, 512) for i in range(2)]
        pt_sb = [at(19 * K + i * 512, 2, T) for i in range(2)]
        rope_t = [at(20 * K + i * 512, HALVES, HEADS, HR) for i in range(2)]
        bgate = at(21 * K + 128, D)
        scores = [at(22 * K + 128 + i * K, 4, T) for i in range(2)]
        dist = at(24 * K + 128, HALVES, T)
        trig = at(24 * K + 640, 6, HALVES * HR)
        kr = at(24 * K + 832, HALVES, ROPE)
        posb = at(6 * K, 4, T)
        posi = at(7 * K, 3, T).bitcast(I32)
        onehot = split_at("onehot", 0, HALVES, EXPERTS * CAP)
        xT_all = at(1 * K, KT, EXPERTS * CAP)
        xe = at(5 * K, KT, CAP)
        hid_g = at(5 * K + 256, FCOL)
        hid = at(5 * K + 768, FCOL)
        hidT = at(6 * K + 256, 4, P)
        gated = at(6 * K + 768, HALVES, P)
        scat = at(7 * K, T)
        ye = at(7 * K + 256, DCOL)
        logit = at(7 * K + 512, HALVES, EXPERTS)
        aff = at(7 * K + 576, HALVES, EXPERTS)
        slot_t = at(7 * K + 640, HALVES, EXPERTS)
        routing = at(8 * K, 6, T)[0:EXPERTS]
        sgu_in = at(22 * K, SG, P)
        p_in = at(22 * K + 512, HALVES, PLE)
        wsT = at(23 * K, SG, P)
        p_f = at(23 * K + 512, PLE // P, T)
        pT = [split_at(n, 24 * K + i * 512, PLE // P, T) for i, n in enumerate(("pT_hi", "pT_lo"))]
        yT = [split_at(n, i * 2 * K, KT, T) for i, n in enumerate(("yT_hi", "yT_lo"))]
        a_bT = at(4 * K, 2, T)
        a_hT = at(4 * K + 512, 2, T)
        conv = at(5 * K, 2, T + CONVW - 1)
        conv_y = at(5 * K + 520, T)
        qk2 = at(7 * K, HALVES, 2 * SATT)
        v2 = at(9 * K, HALVES, SATT)
        u2 = at(10 * K, HALVES, SGU)
        cv2 = at(10 * K + 512, HALVES, SGU)
        qkT2 = at(11 * K, SATT // P, 512)
        SC = 384
        na = [at(13 * K + i * SC, SC) for i in range(2)]
        spl = [at(14 * K + i * SC, SC) for i in range(2)]
        lb = [at(15 * K + i * SC, SC) for i in range(3)]
        lr = [at(16 * K + 128 + i * SC, SC) for i in range(2)]
        yc = at(17 * K, HALVES, SGU)
        fT = [split_at(n, i * 8 * K, DFF // P, T) for i, n in enumerate(("fT_hi", "fT_lo"))]
        f_r = [at(16 * K + i * 512, 2 * T) for i in range(2)]
        f_2 = at(17 * K, 2 * T)
        pe_sb = at(18 * K, HALVES, D)
        gate2 = at(20 * K, HALVES, D)
        sq = xn[:, :, :].rearrange("p h d -> p (h d)")

        ss_x, rstd_x = stat[:, 0:2], stat[:, 2:4]
        ss_c, rstd_c = stat[:, 4:8], stat[:, 8:12]
        ss_h, rstd_h = stat[:, 312:376], stat[:, 376:440]
        mxn = [stat[:, 80 + 4 * i:84 + 4 * i] for i in range(2)]
        sums = [stat[:, 88 + 4 * i:92 + 4 * i] for i in range(2)]
        rec = [stat[:, 96 + 4 * i:100 + 4 * i] for i in range(2)]
        lam, lam_s = stat[:, 104:105], stat[:, 106:108]
        qk_w = stat[:, 126:127]
        freq = stat[:, 108:124]
        posc_f = stat[:, 128:136]
        nw = [stat[:, 440 + 64 * i:504 + 64 * i] for i in range(3)]
        ss_kr = stat[:, 232:234]
        ss_d, rstd_d = stat[:, 16:48], stat[:, 48:80]
        ss_o, rstd_o = stat[:, 272:288], stat[:, 288:304]
        rmax, rsum, rinv = stat[:, 304:306], stat[:, 306:308], stat[:, 308:310]
        rstd_0 = stat[:, 310:312]
        posc = sb("posc", [P, HALVES, 3], I32)
        top8 = sb("top8", [EXPERTS, 4, 8])
        rcount = sb("rcount", [EXPERTS, 2])

        slot_loaded = [sem(f"slot_loaded{i}") for i in range(SLOTS)]
        chunk_used = sem("chunk_used")
        split_hi, split_lo, tile_used = sem("split_hi"), sem("split_lo"), sem("tile_used")
        chunk_split = sem("chunk_split")
        x_loaded, vec_loaded, small_loaded = sem("x_loaded"), sem("vec_loaded"), sem("small_loaded")
        late_loaded, pw_raw = sem("late_loaded"), sem("pw_raw")
        gate_bias_loaded = sem("gate_bias_loaded")
        masks_ready = sem("masks_ready")
        vec_done, vec_ready = sem("vec_done"), sem("vec_ready")
        pw_done, pw_ready = sem("pw_done"), sem("pw_ready")
        tr_done, hi_ready, lo_ready = sem("tr_done"), sem("hi_ready"), sem("lo_ready")
        sq_act, rstd_ready = sem("sq_act"), sem("rstd_ready")
        xn_dve, xn_act, x_ready = sem("xn_dve"), sem("xn_act"), sem("x_ready")
        block_dve, block_act = sem("block_dve"), sem("block_act")
        sq_ready, sq_read = sem("sq_ready"), sem("sq_read")
        c_sq, c_norm = sem("c_sq"), sem("c_norm")
        cT_done, cT_hi, cT_lo = sem("cT_done"), sem("cT_hi"), sem("cT_lo")
        dqk_ready, qk_ready = sem("dqk_ready"), sem("qk_ready")
        lam_in, lam_exp = sem("lam_in"), sem("lam_exp")
        angle_ready, trig_ready = sem("angle_ready"), sem("trig_ready")
        gate_in, gate_ready = sem("gate_in"), sem("gate_ready")
        hT_done, hT_evac, hS_done, hS_read = sem("hT_done"), sem("hT_evac"), sem("hS_done"), sem("hS_read")
        max_ready, exp_done, prob_ready = sem("max_ready"), sem("exp_done"), sem("prob_ready")
        hP_done, hP_evac, hO_done, hO_evac = sem("hP_done"), sem("hP_evac"), sem("hO_done"), sem("hO_evac")
        od_sums, od_root, od_ready, merged_ready = sem("od_sums"), sem("od_root"), sem("od_ready"), sem("merged_ready")
        logit_done, rmax_ready, rexp_done, aff_ready = sem("logit_done"), sem("rmax_ready"), sem("rexp_done"), sem("aff_ready")
        affT_done, slot_done, slotT_done, onehot_ready = sem("affT_done"), sem("slot_done"), sem("slotT_done"), sem("onehot_ready")
        gather_done, gather_dve, gather_act = sem("gather_done"), sem("gather_dve"), sem("gather_act")
        xe_ready, silu_done, hid_ready = sem("xe_ready"), sem("silu_done"), sem("hid_ready")
        hidT_done, hidT_ready, ye_ready = sem("hidT_done"), sem("hidT_ready"), sem("ye_ready")
        gated_ready, scat_done, scat_ready = sem("gated_ready"), sem("scat_done"), sem("scat_ready")
        e_scatter, moe_added = sem("e_scatter"), sem("moe_added")
        a_act, a_dve, conv_ready = sem("a_act"), sem("a_dve"), sem("conv_ready")
        gelu_done, v_ready = sem("gelu_done"), sem("v_ready")
        qk2_ready, qkT2_done, qkT2_evac = sem("qk2_ready"), sem("qkT2_done"), sem("qkT2_evac")
        z_done, sp_ready, lr_ready = sem("z_done"), sem("sp_ready"), sem("lr_ready")
        suf_done, arg_ready, w_exp, w_ready = sem("suf_done"), sem("arg_ready"), sem("w_exp"), sem("w_ready")
        yb_done, yb_evac, y_ready = sem("yb_done"), sem("yb_evac"), sem("y_ready")
        cv_ready, sv_done, yc_ready, ycT_done, ycT_hi = sem("cv_ready"), sem("sv_done"), sem("yc_ready"), sem("ycT_done"), sem("ycT_hi")
        f_relu, f_hi, f_ready = sem("f_relu"), sem("f_hi"), sem("f_ready")
        xn_hi_ready, xn_lo_ready = sem("xn_hi_ready"), sem("xn_lo_ready")
        proj_out = sem("proj_out")
        gate2_ready, out_ready, out_stored = sem("gate2_ready"), sem("out_ready"), sem("out_stored")
        dve_step, act_step, pool_step = sem("dve_step"), sem("act_step"), sem("pool_step")

        FIRST_BLOCK = [("c", "w_in", 0, C_COLS, D, "B"), ("dq", "w_in", C_COLS, D, D, "A"),
                       ("uq0", "mla_w_uq", 0, 768, RANK, "B"), ("uq1", "mla_w_uq", 768, 768, RANK, "A"),
                       ("ukv0", "mla_w_ukv", 0, 1024, RANK, "B"), ("ukv1", "mla_w_ukv", 1024, 1024, RANK, "A"),
                       ("dk", "w_in", C_COLS + D, D, D, "B"), ("dv", "w_in", C_COLS + 2 * D, D, D, "A"),
                       ("gate_a", "w_in", C_COLS + 3 * D, D, D, "A"), ("gate_b", "w_in", C_COLS + 4 * D, D, D, "A"),
                       ("out", "w_out", 0, D, D, "B")]
        SECOND_BLOCK = [("qk2", "w_in_2", 768, 1024, D, "B"), ("v2", "w_in_2", 1792, 512, D, "A"),
                        ("cuv", "w_in_2", 2304, 512, D, "A"), ("conv", "w_in_2", 0, 768, D, "A"),
                        ("out2", "w_out_2", 0, D, D, "A"), ("proj", "w_ple_proj_2", 0, D, PLE, "B"),
                        ("up0", "w_ff1_2", 0, D, D, "B"), ("up1", "w_ff1_2", D, D, D, "A"),
                        ("up2", "w_ff1_2", 2 * D, D, D, "B"), ("up3", "w_ff1_2", 3 * D, D, D, "A"),
                        ("down", "w_ff2_2", 0, D, DFF, "B"), ("gate2", "w_ple_gate_2", 0, D, D, "B")]
        CHUNK_ORDER = {"out2": [3, 0, 1, 2]}
        TILE0, TILES, COLS, SETS = {}, {}, {}, {}
        chunks = []
        for name, weight, c0, cols, rows, banks in FIRST_BLOCK + SECOND_BLOCK:
            if name == "qk2":
                n_first = len(chunks)
            TILE0[name], TILES[name], COLS[name], SETS[name] = 2 * len(chunks), rows // P, cols, banks
            for k in CHUNK_ORDER.get(name, range(rows // (2 * P))):
                chunks.append(t[weight][0][2 * k * P:2 * (k + 1) * P, c0:c0 + cols].rearrange("(k p) c -> p k c", p=P))

        def done(name):
            return TILE0[name] + TILES[name]

        def slot_view(slot, cols):
            return ring[:, slot, 0:2 * cols].rearrange("p (k c) -> p k c", k=2)

        def landed(i):
            return 16 * (i // DENSE_SLOTS + 1 + (0 if i < n_first else EXPERTS * EXPERT_CHUNKS // SLOTS))

        def expert_landed(k):
            before = len(range(k % SLOTS, n_first, DENSE_SLOTS)) if k % SLOTS < DENSE_SLOTS else 0
            return 16 * (before + k // SLOTS + 1)

        ALL_EXPERTS = SLOTS + EXPERTS * EXPERT_CHUNKS

        SET = {"A": 0, "B": 4}

        def pset(s, h, n=D):
            return psf[:, 512 * SET[s] + h * D:512 * SET[s] + h * D + n]

        block = ctx.enter_context(nc.Block())

        @block.sync
        def _(sp):
            x_dram = t["x"][0].rearrange("(h p) d -> p h d", p=P)
            sp.dma_start(xs[:, :, :], x_dram).then_inc(x_loaded, 16)

            def load(i):
                slot = i % DENSE_SLOTS
                if i >= n_first and i - DENSE_SLOTS < n_first:
                    sp.wait_ge(chunk_used, ALL_EXPERTS - SLOTS + slot + 1)
                elif i >= DENSE_SLOTS:
                    sp.wait_ge(chunk_split, i - DENSE_SLOTS + 1)
                sp.dma_start(slot_view(slot, chunks[i].shape[2]), chunks[i]).then_inc(slot_loaded[slot], 16)

            for i in range(n_first):
                load(i)
            with sp.Fori(0, EXPERTS) as e:
                for k in range(EXPERT_CHUNKS):
                    m, kt, slot = k // KT, k % KT, k % SLOTS
                    if m < 2:
                        w = t["expert_w_gate" if m == 0 else "expert_w_up"]
                        src = w[0, e, kt * P:(kt + 1) * P, :]
                        dst = ring[:, slot, :]
                    else:
                        src = t["expert_w_down"][0, e, 2 * kt * P:(2 * kt + 2) * P, :].rearrange("(k p) c -> p k c", p=P)
                        dst = slot_view(slot, D)
                    sp.wait_ge(chunk_used, EXPERT_CHUNKS * e + k + 1)
                    sp.dma_start(dst, src).then_inc(slot_loaded[slot], 16)
            for i in range(n_first, len(chunks)):
                load(i)
            for h in range(HALVES):
                sp.wait_ge(out_ready, h + 1)
                sp.dma_start(t["out"][0, h * P:(h + 1) * P, :], gate2[:, h, :]).then_inc(out_stored, 16)
            sp.wait_ge(out_stored, 16 * HALVES)

        N_VEC = len(VEC_ROWS) + 2
        N_SMALL = len(ROW_VECS) + 5
        N_MASKS = 7
        STAGES = ["attn", "merge", "ffn", "mix", "ff", "ple"]
        EVACS = ["c", "dq", "uq0", "uq1", "ukv0", "ukv1", "dk", "dv", "qk2"]

        def evacuated(name):
            return EVACS.index(name) + 1

        @block.gpsimd
        def _(pool):
            count = [0]

            def step(ins):
                count[0] += 1
                ins.then_inc(pool_step, 1)
                pool.wait_ge(pool_step, count[0])

            def mask(buf, fill_in, fill_out, op, pattern, mult):
                step(pool.memset(buf[:, :], fill_in))
                pool.affine_select(out=buf[:, :], in_=buf[:, :], compare_op=op, fill=fill_out, base=0,
                                   pattern=pattern, channel_multiplier=mult).then_inc(masks_ready, 1)

            def low_parts(name, k0=0, k1=None):
                cols = COLS[name]
                for kt in range(k0, TILES[name] if k1 is None else k1):
                    n = TILE0[name] + kt
                    w = slot_view(n // 2 % DENSE_SLOTS, cols)[:, n % 2, :]
                    buf = w_split[:, n % WBUFS, :, 0:cols]
                    pool.wait_ge(split_hi, n + 1)
                    ins = pool.tensor_tensor(buf[:, 1, :], w, buf[:, 0, :].bitcast(F32), ALU.subtract)
                    ins.then_inc(split_lo, 1)
                    if n % 2:
                        pool.wait_ge(split_lo, n + 1)
                        pool.sem_inc(chunk_split, 1)

            mask(ident, 0.0, 1.0, ALU.not_equal, [[-1, P]], 1)
            mask(tril, 1.0, 0.0, ALU.is_ge, [[1, P]], -1)
            mask(tri, 1.0, 0.0, ALU.is_gt, [[1, P]], -1)
            mask(later, 1.0, 0.0, ALU.is_gt, [[-1, P]], 1)
            pool.memset(ones[:, :], 1.0).then_inc(masks_ready, 1)
            pool.iota(slot_ids[:, :].rearrange("p (j s) -> p j s", s=CAP), pattern=[[0, P // CAP], [1, CAP]], base=0,
                      channel_multiplier=0, allow_small_or_imprecise_dtypes=True).then_inc(masks_ready, 1)
            for i in range(HR):
                f = pool.memset(freq[:, i:i + 1], INV_FREQ[i])
            f.then_inc(masks_ready, 1)

            for name in ("c", "dq", "uq0", "uq1", "ukv0", "ukv1", "dk", "dv", "gate_a"):
                low_parts(name)
            low_parts("gate_b", 0, 4)

            wl = row[:, ROW["diff_subln_w"]:ROW["diff_subln_w"] + DV]
            pool.wait_ge(small_loaded, 16 * N_SMALL)
            step(pool.tensor_scalar(wl, wl, 1.0 - LAM_INIT, None, ALU.mult))
            pool.wait_ge(hO_evac, DHEADS)
            pool.wait_ge(sq_read, 5)
            for h in range(HALVES):
                pool.tensor_tensor(xn[:, h, :], dq[:, h, :], dq[:, h, :], ALU.mult).then_inc(od_sums, 1)
                low_parts("gate_b", 4 + h, 5 + h)
            pool.wait_ge(od_root, 1)
            for h in range(HALVES):
                od = dq[:, h, :].rearrange("p (n d) -> p n d", d=DV)
                r = rstd_o[:, h * DHEADS:(h + 1) * DHEADS]
                step(pool.tensor_tensor(od, od, r.unsqueeze(2).to_broadcast([P, DHEADS, DV]), ALU.mult))
                low_parts("gate_b", 6 + h, 7 + h)
                step(pool.tensor_tensor(od, od, wl.unsqueeze(1).to_broadcast([P, DHEADS, DV]), ALU.mult))
            low_parts("out", 0, 3)
            pool.wait_ge(gate_ready, 2)
            for h in range(HALVES):
                pool.tensor_tensor(dq[:, h, :], dq[:, h, :], gb[:, h, :], ALU.mult).then_inc(od_ready, 1)
            low_parts("out", 3)

            pool.wait_ge(xn_hi_ready, HALVES)
            for h in range(HALVES):
                pool.tensor_tensor(xn_lo[:, h, :], xn[:, h, :], xn_hi[:, h, :].bitcast(F32), ALU.subtract).then_inc(xn_lo_ready, 1)
            pool.wait_ge(pw_raw, 3)
            step(pool.tensor_tensor(wsT, wsT, tril[:, :].unsqueeze(1).to_broadcast([P, SG, P]), ALU.mult))
            pool.tensor_tensor(pT[1], p_f, pT[0].bitcast(F32), ALU.subtract).then_inc(pw_ready, 1)

            for name, *_ in SECOND_BLOCK:
                low_parts(name)

        @block.scalar
        def _(act):
            for name, rows in VEC_ROWS:
                src = t[name]
                if name.startswith("diff"):
                    for i in range(2):
                        act.dma_start(vec_rows[VEC[name]:VEC[name] + 1, i * DQK:(i + 1) * DQK], src).then_inc(vec_loaded, 16)
                    continue
                src = src[0].rearrange("w (r c) -> (w r) c", c=P) if name == "conv_w_2" else (
                    src[0] if name == "sgu_b_2" else src[0].rearrange("(r c) -> r c", c=P))
                act.dma_start(vec_rows[VEC[name]:VEC[name] + rows, :], src).then_inc(vec_loaded, 16)
            act.dma_start(posi[:, 0, :], t["positions"][0].partition_broadcast(P)).then_inc(small_loaded, 16)
            for h in range(HALVES):
                act.dma_start(posc[:, h, 0:1], t["positions"][0, h * P:(h + 1) * P].rearrange("(p o) -> p o", o=1)
                              ).then_inc(small_loaded, 16)
            for name, n in ROW_VECS:
                src = t[name][0]
                src = src.rearrange("a b -> (a b)") if name == "diff_lambda" else src
                act.dma_start(row[:, ROW[name]:ROW[name] + n], src.partition_broadcast(P)).then_inc(small_loaded, 16)
            act.dma_start(bgate, t["b_gate"][0, 0:D].partition_broadcast(P)).then_inc(small_loaded, 16)
            act.dma_start(router[:, :, :], t["router_w"][0].rearrange("(k p) e -> p k e", p=P)).then_inc(small_loaded, 16)

            def high_parts(name, k0=0, k1=None):
                cols = COLS[name]
                for kt in range(k0, TILES[name] if k1 is None else k1):
                    n = TILE0[name] + kt
                    i, slot = n // 2, n // 2 % DENSE_SLOTS
                    act.wait_ge(slot_loaded[slot], landed(i))
                    if n >= WBUFS:
                        act.wait_ge(tile_used, n - WBUFS + 1)
                    act.activation(w_split[:, n % WBUFS, 0, 0:cols], slot_view(slot, cols)[:, n % 2, :],
                                   ACT.Copy).then_inc(split_hi, 1)

            def square_half():
                act.activation(xn[:, 0, :], xs[:, 0, :], ACT.Square, accum_out=ss_x[:, 0:1]).then_inc(sq_act, 1)

            def scale_half(n):
                act.wait_ge(rstd_ready, n + 1)
                act.activation(xn[:, 0, :], xs[:, 0, :], ACT.Copy, scale=rstd_x[:, 0:1]).then_inc(xn_act, 1)

            def high_stage(s, base, weight):
                for kt in range(KT):
                    if kt % 2 == 0:
                        act.wait_ge(tr_done, 4 * STAGES.index(s) + kt // 2 + 1)
                    scale = vec[:, VEC[weight] + kt:VEC[weight] + kt + 1] if weight else 1.0
                    act.activation(hT_hi[:, kt, :], ps[:, base + kt // 2, (kt % 2) * T:(kt % 2 + 1) * T], ACT.Copy,
                                   scale=scale).then_inc(hi_ready, 1)

            def evac(name, *parts):
                act.wait_ge(tile_used, done(name))
                scale = rstd_0[:, 0:1] if name[0] in "cd" else 1.0
                src = pset(SETS[name], 0, COLS[name])
                for dst, cut in parts:
                    ins = act.activation(dst, cut(src), ACT.Copy, scale=scale)
                ins.then_inc(block_act, 1)

            def squares(n, src, dst):
                if n:
                    act.wait_ge(sq_read, n)
                act.activation(dst, src, ACT.Square).then_inc(sq_ready, 1)

            def whole(src):
                return src

            act.wait_ge(x_loaded, 16)
            square_half()
            high_parts("c", 0, 3)
            act.wait_ge(vec_ready, 1)
            high_stage("attn", 0, "attn_norm_w")
            high_parts("c", 3)
            high_parts("dq", 0, 3)
            act.wait_ge(rstd_ready, 1)
            evac("c", (c_sb[:, 0, :], whole))
            act.wait_ge(block_act, evacuated("c"))
            act.wait_ge(block_dve, evacuated("c"))
            for j in range(2):
                for h in range(HALVES):
                    act.activation(sq[:, (2 * j + h) * RANK:(2 * j + h + 1) * RANK], c_sb[:, h, j * RANK:(j + 1) * RANK], ACT.Square,
                                   accum_out=ss_c[:, 2 * j + h:2 * j + h + 1]).then_inc(c_sq, 1)
            for h in range(HALVES):
                act.activation(sq[:, D + h * ROPE:D + (h + 1) * ROPE], c_sb[:, h, 2 * RANK:C_COLS], ACT.Square,
                               accum_out=ss_kr[:, h:h + 1]).then_inc(c_sq, 1)
            high_parts("dq", 3)
            for j in range(2):
                act.wait_ge(cT_done, j + 1)
                for kt in range(RT):
                    w = VEC["mla_q_norm_w" if j == 0 else "mla_kv_norm_w"] + kt
                    act.activation(cT[0][:, j, kt, :], ps[:, 4 + j, kt * T:(kt + 1) * T], ACT.Copy,
                                   scale=vec[:, w:w + 1]).then_inc(cT_hi, 1)
            high_parts("uq0")
            high_parts("uq1", 0, 1)
            evac("dq", (dq[:, 0, :], whole))
            act.wait_ge(block_act, evacuated("dq"))
            act.wait_ge(block_dve, evacuated("dq"))
            act.wait_ge(c_norm, 4)
            squares(0, dq.rearrange("p h d -> p (h d)"), sq)
            high_parts("uq1", 1)
            act.wait_ge(lam_in, 1)
            act.activation(lam_s, lam_s, ACT.Exp).then_inc(lam_exp, 1)
            act.wait_ge(angle_ready, 1)
            act.activation(trig[:, 4:6, :], trig[:, 4:6, :], ACT.Sin).then_inc(trig_ready, 1)
            high_parts("ukv0")
            evac("uq0", (q[:, 0, 0:768], whole))
            high_parts("ukv1", 0, 1)
            evac("uq1", (q[:, 0, 768:1536], whole))
            high_parts("ukv1", 1)
            high_parts("dk", 0, 1)

            def kv_parts(h, i):
                heads = slice(i * HEADS // 2, (i + 1) * HEADS // 2)
                k_out = kf[:, h, :].rearrange("p (n d) -> p n d", d=QK)[:, heads, 0:NOPE]
                v_out = v1[:, h, :].rearrange("p (n d) -> p n d", d=VD)[:, heads, :]
                return ((k_out, lambda src: src.rearrange("p (n d) -> p n d", d=128)[:, :, 0:NOPE]),
                        (v_out, lambda src: src.rearrange("p (n d) -> p n d", d=128)[:, :, NOPE:128]))

            evac("ukv0", *kv_parts(0, 0))
            high_parts("dk", 1, 3)
            evac("ukv1", *kv_parts(0, 1))
            act.wait_ge(block_act, evacuated("ukv1"))
            act.wait_ge(block_dve, evacuated("ukv1"))
            squares(1, q[:, 0, :], sq[:, 0:HEADS * QK])
            high_parts("dk", 3, 5)
            squares(2, q[:, 1, :], sq[:, 0:HEADS * QK])
            high_parts("dk", 5, 7)
            squares(3, kf.rearrange("p h (n d) -> p (h n) d", d=QK)[:, :, 0:NOPE], sq.rearrange("p (n d) -> p n d", d=NOPE))
            high_parts("dk", 7)
            high_parts("dv", 0, 3)
            evac("dk", (dk[:, 0, :], whole))
            act.wait_ge(block_act, evacuated("dk"))
            act.wait_ge(block_dve, evacuated("dk"))
            squares(4, dk.rearrange("p h d -> p (h d)"), sq)
            high_parts("dv", 3)
            high_parts("gate_a", 0, 3)
            evac("dv", (dv[:, 0, :], whole))

            for i in range(DHEADS + 4):
                if i < DHEADS:
                    act.wait_ge(hT_done, i + 1)
                    if i >= 2:
                        act.wait_ge(hS_done, i - 1)
                    act.activation(qkT[i % 2][:, 0:T], ps[:, 4, 0:T], ACT.Copy, scale=qk_w)
                    act.activation(qkT[i % 2][:, T:2 * T], ps[:, 4, T:2 * T], ACT.Copy).then_inc(hT_evac, 1)
                if i + 3 < DHEADS:
                    high_parts("gate_a", i + 3, i + 4)
                if DHEADS <= i < DHEADS + 3:
                    high_parts("gate_b", i - DHEADS, i - DHEADS + 1)
                if 0 <= i - 3 < DHEADS:
                    u = i - 3
                    act.wait_ge(hP_done, u + 1)
                    if u >= 2:
                        act.wait_ge(hO_done, u - 1)
                    act.activation(pt_sb[u % 2], ps[:, 7, :].rearrange("p (k t) -> p k t", k=2), ACT.Copy).then_inc(hP_evac, 1)
                if 0 <= i - 1 < DHEADS:
                    u = i - 1
                    act.wait_ge(max_ready, u + 1)
                    for j in range(4):
                        e = act.activation(scores[u % 2][:, j, :], scores[u % 2][:, j, :], ACT.Exp,
                                           bias=mxn[u % 2][:, j:j + 1], accum_out=sums[u % 2][:, j:j + 1])
                    e.then_inc(exp_done, 1)
                if 0 <= i - 4 < DHEADS:
                    u = i - 4
                    act.wait_ge(hO_done, u + 1)
                    act.activation(dq[:, :, u * DV:(u + 1) * DV],
                                   ps[:, 4, 0:T].rearrange("p (h d) -> p h d", h=2),
                                   ACT.Copy).then_inc(hO_evac, 1)
                if i == DHEADS + 2:
                    act.wait_ge(gate_in, 2)
                    act.activation(ga, ga, ACT.Sigmoid).then_inc(gate_ready, 1)
                    act.dma_start(bgate, t["b_gate"][0, D:2 * D].partition_broadcast(P)).then_inc(gate_bias_loaded, 16)
            for i in range(HEADS + 1):
                if i < HEADS:
                    u = DHEADS + i
                    act.wait_ge(hT_done, u + 1)
                    act.wait_ge(hS_done, u - 1)
                    act.activation(qkT[u % 2][0:QK, :], ps[0:QK, 4, :], ACT.Copy).then_inc(hT_evac, 1)
                if i % 2 == 0:
                    if i // 2 + 3 < KT:
                        high_parts("gate_b", i // 2 + 3, i // 2 + 4)
                    elif 12 <= i:
                        high_parts("out", i // 2 - 6, i // 2 - 5)
                if i >= 1:
                    u = DHEADS + i - 1
                    act.wait_ge(max_ready, u + 1)
                    act.wait_ge(hP_done, u - 1)
                    for h in range(HALVES):
                        e = act.activation(scores[u % 2][:, h, :], ps[:, 5, h * T:(h + 1) * T], ACT.Exp,
                                           bias=mxn[u % 2][:, h:h + 1], scale=QK ** -0.5, accum_out=sums[u % 2][:, h:h + 1])
                    e.then_inc(exp_done, 1)
            act.wait_ge(gate_in, 4)
            act.activation(gb, gb, ACT.Sigmoid).then_inc(gate_ready, 1)

            high_stage("merge", 0, None)
            act.wait_ge(hP_done, DHEADS + HEADS)
            act.dma_start(sgu_in, t["sgu_w_2"][0].rearrange("g a b -> a g b")).then_inc(late_loaded, 16)
            act.dma_start(p_in, t["p_2"][0, 0].rearrange("(h p) d -> p h d", p=P)).then_inc(late_loaded, 16)
            high_parts("out", 3)
            act.wait_ge(x_ready, 1)
            square_half()
            scale_half(1)
            high_stage("ffn", 0, "ffn_norm_w")
            act.wait_ge(rmax_ready, 1)
            for h in range(HALVES):
                e = act.activation(logit[:, h, :], logit[:, h, :], ACT.Exp, bias=rmax[:, h:h + 1],
                                   accum_out=rsum[:, h:h + 1])
            e.then_inc(rexp_done, 1)
            act.wait_ge(logit_done, 1)
            act.wait_ge(xn_act, 1)
            act.wait_ge(xn_dve, 1)
            for h in range(HALVES):
                act.activation(xn_hi[:, h, :], xn[:, h, :], ACT.Copy).then_inc(xn_hi_ready, 1)
            act.wait_ge(pw_done, 2)
            act.activation(wsT, ps[:, 0, :].rearrange("p (g t) -> p g t", g=SG), ACT.Copy).then_inc(pw_raw, 1)
            act.activation(p_f, ps[:, 1, :].rearrange("p (k t) -> p k t", k=2), ACT.Copy).then_inc(pw_raw, 1)
            act.activation(pT[0], ps[:, 1, :].rearrange("p (k t) -> p k t", k=2), ACT.Copy).then_inc(pw_raw, 1)
            for kt in range(1, KT, 2):
                act.wait_ge(gather_done, kt + 1)
                act.activation(xT_all[:, kt, :], ps[:, kt, :], ACT.Copy,
                               scale=vec[:, VEC["ffn_norm_w"] + kt:VEC["ffn_norm_w"] + kt + 1]).then_inc(gather_act, 1)

            act.sem_inc(ye_ready, 1)
            with act.Fori(0, EXPERTS) as e:
                act.wait_ge(scat_done, e + 2)
                act.wait_ge(e_scatter, e + 1)
                act.activation(scat, ps[:, 3, 256:512], ACT.Copy).then_inc(scat_ready, 1)
                act.wait_ge(chunk_used, EXPERT_CHUNKS * e + SLOTS + KT)
                act.wait_ge(hid_ready, e + 1)
                act.activation(hid_g, ps[:, 0, :], ACT.Silu).then_inc(silu_done, 1)
                act.wait_ge(hidT_done, e + 2)
                act.activation(hidT, ps[:, 2, :].rearrange("p (c t) -> p c t", c=4), ACT.Copy).then_inc(hidT_ready, 1)
                act.wait_ge(chunk_used, EXPERT_CHUNKS * e + SLOTS + EXPERT_CHUNKS)
                act.activation(ye, ps[:, 3, 0:DCOL], ACT.Copy).then_inc(ye_ready, 1)

            act.wait_ge(moe_added, EXPERTS + 1)
            square_half()
            act.wait_ge(chunk_used, ALL_EXPERTS)
            high_parts("qk2", 0, 3)
            scale_half(2)
            high_stage("mix", 0, "norm1_g_2")
            high_parts("qk2", 3)
            high_parts("v2", 0, 3)
            evac("qk2", (qk2[:, 0, :], whole))
            act.wait_ge(block_act, evacuated("qk2"))
            act.wait_ge(block_dve, evacuated("qk2"))
            act.activation(sq, qk2.rearrange("p h d -> p (h d)"), ACT.Square).then_inc(sq_ready, 1)
            high_parts("v2", 3)
            high_parts("cuv", 0, 3)
            for j in range(SATT // P):
                act.wait_ge(qkT2_done, j + 1)
                act.activation(qkT2[:, j, :], ps[:, 4 + j, :], ACT.Copy).then_inc(qkT2_evac, 1)
            for i in range(SHEADS + 1):
                if i == 4:
                    act.wait_ge(tile_used, done("cuv"))
                    for h in range(HALVES):
                        src = pset(SETS["cuv"], h)
                        act.activation(u2[:, h, :], src[:, 0:SGU], ACT.Gelu).then_inc(gelu_done, 1)
                        act.activation(cv2[:, h, :], src[:, SGU:2 * SGU], ACT.Gelu).then_inc(gelu_done, 1)
                    act.wait_ge(gelu_done, 4)
                    act.wait_ge(sq_read, 6)
                    act.activation(sq[:, 0:HALVES * SGU], cv2.rearrange("p h d -> p (h d)"), ACT.Square).then_inc(sq_ready, 1)
                if i < SHEADS:
                    z = ps[:, 4 + 2 * (i % 2), 0:SC]
                    act.wait_ge(z_done, i + 1)
                    act.activation(na[i % 2], z, ACT.Abs).then_inc(act_step, 1)
                    act.wait_ge(act_step, 2 * i + 1)
                    act.activation(na[i % 2], na[i % 2], ACT.Exp, scale=-1.0).then_inc(act_step, 1)
                    act.wait_ge(act_step, 2 * i + 2)
                    if i >= 2:
                        act.wait_ge(lr_ready, i - 1)
                    act.activation(spl[i % 2], na[i % 2], ACT.Ln, bias=1.0).then_inc(sp_ready, 1)
                if i == SHEADS:
                    act.wait_ge(tile_used, done("conv"))
                    act.activation(a_hT, ps[:, 2, :].rearrange("p (c t) -> p c t", c=2), ACT.Copy).then_inc(a_act, 1)
                    act.activation(a_bT, ps[:, 0, :].rearrange("p (c t) -> p c t", c=2), ACT.Copy).then_inc(a_act, 1)
                    act.wait_ge(ycT_done, 1)
                    act.activation(yT[0][:, 6:8, :], ps[:, 7, :].rearrange("p (c t) -> p c t", c=2), ACT.Copy).then_inc(ycT_hi, 1)
                if i < 4:
                    high_parts("cuv" if i < 3 else "conv", *((2 * i + 3, min(2 * i + 5, KT)) if i < 3 else (0, 2)))
                else:
                    high_parts("conv", 2 * i - 6, min(2 * i - 4, KT)) if i < 7 else None
                if i >= 1:
                    act.wait_ge(arg_ready, i)
                    act.activation(lb[(i - 1) % 3], lb[(i - 1) % 3], ACT.Exp).then_inc(w_exp, 1)
                if i == 7:
                    high_parts("out2", 0, 3)
            high_parts("out2", 3)
            high_parts("proj")
            high_parts("up0", 0, 1)

            act.wait_ge(x_ready, 3)
            square_half()
            act.wait_ge(tile_used, done("proj"))
            act.activation(pe_sb[:, 0, :], pset(SETS["proj"], 0), ACT.Copy).then_inc(proj_out, 1)
            high_parts("up0", 1, 3)
            scale_half(3)
            high_stage("ff", 0, "norm2_g_2")
            high_parts("up0", 3)
            high_parts("up1", 0, 3)
            for b in range(4):
                act.wait_ge(tile_used, done(f"up{b}"))
                for j in range(4):
                    k = 4 * b + j
                    if k >= 2:
                        act.wait_ge(f_ready, k - 1)
                    act.activation(f_r[k % 2].rearrange("p (c t) -> p c t", c=2),
                                   ps[:, SET[SETS[f"up{b}"]] + j, :].rearrange("p (c t) -> p c t", c=2),
                                   ACT.Relu).then_inc(f_relu, 1)
                    act.wait_ge(f_relu, k + 1)
                    act.activation(fT[0][:, 2 * k:2 * k + 2, :], f_r[k % 2].rearrange("p (c t) -> p c t", c=2),
                                   ACT.Square).then_inc(f_hi, 1)
                    following = f"up{b + 1}" if b < 3 else "down"
                    high_parts(following, 3 + j, 4 + j)
                if b < 3:
                    high_parts(following, 7)
                    high_parts(f"up{b + 2}" if b < 2 else "down", 0, 3)
            high_parts("down", 7)
            high_parts("gate2", 0, 3)

            act.wait_ge(x_ready, 5)
            square_half()
            high_stage("ple", 0, "norm3_g_2")
            high_parts("gate2", 3)
            act.wait_ge(rstd_ready, 5)
            act.wait_ge(tile_used, done("gate2"))
            for h in range(HALVES):
                act.activation(gate2[:, h, :], pset("B", h), ACT.Sigmoid, scale=rstd_x[:, h:h + 1]).then_inc(gate2_ready, 1)

        @block.vector
        def _(dve):
            count = [0]

            def step(ins):
                count[0] += 1
                ins.then_inc(dve_step, 1)
                dve.wait_ge(dve_step, count[0])

            def roots(ss, out, n, dim, ready=None):
                v, a, y = nw[0][:, 0:n], nw[1][:, 0:n], nw[2][:, 0:n]
                step(dve.tensor_scalar(v, ss, 1.0 / dim, EPS, ALU.mult, ALU.add))
                step(dve.tensor_scalar(a.bitcast(I32), v.bitcast(I32), 1, None, ALU.logical_shift_right))
                step(dve.tensor_scalar(y.bitcast(I32), a.bitcast(I32), -1.0, RSQRT_MAGIC, ALU.mult, ALU.add))
                step(dve.tensor_scalar(v, v, -0.5, None, ALU.mult))
                for k in range(3):
                    step(dve.tensor_tensor(a, y, y, ALU.mult))
                    step(dve.tensor_tensor(a, a, v, ALU.mult))
                    last = dve.scalar_tensor_tensor(out if k == 2 else y, a, 1.5, y, ALU.add, ALU.mult)
                    if k < 2 or ready is None:
                        step(last)
                last.then_inc(ready, 1) if ready is not None else None

            def norm(n, scaled=True):
                step(dve.scalar_tensor_tensor(xn[:, 1, :], xs[:, 1, :], 1.0, xs[:, 1, :], ALU.mult, ALU.mult,
                                              accum_out=ss_x[:, 1:2]))
                dve.wait_ge(sq_act, n + 1)
                roots(ss_x, rstd_x, 2, D, rstd_ready)
                dve.wait_ge(rstd_ready, n + 1)
                if scaled:
                    dve.tensor_scalar(xn[:, 1, :], xs[:, 1, :], rstd_x[:, 1:2], None, ALU.mult).then_inc(xn_dve, 1)

            def low_stage(s, base, weight):
                for kt in range(KT):
                    if kt % 2 == 0:
                        dve.wait_ge(hi_ready, KT * STAGES.index(s) + kt + 2)
                    src = ps[:, base + kt // 2, (kt % 2) * T:(kt % 2 + 1) * T]
                    scale = vec[:, VEC[weight] + kt:VEC[weight] + kt + 1] if weight else 1.0
                    dve.scalar_tensor_tensor(hT_lo[:, kt, :], src, scale, hT_hi[:, kt, :].bitcast(F32), ALU.mult,
                                             ALU.subtract).then_inc(lo_ready, 1)

            def evac(name, *parts):
                dve.wait_ge(tile_used, done(name))
                src = pset(SETS[name], 1, COLS[name])
                for dst, cut in parts:
                    if name[0] in "cd":
                        ins = dve.tensor_scalar(dst, cut(src), rstd_0[:, 1:2], None, ALU.mult)
                    else:
                        ins = dve.tensor_copy(dst, cut(src))
                ins.then_inc(block_dve, 1)

            def whole(src):
                return src

            def rows(name):
                n = dict(ROW_VECS)[name]
                return row[:, ROW[name]:ROW[name] + n]

            dve.wait_ge(x_loaded, 16)
            norm(0, scaled=False)
            step(dve.tensor_copy(rstd_0, rstd_x))
            dve.wait_ge(vec_done, 1)
            dve.tensor_copy(vec[:, :], ps[:, 4, 0:NVEC]).then_inc(vec_ready, 1)
            dve.wait_ge(vec_ready, 1)
            low_stage("attn", 0, "attn_norm_w")
            dve.scalar_tensor_tensor(qk_w, vec[:, VEC["diff_q_hnorm_w"]:VEC["diff_q_hnorm_w"] + 1], DQK ** -0.5,
                                     vec[:, VEC["diff_k_hnorm_w"]:VEC["diff_k_hnorm_w"] + 1], ALU.mult, ALU.mult).then_inc(dve_step, 1)
            count[0] += 1

            evac("c", (c_sb[:, 1, :], whole))
            dve.wait_ge(c_sq, 6)
            roots(ss_c, rstd_c, 4, RANK)
            for j in range(2):
                for h in range(HALVES):
                    c = c_sb[:, h, j * RANK:(j + 1) * RANK]
                    dve.tensor_scalar(c, c, rstd_c[:, 2 * j + h:2 * j + h + 1], None, ALU.mult).then_inc(c_norm, 1)

            dve.wait_ge(small_loaded, 16 * N_SMALL)
            for i, (op, c) in enumerate(((ALU.arith_shift_right, 12), (ALU.bitwise_and, 4095))):
                step(dve.tensor_scalar(posi[:, 1 + i, :], posi[:, 0, :], c, None, op))
                step(dve.tensor_scalar(posc[:, :, 1 + i], posc[:, :, 0], c, None, op))
                step(dve.tensor_copy(posb[:, i, :], posi[:, 1 + i, :]))
                step(dve.tensor_copy(posc_f[:, 2 * i:2 * i + 2], posc[:, :, 1 + i]))
            step(dve.tensor_copy(posc_f[:, 4:6], posc[:, :, 0]))
            for h in range(HALVES):
                for i in range(2):
                    step(dve.tensor_scalar(posb[:, 2 + i, :], posb[:, i, :], posc_f[:, 2 * i + h:2 * i + h + 1], None,
                                           ALU.subtract))
                step(dve.scalar_tensor_tensor(posb[:, 2, :], posb[:, 2, :], 4096.0, posb[:, 3, :], ALU.mult, ALU.add))
                step(dve.scalar_tensor_tensor(dist[:, h, :], posb[:, 2, :], -1.0, posb[:, 2, :], ALU.mult, ALU.max))
            ang, turns, sin_a, cos_a, tmp = trig[:, 0, :], trig[:, 1, :], trig[:, 4, :], trig[:, 5, :], trig[:, 2, :]
            for h in range(HALVES):
                step(dve.tensor_scalar(trig[:, 0, h * HR:(h + 1) * HR], freq, posc_f[:, 4 + h:5 + h], None, ALU.mult))
            step(dve.tensor_scalar(turns, ang, 1.0 / (2 * math.pi), ROUND, ALU.mult, ALU.add))
            step(dve.tensor_scalar(turns, turns, -ROUND, None, ALU.add))
            for c in TWO_PI_PARTS:
                step(dve.scalar_tensor_tensor(ang, turns, -c, ang, ALU.mult, ALU.add))
            step(dve.tensor_scalar(sin_a, ang, PI_BELOW, -PI_BELOW, ALU.min, ALU.max))
            step(dve.tensor_scalar(ang, ang, math.pi / 2, None, ALU.add))
            step(dve.tensor_scalar(tmp, ang, math.pi, -2 * math.pi, ALU.is_gt, ALU.mult))
            step(dve.tensor_tensor(ang, ang, tmp, ALU.add))
            dve.tensor_scalar(cos_a, ang, PI_BELOW, -PI_BELOW, ALU.min, ALU.max).then_inc(angle_ready, 1)
            lam_v = rows("diff_lambda").rearrange("p (a b d) -> p a b d", a=2, b=2)
            lam_t = posb[:, 2, 0:2 * DQK].rearrange("p (a d) -> p a d", a=2)
            step(dve.tensor_tensor(lam_t, lam_v[:, :, 0, :], lam_v[:, :, 1, :], ALU.mult))
            dve.tensor_reduce(lam_s, lam_t, AX, ALU.add).then_inc(lam_in, 1)

            step(dve.tensor_tensor(rows("mla_q_hnorm_w")[:, 0:NOPE], rows("mla_q_hnorm_w")[:, 0:NOPE],
                                   rows("mla_k_hnorm_w")[:, 0:NOPE], ALU.mult))

            for j in range(2):
                for kt in range(RT):
                    dve.wait_ge(cT_hi, RT * (j + 1))
                    w = VEC["mla_q_norm_w" if j == 0 else "mla_kv_norm_w"] + kt
                    dve.scalar_tensor_tensor(cT[1][:, j, kt, :], ps[:, 4 + j, kt * T:(kt + 1) * T], vec[:, w:w + 1],
                                             cT[0][:, j, kt, :].bitcast(F32), ALU.mult, ALU.subtract).then_inc(cT_lo, 1)
            evac("dq", (dq[:, 1, :], whole))
            evac("uq0", (q[:, 1, 0:768], whole))
            evac("uq1", (q[:, 1, 768:1536], whole))
            for i in range(2):
                heads = slice(i * HEADS // 2, (i + 1) * HEADS // 2)
                evac(f"ukv{i}", (kf[:, 1, :].rearrange("p (n d) -> p n d", d=QK)[:, heads, 0:NOPE],
                                 lambda src: src.rearrange("p (n d) -> p n d", d=128)[:, :, 0:NOPE]),
                     (v1[:, 1, :].rearrange("p (n d) -> p n d", d=VD)[:, heads, :],
                      lambda src: src.rearrange("p (n d) -> p n d", d=128)[:, :, NOPE:128]))

            def head_sums(n, src, out):
                dve.wait_ge(sq_ready, n + 1)
                dve.tensor_reduce(out, src, AX, ALU.add).then_inc(sq_read, 1)
                dve.wait_ge(sq_read, n + 1)

            def diff_norm(n, buf):
                v = buf.rearrange("p h (n d) -> p (h n) d", d=DQK)
                head_sums(n, sq.rearrange("p (n d) -> p n d", d=DQK), ss_d)
                roots(ss_d, rstd_d, 2 * HEADS, DQK)
                dve.tensor_tensor(v, v, rstd_d.unsqueeze(2).to_broadcast([P, 2 * HEADS, DQK]), ALU.mult).then_inc(dqk_ready, 1)

            def rope(x1, x2, cos, sin, t1, t2):
                step(dve.tensor_tensor(t1, x1, sin, ALU.mult))
                step(dve.tensor_tensor(t2, x2, sin, ALU.mult))
                step(dve.tensor_tensor(x1, x1, cos, ALU.mult))
                step(dve.tensor_tensor(x1, x1, t2, ALU.subtract))
                step(dve.tensor_tensor(x2, x2, cos, ALU.mult))
                step(dve.tensor_tensor(x2, x2, t1, ALU.add))

            diff_norm(0, dq)
            dve.wait_ge(lam_exp, 1)
            step(dve.tensor_scalar(lam, lam_s[:, 0:1], LAM_INIT, lam_s[:, 1:2], ALU.add, ALU.subtract))
            dve.wait_ge(trig_ready, 1)
            sin_t, cos_t = (trig[:, i, :].rearrange("p (h i) -> p h i", h=HALVES) for i in (4, 5))
            step(dve.tensor_tensor(kr, c_sb[:, :, 2 * RANK:C_COLS],
                                   rows("mla_k_hnorm_w")[:, NOPE:QK].unsqueeze(1).to_broadcast([P, HALVES, ROPE]), ALU.mult))
            rt = [trig[:, 0, :].rearrange("p (h i) -> p h i", h=HALVES), trig[:, 1, :].rearrange("p (h i) -> p h i", h=HALVES)]
            rope(kr[:, :, 0:HR], kr[:, :, HR:ROPE], cos_t, sin_t, *rt)
            n_heads = HALVES * HEADS
            ss_q, ss_k, rstd_q, rstd_k = ss_h[:, 0:n_heads], ss_h[:, n_heads:], rstd_h[:, 0:n_heads], rstd_h[:, n_heads:]
            for h in range(HALVES):
                head_sums(1 + h, sq[:, 0:HEADS * QK].rearrange("p (n d) -> p n d", d=QK), ss_q[:, h * HEADS:(h + 1) * HEADS])
            head_sums(3, sq.rearrange("p (n d) -> p n d", d=NOPE), ss_k)
            step(dve.tensor_tensor(ss_k.rearrange("p (h n) -> p h n", h=HALVES), ss_k.rearrange("p (h n) -> p h n", h=HALVES),
                                   ss_kr.unsqueeze(2).to_broadcast([P, HALVES, HEADS]), ALU.add))
            roots(ss_h, rstd_h, 2 * n_heads, QK)
            evac("dk", (dk[:, 1, :], whole))
            diff_norm(4, dk)
            qh = q.rearrange("p h (n d) -> p (h n) d", d=QK)
            step(dve.tensor_tensor(qh, qh, rstd_q.unsqueeze(2).to_broadcast([P, n_heads, QK]), ALU.mult))
            step(dve.tensor_tensor(qh, qh, rows("mla_q_hnorm_w").unsqueeze(1).to_broadcast([P, n_heads, QK]), ALU.mult))
            q4 = q.rearrange("p h (n d) -> p h n d", d=QK)
            full = [P, HALVES, HEADS, HR]
            rope(q4[:, :, :, NOPE:NOPE + HR], q4[:, :, :, NOPE + HR:QK], cos_t.unsqueeze(2).to_broadcast(full),
                 sin_t.unsqueeze(2).to_broadcast(full), *rope_t)
            kh = kf.rearrange("p h (n d) -> p (h n) d", d=QK)
            dve.tensor_tensor(kh[:, :, 0:NOPE], kh[:, :, 0:NOPE], rstd_k.unsqueeze(2).to_broadcast([P, n_heads, NOPE]),
                              ALU.mult).then_inc(qk_ready, 1)
            wide = [P, HALVES, HEADS, ROPE]
            dve.tensor_tensor(kf.rearrange("p h (n d) -> p h n d", d=QK)[:, :, :, NOPE:QK], kr.unsqueeze(2).to_broadcast(wide),
                              rstd_k.rearrange("p (h n) -> p h n", h=HALVES).unsqueeze(3).to_broadcast(wide),
                              ALU.mult).then_inc(qk_ready, 1)
            evac("dv", (dv[:, 1, :], whole))

            def gate_bias(name, g):
                dve.wait_ge(tile_used, done(name))
                for h in range(HALVES):
                    dve.scalar_tensor_tensor(g[:, h, :], pset(SETS[name], h), rstd_0[:, h:h + 1], bgate,
                                             ALU.mult, ALU.add).then_inc(gate_in, 1)

            for i in range(1, DHEADS + 2):
                if i - 1 < DHEADS:
                    u = i - 1
                    s = scores[u % 2]
                    dve.wait_ge(hS_done, u + 1)
                    if u >= 2:
                        dve.wait_ge(hP_done, u - 1)
                    for m in range(2):
                        dve.scalar_tensor_tensor(s[:, 2 * m:2 * m + 2, :].rearrange("p h k -> p (h k)"),
                                                 dist.rearrange("p h k -> p (h k)"), -2.0 ** (-8.0 * (u + 1) / DHEADS),
                                                 ps[:, 5 + m, :], ALU.mult, ALU.add).then_inc(hS_read, 1)
                    dve.wait_ge(hS_read, 2 * u + 2)
                    step(dve.tensor_reduce(mxn[u % 2], s, AX, ALU.max))
                    dve.tensor_scalar(mxn[u % 2], mxn[u % 2], -1.0, None, ALU.mult).then_inc(max_ready, 1)
                if i >= 2:
                    u = i - 2
                    s, r = scores[u % 2], rec[u % 2]
                    dve.wait_ge(exp_done, u + 1)
                    step(dve.reciprocal(r, sums[u % 2]))
                    step(dve.tensor_scalar(r[:, 2:4], r[:, 2:4], lam, None, ALU.mult))
                    for h in range(HALVES):
                        dve.tensor_scalar(s[:, 2 + h, :], s[:, 2 + h, :], r[:, 2 + h:3 + h], None, ALU.mult).then_inc(dve_step, 1)
                        count[0] += 1
                    dve.wait_ge(dve_step, count[0])
                    for h in range(HALVES):
                        dve.scalar_tensor_tensor(s[:, h, :], s[:, h, :], r[:, h:h + 1], s[:, 2 + h, :], ALU.mult,
                                                 ALU.subtract).then_inc(prob_ready, 1)
                if i == DHEADS + 1:
                    gate_bias("gate_a", ga)
            for i in range(1, HEADS + 3):
                if i >= 3:
                    step(dve.reciprocal(rec[(DHEADS + i - 3) % 2][:, 0:2], sums[(DHEADS + i - 3) % 2][:, 0:2]))
                if i - 1 < HEADS:
                    u = DHEADS + i - 1
                    dve.wait_ge(hS_done, u + 1)
                    if i >= 3:
                        dve.wait_ge(exp_done, u - 1)
                    step(dve.tensor_reduce(mxn[u % 2][:, 0:2], ps[:, 5, :].rearrange("p (h k) -> p h k", h=2), AX, ALU.max))
                    dve.tensor_scalar(mxn[u % 2][:, 0:2], mxn[u % 2][:, 0:2], -QK ** -0.5, None, ALU.mult).then_inc(max_ready, 1)
                if 0 <= i - 2 < HEADS:
                    u = DHEADS + i - 2
                    dve.wait_ge(hP_done, u + 1)
                    dve.wait_ge(hO_done, u - 1)
                    dve.tensor_copy(pt_sb[u % 2], ps[:, 6, :].rearrange("p (k t) -> p k t", k=2)).then_inc(hP_evac, 1)
                if 0 <= i - 3 < HEADS:
                    hd = i - 3
                    u = DHEADS + hd
                    r = rec[u % 2]
                    dve.wait_ge(hO_done, u + 1)
                    for h in range(HALVES):
                        g = ga[:, h, hd * VD:(hd + 1) * VD]
                        dve.wait_ge(gate_ready, 1)
                        o = dve.scalar_tensor_tensor(g, ps[:, 7, h * VD:(h + 1) * VD], r[:, h:h + 1], g, ALU.mult, ALU.mult)
                    o.then_inc(hO_evac, 1)
                if i == HEADS + 1:
                    dve.wait_ge(gate_bias_loaded, 16)
                    gate_bias("gate_b", gb)
                if i == 6:
                    dve.wait_ge(od_sums, HALVES)
                    step(dve.tensor_reduce(ss_o, sq.rearrange("p (n d) -> p n d", d=DV), AX, ALU.add))
                    roots(ss_o, rstd_o, 2 * DHEADS, DV, od_root)
            dve.wait_ge(hO_evac, DHEADS + HEADS)
            for h in range(HALVES):
                dve.wait_ge(od_ready, h + 1)
                dve.tensor_tensor(ga[:, h, :], ga[:, h, :], dq[:, h, :], ALU.add).then_inc(merged_ready, 1)
            low_stage("merge", 0, None)

            def add_product(name):
                dve.wait_ge(tile_used, done(name))
                for h in range(HALVES):
                    dve.tensor_tensor(xs[:, h, :], pset(SETS[name], h), xs[:, h, :], ALU.add).then_inc(x_ready, 1)

            add_product("out")
            dve.wait_ge(x_ready, 2)
            norm(1)
            low_stage("ffn", 0, "ffn_norm_w")
            dve.wait_ge(logit_done, 1)
            lp = ps[:, 4, 0:HALVES * EXPERTS].rearrange("p (h e) -> p h e", h=HALVES)
            step(dve.tensor_copy(logit, lp))
            step(dve.tensor_reduce(rmax, logit, AX, ALU.max))
            dve.tensor_scalar(rmax, rmax, -1.0, None, ALU.mult).then_inc(rmax_ready, 1)
            dve.wait_ge(rexp_done, 1)
            step(dve.reciprocal(rinv, rsum))
            for h in range(HALVES):
                dve.tensor_scalar(aff[:, h, :], logit[:, h, :], rinv[:, h:h + 1], None, ALU.mult).then_inc(aff_ready, 1)
            r0, work, sel, eq, cum, zero = (routing[:, i, :] for i in range(6))
            dve.wait_ge(affT_done, 1)
            step(dve.memset(zero, 0.0))
            step(dve.tensor_copy(r0, ps[0:EXPERTS, 5, 0:T]))
            src = r0
            for k in range(CAP // 8):
                step(dve.max(top8[:, k, :], src))
                if k + 1 < CAP // 8:
                    step(dve.match_replace(work, top8[:, k, :], src, -1.0))
                    src = work
            least = top8[:, CAP // 8 - 1, 7:8]
            step(dve.tensor_scalar(sel, r0, least, None, ALU.is_gt, ALU.add, accum_out=rcount[:, 0:1]))
            step(dve.tensor_scalar(rcount[:, 1:2], rcount[:, 0:1], -1.0, float(CAP), ALU.mult, ALU.add))
            step(dve.tensor_scalar(eq, r0, least, None, ALU.is_equal))
            step(dve.tensor_tensor_scan(cum, eq, zero, 0.0, ALU.add, ALU.add))
            step(dve.scalar_tensor_tensor(eq, cum, rcount[:, 1:2], eq, ALU.is_le, ALU.mult))
            step(dve.tensor_tensor(sel, sel, eq, ALU.add))
            step(dve.tensor_tensor_scan(cum, sel, zero, 0.0, ALU.add, ALU.add))
            step(dve.tensor_tensor(cum, cum, sel, ALU.mult))
            dve.tensor_scalar(cum, cum, -1.0, None, ALU.add).then_inc(slot_done, 1)
            dve.wait_ge(slotT_done, 1)
            step(dve.tensor_copy(slot_t, ps[:, 6, 0:HALVES * EXPERTS].rearrange("p (h e) -> p h e", h=HALVES)))
            grid = [P, EXPERTS, CAP]
            for h in range(HALVES):
                dve.tensor_tensor(onehot[:, h, :].rearrange("p (e s) -> p e s", e=EXPERTS),
                                  slot_t[:, h, :].unsqueeze(2).to_broadcast(grid),
                                  slot_ids[:, 0:CAP].unsqueeze(1).to_broadcast(grid), ALU.is_equal).then_inc(onehot_ready, 1)
            for kt in range(0, KT, 2):
                dve.wait_ge(gather_done, kt + 1)
                dve.tensor_scalar(xT_all[:, kt, :], ps[:, kt, :], vec[:, VEC["ffn_norm_w"] + kt:VEC["ffn_norm_w"] + kt + 1],
                                  None, ALU.mult).then_inc(gather_dve, 1)
            dve.wait_ge(gather_dve, KT // 2)
            dve.wait_ge(gather_act, KT // 2)

            dve.sem_inc(hid_ready, 1)
            dve.sem_inc(moe_added, 1)
            with dve.Fori(0, EXPERTS) as e:
                dve.tensor_copy(xe, xT_all[:, :, bass.ds(e * CAP, CAP)]).then_inc(xe_ready, 1)
                dve.wait_ge(scat_done, e + 1)
                for h in range(HALVES):
                    dve.tensor_scalar(gated[:, h, :], slot_ids[:, :], slot_t[:, h, bass.ds(e, 1)], aff[:, h, bass.ds(e, 1)],
                                      ALU.is_equal, ALU.mult).then_inc(gated_ready, 1)
                dve.wait_ge(silu_done, e + 1)
                dve.wait_ge(chunk_used, EXPERT_CHUNKS * e + SLOTS + 2 * KT)
                dve.wait_ge(hidT_done, e + 1)
                dve.tensor_tensor(hid, hid_g, ps[:, 1, :], ALU.mult).then_inc(hid_ready, 1)
                dve.wait_ge(e_scatter, e + 2)
                for j in range(4):
                    xv = xs[:, :, j * DCOL:(j + 1) * DCOL]
                    a = dve.tensor_tensor(xv, ps[:, 4 + j, :].rearrange("p (h d) -> p h d", h=HALVES), xv, ALU.add)
                a.then_inc(moe_added, 1)

            dve.wait_ge(moe_added, EXPERTS + 1)
            norm(2)
            low_stage("mix", 0, "norm1_g_2")
            step(dve.scalar_tensor_tensor(rows("q_norm_g_2"), rows("q_norm_g_2"), SHD ** -0.5, rows("k_norm_g_2"), ALU.mult, ALU.mult))
            step(dve.memset(conv[:, :, 0:CONVW - 1], 0.0))
            evac("qk2", (qk2[:, 1, :], whole))
            head_sums(5, sq.rearrange("p (n d) -> p n d", d=SHD), ss_d)
            roots(ss_d, rstd_d, 4 * SHEADS, SHD)
            v = qk2.rearrange("p h (n d) -> p (h n) d", d=SHD)
            step(dve.tensor_tensor(v, v, rstd_d.unsqueeze(2).to_broadcast([P, 4 * SHEADS, SHD]), ALU.mult))
            v = qk2.rearrange("p h (n d) -> p h n d", d=SHD)[:, :, 0:SHEADS, :]
            w = rows("q_norm_g_2").unsqueeze(1).unsqueeze(1).to_broadcast([P, HALVES, SHEADS, SHD])
            dve.tensor_tensor(v, v, w, ALU.mult).then_inc(qk2_ready, 1)
            dve.wait_ge(tile_used, done("v2"))
            for h in range(HALVES):
                dve.tensor_copy(v2[:, h, :], pset(SETS["v2"], h, SATT)).then_inc(v_ready, 1)

            def gating_norm():
                head_sums(6, sq[:, 0:HALVES * SGU].rearrange("p (n d) -> p n d", d=SGU // SG), ss_d[:, 0:2 * SG])
                roots(ss_d[:, 0:2 * SG], rstd_d[:, 0:2 * SG], 2 * SG, SGU // SG)
                v = cv2.rearrange("p h (n d) -> p (h n) d", d=SGU // SG)
                step(dve.tensor_tensor(v, v, rstd_d[:, 0:2 * SG].unsqueeze(2).to_broadcast([P, 2 * SG, SGU // SG]), ALU.mult))
                dve.tensor_tensor(cv2, cv2, rows("sgu_norm_g_2").unsqueeze(1).to_broadcast([P, HALVES, SGU]),
                                  ALU.mult).then_inc(cv_ready, 1)

            def gated_unit():
                dve.wait_ge(sv_done, 1)
                for g in range(SG):
                    w = SGU // SG
                    s = ps[:, 7, :].rearrange("p (h d) -> p h d", h=HALVES)[:, :, g * w:(g + 1) * w]
                    b = vec[:, VEC["sgu_b_2"] + g:VEC["sgu_b_2"] + g + 1]
                    dve.scalar_tensor_tensor(yc[:, :, g * w:(g + 1) * w], s, b, u2[:, :, g * w:(g + 1) * w], ALU.add,
                                             ALU.mult).then_inc(yc_ready, 1)

            def split_y(src, k, n):
                step(dve.tensor_copy(yT[0][:, k:k + n, :], src))
                dve.tensor_tensor(yT[1][:, k:k + n, :], src, yT[0][:, k:k + n, :].bitcast(F32), ALU.subtract).then_inc(y_ready, n)

            def diagonal(buf):
                return buf.rearrange("p (c t) -> p c t", t=P)[:, 0:3:2, :]

            for i in range(SHEADS + 2):
                if i < SHEADS:
                    z = ps[:, 4 + 2 * (i % 2), 0:SC]
                    dve.wait_ge(sp_ready, i + 1)
                    if i >= 3:
                        dve.wait_ge(yb_done, i - 2)
                    step(dve.scalar_tensor_tensor(lb[i % 3], z, 0.0, spl[i % 2], ALU.min, ALU.subtract))
                    if i >= 2:
                        dve.wait_ge(suf_done, i - 1)
                    step(dve.tensor_tensor(lr[i % 2], lb[i % 3], z, ALU.subtract))
                    dve.tensor_tensor(diagonal(lr[i % 2]), diagonal(lr[i % 2]), tri[:, :].unsqueeze(1).to_broadcast([P, 2, P]),
                                      ALU.mult).then_inc(lr_ready, 1)
                if 0 <= i - 1 < SHEADS:
                    u = i - 1
                    dve.wait_ge(suf_done, u + 1)
                    dve.tensor_tensor(lb[u % 3], ps[:, 5, 0:SC], lb[u % 3], ALU.add).then_inc(arg_ready, 1)
                if i == 5:
                    gating_norm()
                if i == 6:
                    gated_unit()
                if i == SHEADS:
                    dve.wait_ge(ycT_hi, 1)
                    dve.tensor_tensor(yT[1][:, 6:8, :], ps[:, 7, :].rearrange("p (c t) -> p c t", c=2),
                                      yT[0][:, 6:8, :].bitcast(F32), ALU.subtract).then_inc(y_ready, 2)
                if 0 <= i - 2 < SHEADS:
                    u = i - 2
                    dve.wait_ge(w_exp, u + 1)
                    dve.tensor_tensor(diagonal(lb[u % 3]), diagonal(lb[u % 3]), tri[:, :].unsqueeze(1).to_broadcast([P, 2, P]),
                                      ALU.mult).then_inc(w_ready, 1)
                    if u == SHEADS - 1:
                        dve.wait_ge(tile_used, done("conv"))
                        dve.wait_ge(a_act, 1)
                        step(dve.tensor_tensor(conv[:, :, CONVW - 1:], ps[:, 1, :].rearrange("p (c t) -> p c t", c=2), a_hT, ALU.mult))
                        dve.wait_ge(a_act, 2)
                        for ct in range(2):
                            w = [vec[:, VEC["conv_w_2"] + 2 * j + ct:VEC["conv_w_2"] + 2 * j + ct + 1] for j in range(CONVW)]
                            step(dve.tensor_scalar(conv_y, conv[:, ct, 0:T], w[0], None, ALU.mult))
                            for j in range(1, CONVW):
                                step(dve.scalar_tensor_tensor(conv_y, conv[:, ct, j:j + T], w[j], conv_y, ALU.mult, ALU.add))
                            step(dve.tensor_tensor(conv_y, conv_y, a_bT[:, ct, :], ALU.mult))
                            split_y(conv_y.unsqueeze(1), ct, 1)
                            dve.wait_ge(y_ready, 6 + ct)
                    if u % 2:
                        pair = u // 2
                        dve.wait_ge(yb_done, u + 1)
                        split_y(ps[:, 3, 0:T].unsqueeze(1), 2 + pair, 1)
            add_product("out2")
            dve.wait_ge(x_ready, 4)
            norm(3)
            low_stage("ff", 0, "norm2_g_2")
            dve.wait_ge(tile_used, done("proj"))
            dve.tensor_copy(pe_sb[:, 1, :], pset(SETS["proj"], 1)).then_inc(proj_out, 1)
            for k in range(4 * 4):
                dve.wait_ge(f_relu, k + 1)
                step(dve.tensor_tensor(f_2, f_r[k % 2], f_r[k % 2], ALU.mult))
                dve.wait_ge(f_hi, k + 1)
                lo = fT[1][:, 2 * k:2 * k + 2, :]
                dve.tensor_tensor(lo, f_2.rearrange("p (c t) -> p c t", c=2), fT[0][:, 2 * k:2 * k + 2, :].bitcast(F32),
                                  ALU.subtract).then_inc(f_ready, 1)
                dve.wait_ge(f_ready, k + 1)
            add_product("down")
            dve.wait_ge(x_ready, 6)
            norm(4, scaled=False)
            low_stage("ple", 0, "norm3_g_2")
            dve.wait_ge(proj_out, 2)
            for h in range(HALVES):
                dve.wait_ge(gate2_ready, h + 1)
                step(dve.tensor_tensor(gate2[:, h, :], pe_sb[:, h, :], gate2[:, h, :], ALU.mult))
                dve.tensor_tensor(gate2[:, h, :], xs[:, h, :], gate2[:, h, :], ALU.add).then_inc(out_ready, 1)

        @block.tensor
        def _(pe):
            def transposes(s, src, base):
                for b in range(4):
                    for kt in (2 * b, 2 * b + 1):
                        for h in range(HALVES):
                            m = pe.transpose(ps[:, base + b, (kt % 2) * T + h * P:(kt % 2) * T + (h + 1) * P],
                                             src[:, h, kt * P:(kt + 1) * P], ident[:, :])
                    m.then_inc(tr_done, 1)

            def stage_ready(s, kt=KT - 1):
                pe.wait_ge(lo_ready, KT * STAGES.index(s) + kt + 1)

            def tiles(name, left, kts=None, c0s=None, ready=None, order=None):
                cols = COLS[name]
                order = order or list(range(TILES[name]))
                all_c0 = list(range(0, cols, 512))
                c0s = all_c0 if c0s is None else c0s
                for i in kts if kts is not None else range(TILES[name]):
                    n, kt = TILE0[name] + i, order[i]
                    w = w_split[:, n % WBUFS]
                    first, last = i == 0, i == TILES[name] - 1
                    if ready is not None:
                        ready(kt)
                    pe.wait_ge(split_hi, n + 1)
                    for part in (0, 1):
                        for h in range(HALVES):
                            for c0 in c0s:
                                c = slice(c0, min(c0 + 512, cols))
                                pe.matmul(pset(SETS[name], h)[:, c], left[part][:, kt, h * P:(h + 1) * P], w[:, 0, c],
                                          start=first and part == 0, stop=False)
                    pe.wait_ge(split_lo, n + 1)
                    for h in range(HALVES):
                        for c0 in c0s:
                            c = slice(c0, min(c0 + 512, cols))
                            m = pe.matmul(pset(SETS[name], h)[:, c], left[0][:, kt, h * P:(h + 1) * P], w[:, 1, c],
                                          start=False, stop=last)
                    if c0s[-1] == all_c0[-1]:
                        m.then_inc(tile_used, 1)

            def tiles_T(name, kts=None, ready=None):
                for kt in kts if kts is not None else range(TILES[name]):
                    n = TILE0[name] + kt
                    w = w_split[:, n % WBUFS]
                    first, last = kt == 0, kt == TILES[name] - 1
                    if ready is not None:
                        ready(kt)

                    def pass_T(ct, part_w, left, start, stop):
                        return pe.matmul(ps[:, SET[SETS[name]] + ct // 2, (ct % 2) * T:(ct % 2 + 1) * T],
                                         w[:, part_w, ct * P:(ct + 1) * P], left[:, kt, :], start=start, stop=stop,
                                         skip_group_check=True)

                    pe.wait_ge(split_hi, n + 1)
                    for ct in range(COLS[name] // P):
                        pass_T(ct, 0, hT_hi, first and ct % 2 == 0, False)
                        pass_T(ct, 0, hT_lo, False, False)
                    pe.wait_ge(split_lo, n + 1)
                    for ct in range(COLS[name] // P):
                        m = pass_T(ct, 1, hT_hi, False, last)
                    m.then_inc(tile_used, 1)

            hT = (hT_hi, hT_lo)

            def out_of_psum(name):
                pe.wait_ge(block_act, evacuated(name))
                pe.wait_ge(block_dve, evacuated(name))

            pe.wait_ge(masks_ready, 1)
            pe.wait_ge(x_loaded, 16)
            transposes("attn", xs, 0)
            pe.wait_ge(vec_loaded, 16 * N_VEC)
            pe.transpose(ps[:, 4, 0:NVEC], vec_rows[:, :], ident[0:NVEC, 0:NVEC]).then_inc(vec_done, 1)

            pe.wait_ge(vec_ready, 1)
            tiles("c", hT, ready=lambda kt: stage_ready("attn", kt))
            tiles("dq", hT, range(0, 6))
            pe.wait_ge(c_norm, 4)
            out_of_psum("c")
            for j in range(2):
                for kt in range(RT):
                    for h in range(HALVES):
                        c0 = j * RANK + kt * P
                        m = pe.transpose(ps[:, 4 + j, kt * T + h * P:kt * T + (h + 1) * P], c_sb[:, h, c0:c0 + P], ident[:, :])
                m.then_inc(cT_done, 1)
            tiles("dq", hT, range(6, KT))
            pe.wait_ge(cT_lo, 2 * RT)
            tiles("uq0", [c[:, 0] for c in cT])
            out_of_psum("dq")
            tiles("uq1", [c[:, 0] for c in cT])
            out_of_psum("uq0")
            tiles("ukv0", [c[:, 1] for c in cT])
            out_of_psum("uq1")
            tiles("ukv1", [c[:, 1] for c in cT])
            out_of_psum("ukv0")
            tiles("dk", hT)
            out_of_psum("ukv1")
            tiles("dv", hT)

            pe.wait_ge(dqk_ready, 2)
            out_of_psum("dk")
            for i in range(DHEADS + 4):
                if 0 <= i - 1 < DHEADS:
                    u = i - 1
                    pe.wait_ge(hT_evac, u + 1)
                    if u >= 1:
                        pe.wait_ge(hS_read, 2 * u)
                    for h in range(HALVES):
                        for mp in range(2):
                            r = slice(DQK * mp, DQK * (mp + 1))
                            m = pe.matmul(ps[:, 5 + mp, h * T:(h + 1) * T], qkT[u % 2][r, h * P:(h + 1) * P],
                                          qkT[u % 2][r, T:2 * T], start=True, stop=True)
                    m.then_inc(hS_done, 1)
                if i < DHEADS:
                    if i >= 1:
                        pe.wait_ge(hT_evac, i)
                    if i >= 5:
                        pe.wait_ge(hO_evac, i - 4)
                    for j, buf in enumerate((dq, dk)):
                        for h in range(HALVES):
                            m = pe.transpose(ps[:, 4, j * T + h * P:j * T + (h + 1) * P], buf[:, h, i * P:(i + 1) * P], ident[:, :])
                    m.then_inc(hT_done, 1)
                if i < KT:
                    if i == 0:
                        out_of_psum("dv")
                    tiles("gate_a", hT, [i])
                if i >= DHEADS + 2:
                    pe.wait_ge(gate_in, 2)
                    tiles("gate_b", hT, [(i - DHEADS - 2) // 2], [512 * (i % 2)])
                if 0 <= i - 3 < DHEADS:
                    u = i - 3
                    pe.wait_ge(prob_ready, 2 * u + 2)
                    if u >= 1:
                        pe.wait_ge(hP_evac, u)
                    for kb in range(2):
                        for h in range(HALVES):
                            m = pe.transpose(ps[:, 7, kb * T + h * P:kb * T + (h + 1) * P], scores[u % 2][:, h, kb * P:(kb + 1) * P], ident[:, :])
                    m.then_inc(hP_done, 1)
                if 0 <= i - 4 < DHEADS:
                    u = i - 4
                    pe.wait_ge(hP_evac, u + 1)
                    pe.wait_ge(hT_evac, min(i + 1, DHEADS))
                    if u >= 1:
                        pe.wait_ge(hO_evac, u)
                    for h in range(HALVES):
                        for kb in range(2):
                            m = pe.matmul(ps[:, 4, h * P:(h + 1) * P], pt_sb[u % 2][:, kb, h * P:(h + 1) * P],
                                          dv[:, kb, u * DV:(u + 1) * DV], start=kb == 0, stop=kb == 1)
                    m.then_inc(hO_done, 1)
            pe.wait_ge(qk_ready, 2)
            pe.wait_ge(hO_evac, DHEADS)
            for i in range(HEADS + 3):
                if i < HEADS:
                    u = DHEADS + i
                    pe.wait_ge(hT_evac, u)
                    for j, buf in enumerate((q, kf)):
                        for h in range(HALVES):
                            m = pe.transpose(ps[0:QK, 4, j * T + h * P:j * T + (h + 1) * P], buf[:, h, i * QK:(i + 1) * QK], ident[:, :])
                    m.then_inc(hT_done, 1)
                if 0 <= i - 1 < HEADS:
                    u = DHEADS + i - 1
                    pe.wait_ge(hT_evac, u + 1)
                    pe.wait_ge(exp_done, u)
                    for h in range(HALVES):
                        m = pe.matmul(ps[:, 5, h * T:(h + 1) * T], qkT[u % 2][0:QK, h * P:(h + 1) * P],
                                      qkT[u % 2][0:QK, T:2 * T], start=True, stop=True)
                    m.then_inc(hS_done, 1)
                if i + 2 < 2 * KT:
                    tiles("gate_b", hT, [(i + 2) // 2], [512 * (i % 2)])
                if 0 <= i - 2 < HEADS:
                    u = DHEADS + i - 2
                    pe.wait_ge(exp_done, u + 1)
                    pe.wait_ge(hP_evac, u)
                    for kb in range(2):
                        for h in range(HALVES):
                            m = pe.transpose(ps[:, 6, kb * T + h * P:kb * T + (h + 1) * P], scores[u % 2][:, h, kb * P:(kb + 1) * P], ident[:, :])
                    m.then_inc(hP_done, 1)
                if 0 <= i - 3 < HEADS:
                    hd = i - 3
                    u = DHEADS + hd
                    pe.wait_ge(hP_evac, u + 1)
                    pe.wait_ge(hO_evac, u)
                    for h in range(HALVES):
                        for kb in range(2):
                            m = pe.matmul(ps[:, 7, h * VD:(h + 1) * VD], pt_sb[u % 2][:, kb, h * P:(h + 1) * P],
                                          v1[:, kb, hd * VD:(hd + 1) * VD], start=kb == 0, stop=kb == 1)
                    m.then_inc(hO_done, 1)

            pe.wait_ge(merged_ready, 2)
            pe.wait_ge(gate_in, 4)
            transposes("merge", ga, 0)
            tiles("out", hT, ready=lambda kt: stage_ready("merge", kt))
            pe.wait_ge(tile_used, done("out"))
            pe.sem_inc(chunk_used, SLOTS)
            pe.wait_ge(xn_act, 1)
            pe.wait_ge(xn_dve, 1)
            transposes("ffn", xn, 0)
            stage_ready("ffn")
            pe.wait_ge(x_ready, 2)
            for h in range(HALVES):
                for kt in range(KT):
                    for part in (0, 1):
                        m = pe.matmul(ps[:, 4, h * EXPERTS:(h + 1) * EXPERTS], hT[part][:, kt, h * P:(h + 1) * P].bitcast(F32),
                                      router[:, kt, :], start=kt == 0 and part == 0, stop=kt == KT - 1 and part == 1)
            m.then_inc(logit_done, 1)
            pe.wait_ge(late_loaded, 32)
            for g in range(SG):
                m = pe.transpose(ps[:, 0, g * P:(g + 1) * P], sgu_in[:, g, :], ident[:, :])
            m.then_inc(pw_done, 1)
            for kt in range(PLE // P):
                for h in range(HALVES):
                    m = pe.transpose(ps[:, 1, kt * T + h * P:kt * T + (h + 1) * P], p_in[:, h, kt * P:(kt + 1) * P], ident[:, :])
            m.then_inc(pw_done, 1)
            pe.wait_ge(aff_ready, 2)
            for h in range(HALVES):
                m = pe.transpose(ps[0:EXPERTS, 5, h * P:(h + 1) * P], aff[:, h, :], ident[:, :])
            m.then_inc(affT_done, 1)
            pe.wait_ge(slot_done, 1)
            for h in range(HALVES):
                m = pe.transpose(ps[:, 6, h * EXPERTS:(h + 1) * EXPERTS], routing[:, 4, h * P:(h + 1) * P], ident[0:EXPERTS, 0:EXPERTS])
            m.then_inc(slotT_done, 1)
            pe.wait_ge(onehot_ready, 2)
            pe.wait_ge(xn_lo_ready, HALVES)
            pe.wait_ge(pw_raw, 3)
            for kt in range(KT):
                for h in range(HALVES):
                    for part, src in enumerate((xn_hi, xn_lo)):
                        m = pe.matmul(ps[:, kt, :], src[:, h, kt * P:(kt + 1) * P], onehot[:, h, :],
                                      start=h == 0 and part == 0, stop=h == HALVES - 1 and part == 1)
                m.then_inc(gather_done, 1)
            pe.wait_ge(gather_act, KT // 2)
            pe.wait_ge(gather_dve, KT // 2)

            for s in (scat_done, hidT_done, e_scatter):
                pe.sem_inc(s, 1)
            with pe.Fori(0, EXPERTS) as e:
                def chunk_wait(k):
                    pe.wait_ge(slot_loaded[k % SLOTS], 16 * (EXPERT_CHUNKS // SLOTS) * e + expert_landed(k))

                pe.wait_ge(gated_ready, 2 * e + 2)
                pe.wait_ge(ye_ready, e + 1)
                for h in range(HALVES):
                    m = pe.transpose(ps[:, 3, 256 + h * P:256 + (h + 1) * P], gated[:, h, :], ident[:, :])
                m.then_inc(scat_done, 1)
                pe.wait_ge(xe_ready, e + 1)
                pe.wait_ge(hid_ready, e + 1)
                for bank in range(2):
                    for kt in range(KT):
                        chunk_wait(bank * KT + kt)
                        w = ring[:, (bank * KT + kt) % SLOTS, :]
                        for j in range(4):
                            m = pe.matmul(ps[j * CAP:(j + 1) * CAP, bank, :], xe[:, kt, :], w[:, j * FCOL:(j + 1) * FCOL],
                                          start=kt == 0, stop=kt == KT - 1, skip_group_check=True)
                        m.then_inc(chunk_used, 1)
                pe.wait_ge(hid_ready, e + 2)
                for c in range(4):
                    m = pe.transpose(ps[:, 2, c * P:(c + 1) * P], hid[:, c * P:(c + 1) * P], ident[:, :])
                m.then_inc(hidT_done, 1)
                pe.wait_ge(scat_ready, e + 1)
                pe.wait_ge(hidT_ready, e + 1)
                for c in range(KT):
                    chunk_wait(2 * KT + c)
                    w = slot_view((2 * KT + c) % SLOTS, D)
                    for k in range(2):
                        ft = 2 * c + k
                        for j in range(4):
                            m = pe.matmul(ps[j * CAP:(j + 1) * CAP, 3, 0:DCOL], hidT[:, ft % 4, (ft // 4) * CAP:(ft // 4 + 1) * CAP],
                                          w[:, k, j * DCOL:(j + 1) * DCOL], start=ft == 0, stop=ft == FF // P - 1, skip_group_check=True)
                    m.then_inc(chunk_used, 1)
                pe.wait_ge(ye_ready, e + 2)
                pe.wait_ge(moe_added, e + 1)
                for h in range(HALVES):
                    for j in range(4):
                        m = pe.matmul(ps[:, 4 + j, h * DCOL:(h + 1) * DCOL], scat[j * CAP:(j + 1) * CAP, h * P:(h + 1) * P],
                                      ye[j * CAP:(j + 1) * CAP, :], start=True, stop=True)
                m.then_inc(e_scatter, 1)

            pe.wait_ge(xn_act, 2)
            pe.wait_ge(xn_dve, 2)
            transposes("mix", xn, 0)
            pe.wait_ge(moe_added, EXPERTS + 1)
            tiles("qk2", hT, ready=lambda kt: stage_ready("mix", kt))
            stage_ready("mix")
            tiles("v2", hT)
            pe.wait_ge(qk2_ready, 1)
            out_of_psum("qk2")
            for j in range(SATT // P):
                for i in range(2):
                    for h in range(HALVES):
                        m = pe.transpose(ps[:, 4 + j, i * T + h * P:i * T + (h + 1) * P],
                                         qk2[:, h, i * SATT + j * P:i * SATT + (j + 1) * P], ident[:, :])
                m.then_inc(qkT2_done, 1)
            pe.wait_ge(v_ready, 2)
            for i in range(SHEADS + 2):
                if i < SHEADS:
                    r = slice(SHD * (i % 2), SHD * (i % 2 + 1))
                    if i == 0:
                        pe.wait_ge(qkT2_evac, SATT // P)
                    if i >= 2:
                        pe.wait_ge(lr_ready, i - 1)
                    z = ps[:, 4 + 2 * (i % 2), :]
                    pe.matmul(z[:, 0:T], qkT2[r, i // 2, T:T + P], qkT2[r, i // 2, 0:T], start=True, stop=True)
                    pe.matmul(z[:, T:SC], qkT2[r, i // 2, T + P:2 * T], qkT2[r, i // 2, P:T], start=True,
                              stop=True).then_inc(z_done, 1)
                if 0 <= i - 1 < SHEADS:
                    u = i - 1
                    pe.wait_ge(lr_ready, u + 1)
                    if u >= 1:
                        pe.wait_ge(arg_ready, u)
                    pe.matmul(ps[:, 5, 0:SC], later[:, :], lr[u % 2], start=True, stop=False)
                    pe.matmul(ps[:, 5, P:T], ones[:, :], lr[u % 2][:, T:SC], start=False, stop=True).then_inc(suf_done, 1)
                if i == 6:
                    pe.wait_ge(cv_ready, 1)
                    for h in range(HALVES):
                        for g in range(SG):
                            w = SGU // SG
                            m = pe.matmul(ps[:, 7, h * SGU + g * w:h * SGU + (g + 1) * w], wsT[:, g, :], cv2[:, h, g * w:(g + 1) * w],
                                          start=True, stop=True)
                    m.then_inc(sv_done, 1)
                if i == SHEADS:
                    pe.wait_ge(yc_ready, SG)
                    for kt in range(SGU // P):
                        for h in range(HALVES):
                            m = pe.transpose(ps[:, 7, kt * T + h * P:kt * T + (h + 1) * P], yc[:, h, kt * P:(kt + 1) * P], ident[:, :])
                    m.then_inc(ycT_done, 1)
                if i < 4:
                    tiles("cuv", hT, [2 * i, 2 * i + 1])
                elif i < 8:
                    if i == 4:
                        pe.wait_ge(gelu_done, 4)
                    tiles_T("conv", [2 * i - 8, 2 * i - 7])
                if 0 <= i - 2 < SHEADS:
                    u = i - 2
                    r = slice(SHD * (u % 2), SHD * (u % 2 + 1))
                    pe.wait_ge(w_ready, u + 1)
                    if u >= 2:
                        pe.wait_ge(y_ready, u // 2)
                    pe.matmul(ps[r, 3, 0:T], v2[:, 0, u * SHD:(u + 1) * SHD], lb[u % 3][:, 0:T], start=True, stop=False,
                              skip_group_check=True)
                    pe.matmul(ps[r, 3, P:T], v2[:, 1, u * SHD:(u + 1) * SHD], lb[u % 3][:, T:SC], start=False, stop=True,
                              skip_group_check=True).then_inc(yb_done, 1)
            pe.wait_ge(y_ready, KT)
            tiles("out2", yT, order=[6, 7, 0, 1, 2, 3, 4, 5])
            pe.wait_ge(pw_ready, 1)
            tiles("proj", pT)
            pe.wait_ge(xn_act, 3)
            pe.wait_ge(xn_dve, 3)
            transposes("ff", xn, 0)
            pe.wait_ge(proj_out, 2)
            for b in range(4):
                if b == 1:
                    stage_ready("ff")
                if b >= 2:
                    pe.wait_ge(f_relu, 4 * (b - 1))
                tiles_T(f"up{b}", ready=(lambda kt: stage_ready("ff", kt)) if b == 0 else None)
            pe.wait_ge(f_relu, 12)
            tiles("down", fT, ready=lambda kt: pe.wait_ge(f_ready, kt // 2 + 1))
            pe.wait_ge(x_ready, 6)
            transposes("ple", xs, 0)
            tiles("gate2", hT, ready=lambda kt: stage_ready("ple", kt))


INPUTS = ["x", "positions", "attn_norm_w", "w_in", "b_gate", "mla_q_norm_w", "mla_w_uq", "mla_kv_norm_w", "mla_w_ukv",
          "mla_q_hnorm_w", "mla_k_hnorm_w", "diff_q_hnorm_w", "diff_k_hnorm_w", "diff_lambda", "diff_subln_w", "w_out",
          "ffn_norm_w", "router_w", "expert_w_gate", "expert_w_up", "expert_w_down", "p_2", "norm1_g_2", "w_in_2",
          "conv_w_2", "q_norm_g_2", "k_norm_g_2", "sgu_norm_g_2", "sgu_w_2", "sgu_b_2", "w_out_2", "norm2_g_2",
          "w_ff1_2", "w_ff2_2", "norm3_g_2", "w_ple_gate_2", "w_ple_proj_2"]


def kernel(**inputs):
    import numpy as np
    import concourse.bacc as bacc
    from concourse.bass_utils import run_bass_kernel_spmd

    nc = bacc.Bacc("TRN2", target_bir_lowering=False, num_devices=1)
    arrays, t = {}, {}
    for name in INPUTS:
        a = np.ascontiguousarray(inputs[name])
        arrays[f"in_{name}"] = a
        t[name] = nc.dram_tensor(f"in_{name}", a.shape, mybir.dt.from_np(a.dtype), kind="ExternalInput").ap()
    t["out"] = nc.dram_tensor("out_x", (1, T, D), F32, kind="ExternalOutput").ap()
    hybrid_blocks(nc, t)
    result = run_bass_kernel_spmd(nc, [arrays], core_ids=[0])
    return result.results[0]["out_x"]
```

```python
from contextlib import ExitStack
import math

import concourse.bass as bass
import concourse.mybir as mybir

F32 = mybir.dt.float32
F32R = mybir.dt.float32r
I32 = mybir.dt.int32
ALU = mybir.AluOpType
ACT = mybir.ActivationFunctionType
AX = mybir.AxisListType.X

P = 128
T = 256
HALVES = T // P
D = 1024
KT = D // P
EPS = 1e-6

HEADS, QK, NOPE, ROPE, VD = 16, 96, 64, 32, 64
HR = ROPE // 2
RANK = 256
RT = RANK // P
C_COLS = 2 * RANK + ROPE
THETA = 10000.0
DHEADS, DQK, DV = 8, 64, 128
LAM_INIT = 0.8 - 0.6 * math.exp(-0.3 * 0)

EXPERTS, CAP, FF = 16, 32, 2048
FCOL = FF // 4
DCOL = D // 4

CONV, CONVW = 256, 3
SHEADS, SHD = 8, 64
SATT = SHEADS * SHD
SGU, SG = 256, 4
DFF = 4096
PLE = 256

SLOTS, SLOT = 16, 2048
OWN_SLOTS = 8
EXPERT_CHUNKS = 3 * KT
PAIR = 2
assert PAIR * EXPERT_CHUNKS % SLOTS == 0
DENSE_SLOTS = 5
WBUFS = OWN_SLOTS - DENSE_SLOTS
SBUF_BASE = 16512

VEC_ROWS = [("attn_norm_w", 8), ("mla_q_norm_w", 2), ("mla_kv_norm_w", 2), ("ffn_norm_w", 8), ("norm1_g_2", 8),
            ("norm2_g_2", 8), ("norm3_g_2", 8), ("conv_w_2", 6), ("sgu_b_2", 4), ("diff_q_hnorm_w", 1),
            ("diff_k_hnorm_w", 1)]
VEC = {}
for _name, _rows in VEC_ROWS:
    VEC[_name] = sum(r for _, r in VEC_ROWS[:len(VEC)])
NVEC = sum(r for _, r in VEC_ROWS)

ROW_VECS = [("mla_q_hnorm_w", QK), ("mla_k_hnorm_w", QK),
            ("diff_subln_w", DV), ("q_norm_g_2", SHD), ("k_norm_g_2", SHD), ("sgu_norm_g_2", SGU),
            ("diff_lambda", 4 * DQK)]
ROW = {}
for _name, _n in ROW_VECS:
    ROW[_name] = sum(n for _, n in ROW_VECS[:len(ROW)])
NROW = sum(n for _, n in ROW_VECS)

INV_FREQ = [1.0 / THETA ** (2 * i / ROPE) for i in range(HR)]
TWO_PI_PARTS = (6.28125, 0.0019350051879882812, 3.0199157663446332e-07)
ROUND = 1.5 * 2.0 ** 23
PI_BELOW = 3.1415925
RSQRT_MAGIC = float(0x5F3759DF)


def hybrid_blocks(nc, t):
    ctx = ExitStack()
    with ctx:
        used = [SBUF_BASE]

        def sb(name, shape, dt=F32):
            v = nc.alloc_sbuf_tensor_at(name, shape, dt, offset=used[0]).ap()
            used[0] += (math.prod(shape[1:]) * 4 + 31) // 32 * 32
            return v

        def sem(name):
            return ctx.enter_context(nc.semaphore(name))

        ring = sb("ring", [P, OWN_SLOTS, SLOT])
        w_split = nc.alloc_sbuf_tensor_at("w_split", [P, WBUFS, 2, SLOT // 2], F32R,
                                          offset=SBUF_BASE + DENSE_SLOTS * SLOT * 4).ap()
        xs = sb("xs", [P, HALVES, D])
        xn = sb("xn", [P, HALVES, D])
        hT_at = used[0]
        hT_hi, hT_lo = sb("hT_hi", [P, KT, T], F32R), sb("hT_lo", [P, KT, T], F32R)
        hT_f = nc.alloc_sbuf_tensor_at("hT_f", [P, KT, T], F32, offset=hT_at).ap()
        xn_hi, xn_lo = (nc.alloc_sbuf_tensor_at(n, [P, HALVES, D], F32R, offset=hT_at + i * HALVES * D * 4).ap()
                        for i, n in enumerate(("xn_hi", "xn_lo")))
        ident = sb("ident", [P, P])
        ones = sb("ones", [P, P])
        later = sb("later", [P, P])
        tri = sb("tri", [P, P])
        tril = sb("tril", [P, P])
        slot_ids = sb("slot_ids", [P, P])
        vec_rows = sb("vec_rows", [NVEC, P])
        vec = sb("vec", [P, NVEC])
        row = sb("row", [P, NROW])
        router = sb("router", [P, KT, EXPERTS])
        stat = sb("stat", [P, 640])
        arena_at = used[0]
        arena = sb("arena", [P, 25 * 1024])
        ps = ctx.enter_context(nc.psum_tensor("ps", [P, 8, 512], F32))
        psf = ps[:, :, :].rearrange("p b n -> p (b n)")

        def at(off, *shape):
            n = math.prod(shape)
            v = arena[:, off:off + n]
            names = "abcd"[:len(shape)]
            if len(shape) > 1:
                v = v.rearrange(f"p ({' '.join(names)}) -> p {' '.join(names)}", **dict(zip(names, shape)))
            return v

        def split_at(name, off, *shape):
            return nc.alloc_sbuf_tensor_at(name, [P, *shape], F32R, offset=arena_at + off * 4).ap()

        K = 1024
        dq = at(0, HALVES, D)
        dk = at(2 * K, HALVES, D)
        dv = at(4 * K, HALVES, D)
        q = at(6 * K, HALVES, HEADS * QK)
        v1 = at(9 * K, HALVES, HEADS * VD)
        kf = at(11 * K, HALVES, HEADS * QK)
        ga = at(14 * K, HALVES, D)
        gb = at(16 * K, HALVES, D)
        c_sb = at(18 * K, HALVES, C_COLS)
        cT = [split_at(n, 18 * K + 1152 + i * K, 2, RT, T) for i, n in enumerate(("cT_hi", "cT_lo"))]
        qkT = [at(18 * K + i * 512, 512) for i in range(2)]
        pt_sb = [at(19 * K + i * 512, 2, T) for i in range(2)]
        rope_t = [at(20 * K + i * 512, HALVES, HEADS, HR) for i in range(2)]
        bgate = at(21 * K + 128, D)
        scores = [at(22 * K + 128 + i * K, 4, T) for i in (1, 0)]
        diff_scores = [xn[:, 0, :].rearrange("p (j t) -> p j t", j=4), scores[1], scores[0]]
        dist = at(24 * K + 128, HALVES, T)
        trig = at(24 * K + 640, 6, HALVES * HR)
        kr = at(24 * K + 832, HALVES, ROPE)
        posb = at(6 * K, 4, T)
        posi = at(7 * K, 3, T).bitcast(I32)
        EXPERT_RING = 2 * K
        hid_g = at(18 * K, FCOL)
        hid = at(18 * K + 512, FCOL)
        hidT = at(19 * K, 4, P)
        xe = at(19 * K + 512, KT, CAP)
        gated = at(19 * K + 768, HALVES, P)
        scat = at(20 * K, T)
        ye = at(20 * K + 256, DCOL)
        onehot = split_at("onehot", 20 * K + 512, HALVES, CAP)
        logit = at(20 * K + 576, HALVES, EXPERTS)
        aff = at(20 * K + 608, HALVES, EXPERTS)
        slot_t = at(20 * K + 640, HALVES, EXPERTS)
        routing = at(20 * K + 672, 5, T)[0:EXPERTS]
        sgu_in = at(22 * K, SG, P)
        p_in = at(22 * K + 512, HALVES, PLE)
        wsT = at(23 * K, SG, P)
        p_f = at(23 * K + 512, PLE // P, T)
        pT = [split_at(n, 24 * K + i * 512, PLE // P, T) for i, n in enumerate(("pT_hi", "pT_lo"))]
        yT = [split_at(n, i * 2 * K, KT, T) for i, n in enumerate(("yT_hi", "yT_lo"))]
        a_bT = at(4 * K, 2, T)
        a_hT = at(4 * K + 512, 2, T)
        root_row = at(6 * K, T)
        diag = at(6 * K + 256, T)
        conv = at(5 * K, 2, T + CONVW - 1)
        conv_y = at(5 * K + 520, T)
        qk2 = at(7 * K, HALVES, 2 * SATT)
        v2 = at(9 * K, HALVES, SATT)
        u2 = at(10 * K, HALVES, SGU)
        cv2 = at(10 * K + 512, HALVES, SGU)
        qkT2 = at(11 * K, SATT // P, 512)
        SC = 384
        na = at(13 * K, 2, SC)
        spl = at(13 * K + 2 * SC, 2, SC)
        lr = at(13 * K + 4 * SC, 2, SC)
        lb = [at(13 * K + (6 + 2 * i) * SC, 2, SC) for i in range(2)]
        yc = at(17 * K, HALVES, SGU)
        fT = [split_at(n, i * 8 * K, DFF // P, T) for i, n in enumerate(("fT_hi", "fT_lo"))]
        f_r = [at(16 * K + i * 512, 2 * T) for i in range(2)]
        f_2 = at(17 * K, 2 * T)
        pe_sb = at(18 * K, HALVES, D)
        gate2 = at(20 * K, HALVES, D)
        sq = xn[:, :, :].rearrange("p h d -> p (h d)")

        ss_x, rstd_x = stat[:, 0:2], stat[:, 2:4]
        ss_c, rstd_c = stat[:, 4:8], stat[:, 8:12]
        ss_h, rstd_h = stat[:, 312:376], stat[:, 376:440]
        mxn = [stat[:, 80 + 4 * i:84 + 4 * i] for i in range(2)]
        sums = [stat[:, 88 + 4 * i:92 + 4 * i] for i in range(2)]
        rec = [stat[:, 96 + 4 * i:100 + 4 * i] for i in range(2)]
        lam, lam_s = stat[:, 104:105], stat[:, 106:108]
        qk_w = stat[:, 126:127]
        freq = stat[:, 108:124]
        posc_f = stat[:, 128:136]
        nw = [stat[:, 440 + 64 * i:504 + 64 * i] for i in range(3)]
        ss_kr = stat[:, 232:234]
        ss_d, rstd_d = stat[:, 16:48], stat[:, 48:80]
        ss_o, rstd_o = stat[:, 272:288], stat[:, 288:304]
        rmax, rsum, rinv = stat[:, 304:306], stat[:, 306:308], stat[:, 308:310]
        rstd_0 = stat[:, 310:312]
        rstd_2 = stat[:, 632:634]
        posc = sb("posc", [P, HALVES, 3], I32)
        top8 = sb("top8", [EXPERTS, 4, 8])
        rcount = sb("rcount", [EXPERTS, 2])

        slot_loaded = [sem(f"slot_loaded{i}") for i in range(SLOTS)]
        chunk_used = sem("chunk_used")
        split_hi, split_lo, tile_used = sem("split_hi"), sem("split_lo"), sem("tile_used")
        chunk_split = sem("chunk_split")
        x_loaded, norm_w_loaded = sem("x_loaded"), sem("norm_w_loaded")
        vec_loaded, small_loaded = sem("vec_loaded"), sem("small_loaded")
        late_loaded, pw_raw = sem("late_loaded"), sem("pw_raw")
        gate_bias_loaded = sem("gate_bias_loaded")
        masks_ready = sem("masks_ready")
        vec_done, vec_ready = sem("vec_done"), sem("vec_ready")
        pw_done, pw_ready = sem("pw_done"), sem("pw_ready")
        tr_done, hi_ready, lo_ready = sem("tr_done"), sem("hi_ready"), sem("lo_ready")
        sq_act, rstd_ready = sem("sq_act"), sem("rstd_ready")
        xn_dve, xn_act, x_ready = sem("xn_dve"), sem("xn_act"), sem("x_ready")
        block_dve, block_act = sem("block_dve"), sem("block_act")
        sq_ready, sq_read = sem("sq_ready"), sem("sq_read")
        c_sq, c_norm = sem("c_sq"), sem("c_norm")
        cT_done, cT_hi, cT_lo = sem("cT_done"), sem("cT_hi"), sem("cT_lo")
        dqk_ready, qk_ready = sem("dqk_ready"), sem("qk_ready")
        lam_in, lam_exp = sem("lam_in"), sem("lam_exp")
        angle_ready, trig_ready = sem("angle_ready"), sem("trig_ready")
        gate_in, gate_ready = sem("gate_in"), sem("gate_ready")
        hT_done, hT_evac, hS_done, hS_read = sem("hT_done"), sem("hT_evac"), sem("hS_done"), sem("hS_read")
        max_ready, exp_done, prob_ready = sem("max_ready"), sem("exp_done"), sem("prob_ready")
        hP_done, hP_evac, hO_done, hO_evac = sem("hP_done"), sem("hP_evac"), sem("hO_done"), sem("hO_evac")
        od_sums, od_root, od_ready = sem("od_sums"), sem("od_root"), sem("od_ready")
        od_gated, merged_ready = sem("od_gated"), sem("merged_ready")
        logit_done, rmax_ready, rexp_done, aff_ready = sem("logit_done"), sem("rmax_ready"), sem("rexp_done"), sem("aff_ready")
        affT_done, slot_done, slotT_done, onehot_ready = sem("affT_done"), sem("slot_done"), sem("slotT_done"), sem("onehot_ready")
        gather_done = sem("gather_done")
        router_act, router_dve = sem("router_act"), sem("router_dve")
        xe_ready, silu_done, hid_ready = sem("xe_ready"), sem("silu_done"), sem("hid_ready")
        hidT_done, hidT_ready, ye_ready = sem("hidT_done"), sem("hidT_ready"), sem("ye_ready")
        gated_ready, scat_done, scat_ready = sem("gated_ready"), sem("scat_done"), sem("scat_ready")
        e_scatter, moe_added = sem("e_scatter"), sem("moe_added")
        diag_ready, row_done, row_read, conv_read = sem("diag_ready"), sem("row_done"), sem("row_read"), sem("conv_read")
        gelu_done, v_ready = sem("gelu_done"), sem("v_ready")
        qk2_ready, qkT2_done, qkT2_evac = sem("qk2_ready"), sem("qkT2_done"), sem("qkT2_evac")
        z_done, sp_ready, lr_ready = sem("z_done"), sem("sp_ready"), sem("lr_ready")
        suf_done, arg_ready, w_exp, w_ready = sem("suf_done"), sem("arg_ready"), sem("w_exp"), sem("w_ready")
        yb_done, y_conv, y_pair, y_gate = sem("yb_done"), sem("y_conv"), sem("y_pair"), sem("y_gate")
        cv_ready, sv_done, yc_ready, ycT_done, ycT_hi = sem("cv_ready"), sem("sv_done"), sem("yc_ready"), sem("ycT_done"), sem("ycT_hi")
        f_relu, f_hi, f_ready = sem("f_relu"), sem("f_hi"), sem("f_ready")
        xn_hi_ready, xn_lo_ready = sem("xn_hi_ready"), sem("xn_lo_ready")
        proj_out, half_done = sem("proj_out"), sem("half_done")
        gate2_ready, out_stored = sem("gate2_ready"), sem("out_stored")
        out_ready, out_ready_pool = sem("out_ready"), sem("out_ready_pool")
        dve_step, act_step, pool_step = sem("dve_step"), sem("act_step"), sem("pool_step")

        FIRST_BLOCK = [("c", "w_in", 0, C_COLS, D, "B"), ("dq", "w_in", C_COLS, D, D, "A"),
                       ("uq0", "mla_w_uq", 0, 768, RANK, "B"), ("uq1", "mla_w_uq", 768, 768, RANK, "A"),
                       ("ukv0", "mla_w_ukv", 0, 1024, RANK, "B"), ("ukv1", "mla_w_ukv", 1024, 1024, RANK, "A"),
                       ("dk", "w_in", C_COLS + D, D, D, "B"), ("dv", "w_in", C_COLS + 2 * D, D, D, "A"),
                       ("gate_a", "w_in", C_COLS + 3 * D, D, D, "A"), ("gate_b", "w_in", C_COLS + 4 * D, D, D, "A"),
                       ("out", "w_out", 0, D, D, "B")]
        SECOND_BLOCK = [("qk2", "w_in_2", 768, 1024, D, "B"), ("v2", "w_in_2", 1792, 512, D, "A"),
                        ("conv", "w_in_2", 0, 768, D, "A"), ("cuv", "w_in_2", 2304, 512, D, "A"),
                        ("out2", "w_out_2", 0, D, D, "B"), ("proj", "w_ple_proj_2", 0, D, PLE, "A"),
                        ("up0", "w_ff1_2", 0, D, D, "A"), ("up1", "w_ff1_2", D, D, D, "B"),
                        ("up2", "w_ff1_2", 2 * D, D, D, "A"), ("up3", "w_ff1_2", 3 * D, D, D, "B"),
                        ("down", "w_ff2_2", 0, D, DFF, "A"), ("gate2", "w_ple_gate_2", 0, D, D, "A")]
        TILE0, TILES, COLS, SETS = {}, {}, {}, {}
        chunks = []
        for name, weight, c0, cols, rows, banks in FIRST_BLOCK + SECOND_BLOCK:
            if name == "qk2":
                n_first = len(chunks)
            TILE0[name], TILES[name], COLS[name], SETS[name] = 2 * len(chunks), rows // P, cols, banks
            for k in range(rows // (2 * P)):
                chunks.append(t[weight][0][2 * k * P:2 * (k + 1) * P, c0:c0 + cols].rearrange("(k p) c -> p k c", p=P))

        def done(name):
            return TILE0[name] + TILES[name]

        def slot_buf(slot):
            return ring[:, slot, :] if slot < OWN_SLOTS else at(EXPERT_RING + (slot - OWN_SLOTS) * SLOT, SLOT)

        def slot_view(slot, cols):
            return slot_buf(slot)[:, 0:2 * cols].rearrange("p (k c) -> p k c", k=2)

        last_dense = [i % DENSE_SLOTS for i in range(n_first - DENSE_SLOTS, n_first)]
        EXPERT_SLOT = [8, 9, last_dense[0], 10, 11, 12, 13, 14, 15, *last_dense[1:], 5, 6, 7]
        assert sorted(EXPERT_SLOT) == list(range(SLOTS))

        def landed(i):
            return 16 * (i // DENSE_SLOTS + 1 + (0 if i < n_first else EXPERTS * EXPERT_CHUNKS // SLOTS))

        def expert_slot(j_e, k):
            return EXPERT_SLOT[(j_e * EXPERT_CHUNKS + k) % SLOTS]

        def expert_landed(j_e, k):
            slot = expert_slot(j_e, k)
            before = len(range(slot, n_first, DENSE_SLOTS)) if slot < DENSE_SLOTS else 0
            return 16 * (before + (j_e * EXPERT_CHUNKS + k) // SLOTS + 1)

        ALL_EXPERTS = SLOTS + EXPERTS * EXPERT_CHUNKS

        SET = {"A": 0, "B": 4}

        def pieces(name):
            cols = COLS[name]
            n = -(-cols // 512)
            width = cols // n if cols % 512 and cols % 512 < 256 else 512
            return [(c, min(width, cols - c)) for c in range(0, cols, width)]

        def pset(s, h, n=D):
            return psf[:, 512 * SET[s] + h * D:512 * SET[s] + h * D + n]

        def cut_up(name):
            return pieces(name)[0][1] < 512 < COLS[name]

        def two_pieces(src):
            return src.rearrange("p (j c) -> p j c", j=2)[:, :, 0:C_COLS // 2]

        N_VEC = len(VEC_ROWS) - 1 + 2
        WARM_START, WARM_MERGE = 9, 6
        WARM_ROUTER, WARM_SOFTMAX, WARM_CHOICE, WARM_GATHER = 4, 4, 12, 2
        WARM_LAST, WARM_MIX, WARM_PAIR = 4, 2, 4
        block = ctx.enter_context(nc.Block())

        @block.sync
        def _(sp):
            x_dram = t["x"][0].rearrange("(h p) d -> p h d", p=P)
            sp.dma_start(xs[:, :, :], x_dram).then_inc(x_loaded, 16)

            def load(i):
                slot = i % DENSE_SLOTS
                if i >= n_first and i - DENSE_SLOTS < n_first:
                    sp.wait_ge(chunk_used, ALL_EXPERTS - SLOTS + EXPERT_SLOT.index(slot) + 1)
                elif i >= DENSE_SLOTS:
                    sp.wait_ge(chunk_split, i - DENSE_SLOTS + 1)
                sp.dma_start(slot_view(slot, chunks[i].shape[2]), chunks[i]).then_inc(slot_loaded[slot], 16)

            def load_vec(name, rows):
                src = t[name]
                if name.startswith("diff"):
                    for i in range(2):
                        sp.dma_start(vec_rows[VEC[name]:VEC[name] + 1, i * DQK:(i + 1) * DQK], src).then_inc(vec_loaded, 16)
                    return
                src = src[0].rearrange("w (r c) -> (w r) c", c=P) if name == "conv_w_2" else (
                    src[0] if name == "sgu_b_2" else src[0].rearrange("(r c) -> r c", c=P))
                loaded = norm_w_loaded if name == "attn_norm_w" else vec_loaded
                sp.dma_start(vec_rows[VEC[name]:VEC[name] + rows, :], src).then_inc(loaded, 16)

            load_vec(*VEC_ROWS[0])
            load(0)
            load(1)
            load(2)
            for name, n in VEC_ROWS[1:]:
                load_vec(name, n)
            sp.dma_start(posi[:, 0, :], t["positions"][0].partition_broadcast(P)).then_inc(small_loaded, 16)
            for h in range(HALVES):
                sp.dma_start(posc[:, h, 0:1], t["positions"][0, h * P:(h + 1) * P].rearrange("(p o) -> p o", o=1)
                              ).then_inc(small_loaded, 16)
            for name, n in ROW_VECS:
                src = t[name][0]
                src = src.rearrange("a b -> (a b)") if name == "diff_lambda" else src
                sp.dma_start(row[:, ROW[name]:ROW[name] + n], src.partition_broadcast(P)).then_inc(small_loaded, 16)
            sp.dma_start(bgate, t["b_gate"][0, 0:D].partition_broadcast(P)).then_inc(small_loaded, 16)
            sp.dma_start(router[:, :, :], t["router_w"][0].rearrange("(k p) e -> p k e", p=P)).then_inc(small_loaded, 16)
            for i in range(3, n_first):
                load(i)
            with sp.Fori(0, EXPERTS // PAIR) as pair_i:
                for j_e in range(PAIR):
                    e = pair_i * PAIR + j_e
                    for k in range(EXPERT_CHUNKS):
                        m, kt, slot = k // KT, k % KT, expert_slot(j_e, k)
                        if m < 2:
                            w = t["expert_w_gate" if m == 0 else "expert_w_up"]
                            src = w[0, e, kt * P:(kt + 1) * P, :]
                            dst = slot_buf(slot)
                        else:
                            src = t["expert_w_down"][0, e, 2 * kt * P:(2 * kt + 2) * P, :].rearrange("(k p) c -> p k c", p=P)
                            dst = slot_view(slot, D)
                        sp.wait_ge(chunk_used, EXPERT_CHUNKS * e + k + 1)
                        sp.dma_start(dst, src).then_inc(slot_loaded[slot], 16)
            for i in range(n_first, len(chunks)):
                load(i)
            sp.wait_ge(out_ready, 1)
            sp.dma_start(t["out"][0, 0:P, :], gate2[:, 0, :]).then_inc(out_stored, 16)
            for c, ready, n in ((0, out_ready, 2), (1, out_ready_pool, 1)):
                cols = slice(c * D // 2, (c + 1) * D // 2)
                sp.wait_ge(ready, n)
                sp.dma_start(t["out"][0, P:T, cols], gate2[:, 1, cols]).then_inc(out_stored, 16)
            sp.wait_ge(out_stored, 16 * 3)

        HALVES_APART = ["out", "out2", "down", "gate2"]
        N_SMALL = len(ROW_VECS) + 5
        N_MASKS = 7
        STAGES = ["attn", "merge", "mix", "ff", "ple"]
        TRANSPOSED = ["attn", "merge", "ffn", "mix", "ff", "ple"]
        EVACS = ["c", "dq", "uq0", "uq1", "ukv0", "ukv1", "dk", "dv", "qk2"]

        def evacuated(name):
            return EVACS.index(name) + 1

        def half_complete(engine, name, h):
            if h == 0:
                engine.wait_ge(half_done, HALVES_APART.index(name) + 1)
            else:
                engine.wait_ge(tile_used, done(name))

        @block.gpsimd
        def _(pool):
            count = [0]

            def step(ins):
                count[0] += 1
                ins.then_inc(pool_step, 1)
                pool.wait_ge(pool_step, count[0])

            def mask(buf, fill_in, fill_out, op, pattern, mult):
                step(pool.memset(buf[:, :], fill_in))
                pool.affine_select(out=buf[:, :], in_=buf[:, :], compare_op=op, fill=fill_out, base=0,
                                   pattern=pattern, channel_multiplier=mult).then_inc(masks_ready, 1)

            def low_parts(name, k0=0, k1=None):
                cols = COLS[name]
                for kt in range(k0, TILES[name] if k1 is None else k1):
                    n = TILE0[name] + kt
                    w = slot_view(n // 2 % DENSE_SLOTS, cols)[:, n % 2, :]
                    buf = w_split[:, n % WBUFS, :, 0:cols]
                    pool.wait_ge(split_hi, n + 1)
                    ins = pool.tensor_tensor(buf[:, 1, :], w, buf[:, 0, :].bitcast(F32), ALU.subtract)
                    ins.then_inc(split_lo, 1)
                    if n % 2:
                        pool.wait_ge(split_lo, n + 1)
                        pool.sem_inc(chunk_split, 1)

            mask(ident, 0.0, 1.0, ALU.not_equal, [[-1, P]], 1)
            mask(tril, 1.0, 0.0, ALU.is_ge, [[1, P]], -1)
            mask(tri, 1.0, 0.0, ALU.is_gt, [[1, P]], -1)
            mask(later, 1.0, 0.0, ALU.is_gt, [[-1, P]], 1)
            pool.memset(ones[:, :], 1.0).then_inc(masks_ready, 1)
            pool.iota(slot_ids[:, :].rearrange("p (j s) -> p j s", s=CAP), pattern=[[0, P // CAP], [1, CAP]], base=1,
                      channel_multiplier=0, allow_small_or_imprecise_dtypes=True).then_inc(masks_ready, 1)
            for i in range(HR):
                f = pool.memset(freq[:, i:i + 1], INV_FREQ[i])
            f.then_inc(masks_ready, 1)

            for name in ("c", "dq", "uq0", "uq1", "ukv0", "ukv1", "dk", "dv", "gate_a"):
                low_parts(name)
            low_parts("gate_b", 0, 4)

            wl = row[:, ROW["diff_subln_w"]:ROW["diff_subln_w"] + DV]
            pool.wait_ge(small_loaded, 16 * N_SMALL)
            step(pool.tensor_scalar(wl, wl, 1.0 - LAM_INIT, None, ALU.mult))
            pool.wait_ge(hO_evac, DHEADS)
            pool.wait_ge(sq_read, 5)
            for h in range(HALVES):
                pool.tensor_tensor(xn[:, h, :], dq[:, h, :], dq[:, h, :], ALU.mult).then_inc(od_sums, 1)
                low_parts("gate_b", 4 + h, 5 + h)
            pool.wait_ge(od_root, 1)
            for h in range(HALVES):
                od = dq[:, h, :].rearrange("p (n d) -> p n d", d=DV)
                r = rstd_o[:, h * DHEADS:(h + 1) * DHEADS]
                step(pool.tensor_tensor(od, od, r.unsqueeze(2).to_broadcast([P, DHEADS, DV]), ALU.mult))
                low_parts("gate_b", 6 + h, 7 + h)
                step(pool.tensor_tensor(od, od, wl.unsqueeze(1).to_broadcast([P, DHEADS, DV]), ALU.mult))
            low_parts("out", 0, 3)
            pool.wait_ge(pool_step, count[0])
            pool.sem_inc(od_ready, 1)
            pool.wait_ge(gate_ready, 3)
            cols = slice(D // 2, D)
            pool.tensor_tensor(dq[:, :, cols], dq[:, :, cols], gb[:, :, cols], ALU.mult).then_inc(od_gated, 1)
            low_parts("out", 3)

            pool.wait_ge(xn_hi_ready, HALVES)
            for h in range(HALVES):
                pool.tensor_tensor(xn_lo[:, h, :], xn[:, h, :], xn_hi[:, h, :].bitcast(F32), ALU.subtract).then_inc(xn_lo_ready, 1)
            pool.wait_ge(pw_raw, 3)
            step(pool.tensor_tensor(wsT, wsT, tril[:, :].unsqueeze(1).to_broadcast([P, SG, P]), ALU.mult))
            pool.tensor_tensor(pT[1], p_f, pT[0].bitcast(F32), ALU.subtract).then_inc(pw_ready, 1)

            for name, *_ in SECOND_BLOCK:
                low_parts(name)
            cols = slice(D // 2, D)
            pool.wait_ge(proj_out, 2)
            pool.wait_ge(x_ready, 6)
            pool.wait_ge(gate2_ready, 2)
            step(pool.tensor_tensor(gate2[:, 1, cols], pe_sb[:, 1, cols], gate2[:, 1, cols], ALU.mult))
            pool.tensor_tensor(gate2[:, 1, cols], xs[:, 1, cols], gate2[:, 1, cols], ALU.add).then_inc(out_ready_pool, 1)

        @block.scalar
        def _(act):
            def high_parts(name, k0=0, k1=None):
                cols = COLS[name]
                for kt in range(k0, TILES[name] if k1 is None else k1):
                    n = TILE0[name] + kt
                    i, slot = n // 2, n // 2 % DENSE_SLOTS
                    act.wait_ge(slot_loaded[slot], landed(i))
                    if n >= WBUFS:
                        act.wait_ge(tile_used, n - WBUFS + 1)
                    act.activation(w_split[:, n % WBUFS, 0, 0:cols], slot_view(slot, cols)[:, n % 2, :],
                                   ACT.Copy).then_inc(split_hi, 1)

            def square_half():
                act.activation(xn[:, 0, :], xs[:, 0, :], ACT.Square, accum_out=ss_x[:, 0:1]).then_inc(sq_act, 1)

            def scale_half(n):
                act.wait_ge(rstd_ready, n + 1)
                act.activation(xn[:, 0, :], xs[:, 0, :], ACT.Copy, scale=rstd_x[:, 0:1]).then_inc(xn_act, 1)

            def high_stage(s, base, weight):
                for kt in range(KT):
                    if kt % 2 == 0:
                        act.wait_ge(tr_done, 4 * TRANSPOSED.index(s) + kt // 2 + 1)
                    scale = vec[:, VEC[weight] + kt:VEC[weight] + kt + 1] if weight else 1.0
                    act.activation(hT_hi[:, kt, :], ps[:, base + kt // 2, (kt % 2) * T:(kt % 2 + 1) * T], ACT.Copy,
                                   scale=scale).then_inc(hi_ready, 1)

            def evac(name, *parts):
                act.wait_ge(tile_used, done(name))
                scale = rstd_0[:, 0:1] if name[0] in "cd" else rstd_x[:, 0:1] if name == "qk2" else 1.0
                src = pset(SETS[name], 0, D if cut_up(name) else COLS[name])
                for dst, cut in parts:
                    ins = act.activation(dst, cut(src), ACT.Copy, scale=scale)
                ins.then_inc(block_act, 1)

            def squares(n, src, dst):
                if n:
                    act.wait_ge(sq_read, n)
                act.activation(dst, src, ACT.Square).then_inc(sq_ready, 1)

            def whole(src):
                return src

            high_parts("c", 0, 2)
            act.wait_ge(vec_ready, 1)
            high_stage("attn", 0, "attn_norm_w")
            high_parts("c", 2, 4)
            act.wait_ge(x_loaded, 16)
            square_half()
            high_parts("c", 4)
            high_parts("dq", 0, 3)
            act.wait_ge(rstd_ready, 1)
            evac("c", (c_sb[:, 0, :].rearrange("p (j c) -> p j c", j=2), two_pieces))
            act.wait_ge(block_act, evacuated("c"))
            act.wait_ge(block_dve, evacuated("c"))
            for j in range(2):
                for h in range(HALVES):
                    act.activation(sq[:, (2 * j + h) * RANK:(2 * j + h + 1) * RANK], c_sb[:, h, j * RANK:(j + 1) * RANK], ACT.Square,
                                   accum_out=ss_c[:, 2 * j + h:2 * j + h + 1]).then_inc(c_sq, 1)
            for h in range(HALVES):
                act.activation(sq[:, D + h * ROPE:D + (h + 1) * ROPE], c_sb[:, h, 2 * RANK:C_COLS], ACT.Square,
                               accum_out=ss_kr[:, h:h + 1]).then_inc(c_sq, 1)
            high_parts("dq", 3)
            for j in range(2):
                act.wait_ge(vec_ready, 2)
                act.wait_ge(cT_done, j + 1)
                for kt in range(RT):
                    w = VEC["mla_q_norm_w" if j == 0 else "mla_kv_norm_w"] + kt
                    act.activation(cT[0][:, j, kt, :], ps[:, 4 + j, kt * T:(kt + 1) * T], ACT.Copy,
                                   scale=vec[:, w:w + 1]).then_inc(cT_hi, 1)
            high_parts("uq0")
            high_parts("uq1", 0, 1)
            act.wait_ge(lam_in, 1)
            evac("dq", (dq[:, 0, :], whole))
            high_parts("uq1", 1)
            high_parts("ukv0", 0, 1)
            evac("uq0", (q[:, 0, 0:768], whole))
            act.wait_ge(block_act, evacuated("dq"))
            act.wait_ge(block_dve, evacuated("dq"))
            act.wait_ge(c_norm, 4)
            squares(0, dq.rearrange("p h d -> p (h d)"), sq)
            high_parts("ukv0", 1)
            high_parts("ukv1", 0, 1)
            evac("uq1", (q[:, 0, 768:1536], whole))
            high_parts("ukv1", 1)
            high_parts("dk", 0, 1)
            act.wait_ge(lam_in, 1)
            act.activation(lam_s, lam_s, ACT.Exp).then_inc(lam_exp, 1)
            act.wait_ge(angle_ready, 1)
            act.activation(trig[:, 4:6, :], trig[:, 4:6, :], ACT.Sin).then_inc(trig_ready, 1)

            def kv_parts(h, i):
                heads = slice(i * HEADS // 2, (i + 1) * HEADS // 2)
                k_out = kf[:, h, :].rearrange("p (n d) -> p n d", d=QK)[:, heads, 0:NOPE]
                v_out = v1[:, h, :].rearrange("p (n d) -> p n d", d=VD)[:, heads, :]
                return ((k_out, lambda src: src.rearrange("p (n d) -> p n d", d=128)[:, :, 0:NOPE]),
                        (v_out, lambda src: src.rearrange("p (n d) -> p n d", d=128)[:, :, NOPE:128]))

            evac("ukv0", *kv_parts(0, 0))
            high_parts("dk", 1, 3)
            evac("ukv1", *kv_parts(0, 1))
            act.wait_ge(block_act, evacuated("ukv1"))
            act.wait_ge(block_dve, evacuated("ukv1"))
            squares(1, q[:, 0, :], sq[:, 0:HEADS * QK])
            high_parts("dk", 3, 5)
            squares(2, q[:, 1, :], sq[:, 0:HEADS * QK])
            high_parts("dk", 5, 7)
            squares(3, kf.rearrange("p h (n d) -> p (h n) d", d=QK)[:, :, 0:NOPE], sq.rearrange("p (n d) -> p n d", d=NOPE))
            high_parts("dk", 7)
            high_parts("dv", 0, 3)
            evac("dk", (dk[:, 0, :], whole))
            act.wait_ge(block_act, evacuated("dk"))
            act.wait_ge(block_dve, evacuated("dk"))
            squares(4, dk.rearrange("p h d -> p (h d)"), sq)
            high_parts("dv", 3)
            high_parts("gate_a", 0, 2)

            def diff_probs(u):
                act.wait_ge(hP_done, u + 1)
                if u >= 2:
                    act.wait_ge(hO_done, u - 1)
                act.activation(pt_sb[u % 2], ps[:, 7, :].rearrange("p (k t) -> p k t", k=2), ACT.Copy).then_inc(hP_evac, 1)

            def diff_output(u):
                act.wait_ge(hO_done, u + 1)
                act.activation(dq[:, :, u * DV:(u + 1) * DV], ps[:, 4, 0:T].rearrange("p (h d) -> p h d", h=2),
                               ACT.Copy).then_inc(hO_evac, 1)

            for i in range(DHEADS + 1):
                if i < DHEADS:
                    act.wait_ge(hT_done, i + 1)
                    if i >= 2:
                        act.wait_ge(hS_done, i - 1)
                    act.activation(qkT[i % 2][:, 0:T], ps[:, 4, 0:T], ACT.Copy, scale=qk_w)
                    act.activation(qkT[i % 2][:, T:2 * T], ps[:, 4, T:2 * T], ACT.Copy).then_inc(hT_evac, 1)
                if i == 0:
                    evac("dv", (dv[:, 0, :], whole))
                    high_parts("gate_a", 2, 3)
                if 1 <= i < KT - 2:
                    high_parts("gate_a", i + 2, i + 3)
                if i == DHEADS:
                    high_parts("gate_b", 0, 2)
                if i == DHEADS:
                    diff_probs(i - 3)
                    diff_output(i - 4)
                if i >= 1:
                    u = i - 1
                    act.wait_ge(max_ready, u + 1)
                    for j in range(4):
                        e = act.activation(diff_scores[u % 3][:, j, :], diff_scores[u % 3][:, j, :], ACT.Exp,
                                           bias=mxn[u % 2][:, j:j + 1], accum_out=sums[u % 2][:, j:j + 1])
                    e.then_inc(exp_done, 1)
                if 3 <= i < DHEADS:
                    diff_probs(i - 3)
                if 4 <= i < DHEADS:
                    diff_output(i - 4)
            gate_b_at = {0: 2, 2: 3, 3: 4, 5: 5, 7: 6, 9: 7}
            for i in range(HEADS + 1):
                if i < HEADS:
                    u = DHEADS + i
                    act.wait_ge(hT_done, u + 1)
                    act.wait_ge(hS_done, u - 1)
                    act.activation(qkT[u % 2][0:QK, :], ps[0:QK, 4, :], ACT.Copy).then_inc(hT_evac, 1)
                if i in gate_b_at:
                    high_parts("gate_b", gate_b_at[i], gate_b_at[i] + 1)
                if i in (11, 13, 15):
                    high_parts("out", (i - 11) // 2, (i - 9) // 2)
                if i < 2:
                    diff_probs(DHEADS - 2 + i)
                if i >= 1:
                    u = DHEADS + i - 1
                    act.wait_ge(max_ready, u + 1)
                    act.wait_ge(hP_done, u - 1)
                    for h in range(HALVES):
                        e = act.activation(scores[u % 2][:, h, :], ps[:, 5, h * T:(h + 1) * T], ACT.Exp,
                                           bias=mxn[u % 2][:, h:h + 1], scale=QK ** -0.5, accum_out=sums[u % 2][:, h:h + 1])
                    e.then_inc(exp_done, 1)
                if i < 3:
                    diff_output(DHEADS - 3 + i)
                if i == 0:
                    act.wait_ge(gate_in, 2)
                    act.activation(ga, ga, ACT.Sigmoid).then_inc(gate_ready, 1)
                    act.dma_start(bgate, t["b_gate"][0, D:2 * D].partition_broadcast(P)).then_inc(gate_bias_loaded, 16)
            act.wait_ge(gate_in, 4)
            for c in range(2):
                g = gb[:, :, c * 512:(c + 1) * 512]
                act.activation(g, g, ACT.Sigmoid).then_inc(gate_ready, 1)

            high_stage("merge", 0, None)
            act.wait_ge(hP_done, DHEADS + HEADS)
            act.dma_start(sgu_in, t["sgu_w_2"][0].rearrange("g a b -> a g b")).then_inc(late_loaded, 16)
            act.dma_start(p_in, t["p_2"][0, 0].rearrange("(h p) d -> p h d", p=P)).then_inc(late_loaded, 16)
            high_parts("out", 3)
            def square(h):
                act.wait_ge(x_ready, h + 1)
                return act.activation(xn[:, h, :], xs[:, h, :], ACT.Square, accum_out=ss_x[:, h:h + 1])

            square(0)
            for kt in (2, 3, 6, 7):
                act.wait_ge(tr_done, 4 * TRANSPOSED.index("ffn") + kt // 2 + 1)
                act.activation(hT_f[:, kt, :], ps[:, kt // 2, (kt % 2) * T:(kt % 2 + 1) * T], ACT.Copy,
                               scale=vec[:, VEC["ffn_norm_w"] + kt:VEC["ffn_norm_w"] + kt + 1]).then_inc(router_act, 1)
            square(1).then_inc(sq_act, 1)
            act.activation(lam_s[:, 0:1], rstd_0[:, 0:1], ACT.Exp)
            scale_half(1)
            act.wait_ge(rmax_ready, 1)
            for h in range(HALVES):
                e = act.activation(logit[:, h, :], logit[:, h, :], ACT.Exp, bias=rmax[:, h:h + 1],
                                   accum_out=rsum[:, h:h + 1])
            e.then_inc(rexp_done, 1)
            act.wait_ge(logit_done, 1)
            act.wait_ge(xn_act, 1)
            act.wait_ge(xn_dve, 1)
            for h in range(HALVES):
                act.activation(xn_hi[:, h, :], xn[:, h, :], ACT.Copy).then_inc(xn_hi_ready, 1)
            act.wait_ge(pw_done, 2)
            act.activation(wsT, ps[:, 0, :].rearrange("p (g t) -> p g t", g=SG), ACT.Copy).then_inc(pw_raw, 1)
            act.activation(p_f, ps[:, 1, :].rearrange("p (k t) -> p k t", k=2), ACT.Copy).then_inc(pw_raw, 1)
            act.activation(pT[0], ps[:, 1, :].rearrange("p (k t) -> p k t", k=2), ACT.Copy).then_inc(pw_raw, 1)
            act.sem_inc(ye_ready, 1)
            with act.Fori(0, EXPERTS // PAIR) as pair_i:
                for j_e in range(PAIR):
                    e = pair_i * PAIR + j_e
                    act.wait_ge(scat_done, e + 2)
                    act.wait_ge(e_scatter, e + 1)
                    act.activation(scat, ps[:, 3, 256:512], ACT.Copy).then_inc(scat_ready, 1)
                    act.wait_ge(chunk_used, EXPERT_CHUNKS * e + SLOTS + KT)
                    act.wait_ge(hid_ready, e + 1)
                    act.activation(hid_g, ps[:, 0, :], ACT.Silu).then_inc(silu_done, 1)
                    act.wait_ge(hidT_done, e + 2)
                    act.activation(hidT, ps[:, 2, :].rearrange("p (c t) -> p c t", c=4), ACT.Copy).then_inc(hidT_ready, 1)
                    act.wait_ge(chunk_used, EXPERT_CHUNKS * e + SLOTS + EXPERT_CHUNKS)
                    act.activation(ye, ps[:, 3, 0:DCOL], ACT.Copy).then_inc(ye_ready, 1)

            act.wait_ge(chunk_used, ALL_EXPERTS)
            high_parts("qk2", 0, 3)
            high_stage("mix", 0, "norm1_g_2")
            square_half()
            high_parts("qk2", 3)
            high_parts("v2", 0, 3)
            act.wait_ge(rstd_ready, 3)
            evac("qk2", (qk2[:, 0, :], whole))
            act.wait_ge(block_act, evacuated("qk2"))
            act.wait_ge(block_dve, evacuated("qk2"))
            act.activation(sq, qk2.rearrange("p h d -> p (h d)"), ACT.Square).then_inc(sq_ready, 1)
            high_parts("v2", 3)
            high_parts("conv", 0, 3)
            for j in range(SATT // P):
                act.wait_ge(qkT2_done, j + 1)
                act.activation(qkT2[:, j, :], ps[:, 4 + j, :], ACT.Copy).then_inc(qkT2_evac, 1)

            def filling(p, first, n):
                for f in range(4 * p + 3 + first, 4 * p + 3 + first + n):
                    name = ("conv", "cuv", "out2")[f // KT]
                    high_parts(name, f % KT, f % KT + 1)

            for p in range(SHEADS // 2):
                act.wait_ge(z_done, p + 1)
                if p:
                    act.wait_ge(sp_ready, p)
                act.activation(na, ps[:, 4:6, 0:SC], ACT.Abs).then_inc(act_step, 1)
                act.wait_ge(act_step, 2 * p + 1)
                act.activation(na, na, ACT.Exp, scale=-1.0).then_inc(act_step, 1)
                filling(p, 0, 0)
                if p:
                    act.wait_ge(arg_ready, p)
                    act.activation(lb[(p - 1) % 2], lb[(p - 1) % 2], ACT.Exp).then_inc(w_exp, 1)
                    act.wait_ge(lr_ready, p)
                act.wait_ge(act_step, 2 * p + 2)
                act.activation(spl, na, ACT.Ln, bias=1.0).then_inc(sp_ready, 1)
                filling(p, 0, 4 - 0)
            act.wait_ge(tile_used, done("cuv"))
            for h in range(HALVES):
                src = pset(SETS["cuv"], h)
                act.activation(cv2[:, h, :], src[:, SGU:2 * SGU], ACT.Gelu, scale=rstd_x[:, h:h + 1]).then_inc(gelu_done, 1)
                act.activation(u2[:, h, :], src[:, 0:SGU], ACT.Gelu, scale=rstd_x[:, h:h + 1]).then_inc(gelu_done, 1)
            act.wait_ge(gelu_done, 4)
            act.wait_ge(sq_read, 6)
            act.activation(sq[:, 0:HALVES * SGU], cv2.rearrange("p h d -> p (h d)"), ACT.Square).then_inc(sq_ready, 1)
            act.wait_ge(arg_ready, SHEADS // 2)
            act.activation(lb[1], lb[1], ACT.Exp).then_inc(w_exp, 1)
            high_parts("out2", 3, 7)
            act.wait_ge(ycT_done, 1)
            act.activation(yT[0][:, 6:8, :], ps[:, 0, :].rearrange("p (c t) -> p c t", c=2), ACT.Copy).then_inc(ycT_hi, 1)
            high_parts("out2", 7)
            high_parts("proj")
            high_parts("up0", 0, 1)

            act.wait_ge(tile_used, done("proj"))
            act.activation(pe_sb[:, 0, :], pset(SETS["proj"], 0), ACT.Copy).then_inc(proj_out, 1)
            high_stage("ff", 4, "norm2_g_2")
            high_parts("up0", 1, 2)
            act.wait_ge(x_ready, 3)
            square_half()
            high_parts("up0", 2)
            high_parts("up1", 0, 3)
            for b in range(4):
                act.wait_ge(tile_used, done(f"up{b}"))
                for j in range(4):
                    k = 4 * b + j
                    if k >= 2:
                        act.wait_ge(f_ready, k - 1)
                    act.activation(f_r[k % 2].rearrange("p (c t) -> p c t", c=2),
                                   ps[:, SET[SETS[f"up{b}"]] + j, :].rearrange("p (c t) -> p c t", c=2),
                                   ACT.Relu).then_inc(f_relu, 1)
                    act.wait_ge(f_relu, k + 1)
                    act.activation(fT[0][:, 2 * k:2 * k + 2, :], f_r[k % 2].rearrange("p (c t) -> p c t", c=2),
                                   ACT.Square).then_inc(f_hi, 1)
                    following = f"up{b + 1}" if b < 3 else "down"
                    high_parts(following, 3 + j, 4 + j)
                if b < 3:
                    high_parts(following, 7)
                    high_parts(f"up{b + 2}" if b < 2 else "down", 0, 3)
            high_parts("down", 7)
            high_parts("gate2", 0, 3)

            high_stage("ple", 4, "norm3_g_2")
            act.wait_ge(x_ready, 5)
            square_half()
            high_parts("gate2", 3)
            act.wait_ge(rstd_ready, 5)
            act.activation(lam_s[:, 0:1], rstd_x[:, 0:1], ACT.Sigmoid)
            for h in range(HALVES):
                half_complete(act, "gate2", h)
                act.activation(gate2[:, h, :], pset(SETS["gate2"], h), ACT.Sigmoid, scale=rstd_x[:, h:h + 1]).then_inc(gate2_ready, 1)

        @block.vector
        def _(dve):
            count = [0]

            def step(ins):
                count[0] += 1
                ins.then_inc(dve_step, 1)
                dve.wait_ge(dve_step, count[0])

            def roots(ss, out, n, dim, ready=None):
                v, a, y = nw[0][:, 0:n], nw[1][:, 0:n], nw[2][:, 0:n]
                step(dve.tensor_scalar(v, ss, 1.0 / dim, EPS, ALU.mult, ALU.add))
                step(dve.tensor_scalar(a.bitcast(I32), v.bitcast(I32), 1, None, ALU.logical_shift_right))
                step(dve.tensor_scalar(y.bitcast(I32), a.bitcast(I32), -1.0, RSQRT_MAGIC, ALU.mult, ALU.add))
                step(dve.tensor_scalar(v, v, -0.5, None, ALU.mult))
                for k in range(3):
                    step(dve.tensor_tensor(a, y, y, ALU.mult))
                    step(dve.tensor_tensor(a, a, v, ALU.mult))
                    last = dve.scalar_tensor_tensor(out if k == 2 else y, a, 1.5, y, ALU.add, ALU.mult)
                    if k < 2 or ready is None:
                        step(last)
                last.then_inc(ready, 1) if ready is not None else None

            def square_half():
                step(dve.scalar_tensor_tensor(xn[:, 1, :], xs[:, 1, :], 1.0, xs[:, 1, :], ALU.mult, ALU.mult,
                                              accum_out=ss_x[:, 1:2]))

            def norm(n, root=rstd_x, scaled=True, squared=False):
                if not squared:
                    square_half()
                dve.wait_ge(sq_act, n + 1)
                roots(ss_x, root, 2, D, rstd_ready)
                dve.wait_ge(rstd_ready, n + 1)
                if scaled:
                    dve.tensor_scalar(xn[:, 1, :], xs[:, 1, :], rstd_x[:, 1:2], None, ALU.mult).then_inc(xn_dve, 1)

            def low_stage(s, base, weight):
                for kt in range(KT):
                    if kt % 2 == 0:
                        dve.wait_ge(hi_ready, KT * STAGES.index(s) + kt + 2)
                    src = ps[:, base + kt // 2, (kt % 2) * T:(kt % 2 + 1) * T]
                    scale = vec[:, VEC[weight] + kt:VEC[weight] + kt + 1] if weight else 1.0
                    dve.scalar_tensor_tensor(hT_lo[:, kt, :], src, scale, hT_hi[:, kt, :].bitcast(F32), ALU.mult,
                                             ALU.subtract).then_inc(lo_ready, 1)

            def evac(name, *parts):
                dve.wait_ge(tile_used, done(name))
                src = pset(SETS[name], 1, D if cut_up(name) else COLS[name])
                for dst, cut in parts:
                    if name[0] in "cd" or name == "qk2":
                        root = rstd_x if name == "qk2" else rstd_0
                        ins = dve.tensor_scalar(dst, cut(src), root[:, 1:2], None, ALU.mult)
                    else:
                        ins = dve.tensor_copy(dst, cut(src))
                ins.then_inc(block_dve, 1)

            def whole(src):
                return src

            def rows(name):
                n = dict(ROW_VECS)[name]
                return row[:, ROW[name]:ROW[name] + n]

            dve.wait_ge(vec_done, 1)
            dve.tensor_copy(vec[:, 0:KT], ps[:, 4, 0:KT]).then_inc(vec_ready, 1)
            dve.wait_ge(vec_ready, 1)
            low_stage("attn", 0, "attn_norm_w")
            dve.wait_ge(x_loaded, 16)
            norm(0, rstd_0, scaled=False)
            dve.wait_ge(vec_done, 2)
            dve.tensor_copy(vec[:, KT:NVEC], ps[:, 0, KT:NVEC]).then_inc(vec_ready, 1)
            dve.wait_ge(vec_ready, 2)
            dve.scalar_tensor_tensor(qk_w, vec[:, VEC["diff_q_hnorm_w"]:VEC["diff_q_hnorm_w"] + 1], DQK ** -0.5,
                                     vec[:, VEC["diff_k_hnorm_w"]:VEC["diff_k_hnorm_w"] + 1], ALU.mult, ALU.mult).then_inc(dve_step, 1)
            count[0] += 1

            evac("c", (c_sb[:, 1, :].rearrange("p (j c) -> p j c", j=2), two_pieces))
            dve.wait_ge(c_sq, 6)
            roots(ss_c, rstd_c, 4, RANK)
            for j in range(2):
                for h in range(HALVES):
                    c = c_sb[:, h, j * RANK:(j + 1) * RANK]
                    dve.tensor_scalar(c, c, rstd_c[:, 2 * j + h:2 * j + h + 1], None, ALU.mult).then_inc(c_norm, 1)

            dve.wait_ge(small_loaded, 16 * N_SMALL)
            for i, (op, c) in enumerate(((ALU.arith_shift_right, 12), (ALU.bitwise_and, 4095))):
                step(dve.tensor_scalar(posi[:, 1 + i, :], posi[:, 0, :], c, None, op))
                step(dve.tensor_scalar(posc[:, :, 1 + i], posc[:, :, 0], c, None, op))
                step(dve.tensor_copy(posb[:, i, :], posi[:, 1 + i, :]))
                step(dve.tensor_copy(posc_f[:, 2 * i:2 * i + 2], posc[:, :, 1 + i]))
            step(dve.tensor_copy(posc_f[:, 4:6], posc[:, :, 0]))
            for h in range(HALVES):
                for i in range(2):
                    step(dve.tensor_scalar(posb[:, 2 + i, :], posb[:, i, :], posc_f[:, 2 * i + h:2 * i + h + 1], None,
                                           ALU.subtract))
                step(dve.scalar_tensor_tensor(posb[:, 2, :], posb[:, 2, :], 4096.0, posb[:, 3, :], ALU.mult, ALU.add))
                step(dve.scalar_tensor_tensor(dist[:, h, :], posb[:, 2, :], -1.0, posb[:, 2, :], ALU.mult, ALU.max))
            ang, turns, sin_a, cos_a, tmp = trig[:, 0, :], trig[:, 1, :], trig[:, 4, :], trig[:, 5, :], trig[:, 2, :]
            for h in range(HALVES):
                step(dve.tensor_scalar(trig[:, 0, h * HR:(h + 1) * HR], freq, posc_f[:, 4 + h:5 + h], None, ALU.mult))
            step(dve.tensor_scalar(turns, ang, 1.0 / (2 * math.pi), ROUND, ALU.mult, ALU.add))
            step(dve.tensor_scalar(turns, turns, -ROUND, None, ALU.add))
            for c in TWO_PI_PARTS:
                step(dve.scalar_tensor_tensor(ang, turns, -c, ang, ALU.mult, ALU.add))
            step(dve.tensor_scalar(sin_a, ang, PI_BELOW, -PI_BELOW, ALU.min, ALU.max))
            step(dve.tensor_scalar(ang, ang, math.pi / 2, None, ALU.add))
            step(dve.tensor_scalar(tmp, ang, math.pi, -2 * math.pi, ALU.is_gt, ALU.mult))
            step(dve.tensor_tensor(ang, ang, tmp, ALU.add))
            dve.tensor_scalar(cos_a, ang, PI_BELOW, -PI_BELOW, ALU.min, ALU.max).then_inc(angle_ready, 1)
            lam_v = rows("diff_lambda").rearrange("p (a b d) -> p a b d", a=2, b=2)
            lam_t = posb[:, 2, 0:2 * DQK].rearrange("p (a d) -> p a d", a=2)
            step(dve.tensor_tensor(lam_t, lam_v[:, :, 0, :], lam_v[:, :, 1, :], ALU.mult))
            dve.tensor_reduce(lam_s, lam_t, AX, ALU.add).then_inc(lam_in, 1)

            step(dve.tensor_tensor(rows("mla_q_hnorm_w")[:, 0:NOPE], rows("mla_q_hnorm_w")[:, 0:NOPE],
                                   rows("mla_k_hnorm_w")[:, 0:NOPE], ALU.mult))

            for j in range(2):
                for kt in range(RT):
                    dve.wait_ge(cT_hi, RT * (j + 1))
                    w = VEC["mla_q_norm_w" if j == 0 else "mla_kv_norm_w"] + kt
                    dve.scalar_tensor_tensor(cT[1][:, j, kt, :], ps[:, 4 + j, kt * T:(kt + 1) * T], vec[:, w:w + 1],
                                             cT[0][:, j, kt, :].bitcast(F32), ALU.mult, ALU.subtract).then_inc(cT_lo, 1)
            evac("dq", (dq[:, 1, :], whole))
            evac("uq0", (q[:, 1, 0:768], whole))
            evac("uq1", (q[:, 1, 768:1536], whole))
            for i in range(2):
                heads = slice(i * HEADS // 2, (i + 1) * HEADS // 2)
                evac(f"ukv{i}", (kf[:, 1, :].rearrange("p (n d) -> p n d", d=QK)[:, heads, 0:NOPE],
                                 lambda src: src.rearrange("p (n d) -> p n d", d=128)[:, :, 0:NOPE]),
                     (v1[:, 1, :].rearrange("p (n d) -> p n d", d=VD)[:, heads, :],
                      lambda src: src.rearrange("p (n d) -> p n d", d=128)[:, :, NOPE:128]))

            def head_sums(n, src, out):
                dve.wait_ge(sq_ready, n + 1)
                dve.tensor_reduce(out, src, AX, ALU.add).then_inc(sq_read, 1)
                dve.wait_ge(sq_read, n + 1)

            def diff_sums(n):
                head_sums(n, sq.rearrange("p (n d) -> p n d", d=DQK), ss_d)

            def diff_norm(buf):
                v = buf.rearrange("p h (n d) -> p (h n) d", d=DQK)
                roots(ss_d, rstd_d, 2 * HEADS, DQK)
                dve.tensor_tensor(v, v, rstd_d.unsqueeze(2).to_broadcast([P, 2 * HEADS, DQK]), ALU.mult).then_inc(dqk_ready, 1)

            def rotate(x1, x2, cos, sin, t1, t2, third=None):
                if third in (None, 0):
                    step(dve.tensor_tensor(t1, x1, sin, ALU.mult))
                    step(dve.tensor_tensor(t2, x2, sin, ALU.mult))
                if third in (None, 1):
                    step(dve.tensor_tensor(x1, x1, cos, ALU.mult))
                    step(dve.tensor_tensor(x1, x1, t2, ALU.subtract))
                if third in (None, 2):
                    step(dve.tensor_tensor(x2, x2, cos, ALU.mult))
                    step(dve.tensor_tensor(x2, x2, t1, ALU.add))

            def rope(third):
                q4 = q.rearrange("p h (n d) -> p h n d", d=QK)
                full = [P, HALVES, HEADS, HR]
                rotate(q4[:, :, :, NOPE:NOPE + HR], q4[:, :, :, NOPE + HR:QK], cos_t.unsqueeze(2).to_broadcast(full),
                       sin_t.unsqueeze(2).to_broadcast(full), *rope_t, third=third)

            diff_sums(0)
            dve.wait_ge(lam_exp, 1)
            step(dve.tensor_scalar(lam, lam_s[:, 0:1], LAM_INIT, lam_s[:, 1:2], ALU.add, ALU.subtract))
            dve.wait_ge(trig_ready, 1)
            sin_t, cos_t = (trig[:, i, :].rearrange("p (h i) -> p h i", h=HALVES) for i in (4, 5))
            step(dve.tensor_tensor(kr, c_sb[:, :, 2 * RANK:C_COLS],
                                   rows("mla_k_hnorm_w")[:, NOPE:QK].unsqueeze(1).to_broadcast([P, HALVES, ROPE]), ALU.mult))
            rt = [trig[:, 0, :].rearrange("p (h i) -> p h i", h=HALVES), trig[:, 1, :].rearrange("p (h i) -> p h i", h=HALVES)]
            rotate(kr[:, :, 0:HR], kr[:, :, HR:ROPE], cos_t, sin_t, *rt)
            n_heads = HALVES * HEADS
            ss_q, ss_k, rstd_q, rstd_k = ss_h[:, 0:n_heads], ss_h[:, n_heads:], rstd_h[:, 0:n_heads], rstd_h[:, n_heads:]
            def query_sums(h):
                head_sums(1 + h, sq[:, 0:HEADS * QK].rearrange("p (n d) -> p n d", d=QK), ss_q[:, h * HEADS:(h + 1) * HEADS])

            query_sums(0)
            diff_norm(dq)
            query_sums(1)
            head_sums(3, sq.rearrange("p (n d) -> p n d", d=NOPE), ss_k)
            step(dve.tensor_tensor(ss_k.rearrange("p (h n) -> p h n", h=HALVES), ss_k.rearrange("p (h n) -> p h n", h=HALVES),
                                   ss_kr.unsqueeze(2).to_broadcast([P, HALVES, HEADS]), ALU.add))
            roots(ss_h, rstd_h, 2 * n_heads, QK)
            evac("dk", (dk[:, 1, :], whole))
            diff_sums(4)
            diff_norm(dk)
            qh = q.rearrange("p h (n d) -> p (h n) d", d=QK)
            step(dve.tensor_tensor(qh, qh, rstd_q.unsqueeze(2).to_broadcast([P, n_heads, QK]), ALU.mult))
            step(dve.tensor_tensor(qh, qh, rows("mla_q_hnorm_w").unsqueeze(1).to_broadcast([P, n_heads, QK]), ALU.mult))
            evac("dv", (dv[:, 1, :], whole))

            def gate_bias(name, g, h):
                dve.wait_ge(tile_used, done(name))
                dve.scalar_tensor_tensor(g[:, h, :], pset(SETS[name], h), rstd_0[:, h:h + 1], bgate,
                                         ALU.mult, ALU.add).then_inc(gate_in, 1)

            for i in range(1, DHEADS + 2):
                if i - 1 < DHEADS:
                    u = i - 1
                    s = diff_scores[u % 3]
                    dve.wait_ge(hS_done, u + 1)
                    if u >= 3:
                        dve.wait_ge(hP_done, u - 2)
                    for m in range(2):
                        dve.scalar_tensor_tensor(s[:, 2 * m:2 * m + 2, :].rearrange("p h k -> p (h k)"),
                                                 dist.rearrange("p h k -> p (h k)"), -2.0 ** (-8.0 * (u + 1) / DHEADS),
                                                 ps[:, 5 + m, :], ALU.mult, ALU.add).then_inc(hS_read, 1)
                    dve.wait_ge(hS_read, 2 * u + 2)
                    step(dve.tensor_reduce(mxn[u % 2], s, AX, ALU.max))
                    dve.tensor_scalar(mxn[u % 2], mxn[u % 2], -1.0, None, ALU.mult).then_inc(max_ready, 1)
                if i >= 2:
                    u = i - 2
                    s, r = diff_scores[u % 3], rec[u % 2]
                    dve.wait_ge(exp_done, u + 1)
                    step(dve.reciprocal(r, sums[u % 2]))
                    step(dve.tensor_scalar(r[:, 2:4], r[:, 2:4], lam, None, ALU.mult))
                    for h in range(HALVES):
                        dve.tensor_scalar(s[:, 2 + h, :], s[:, 2 + h, :], r[:, 2 + h:3 + h], None, ALU.mult).then_inc(dve_step, 1)
                        count[0] += 1
                    dve.wait_ge(dve_step, count[0])
                    for h in range(HALVES):
                        dve.scalar_tensor_tensor(s[:, h, :], s[:, h, :], r[:, h:h + 1], s[:, 2 + h, :], ALU.mult,
                                                 ALU.subtract).then_inc(prob_ready, 1)
                if i == 2:
                    rope(0)
                if i == 3:
                    rope(1)
                if i == 4:
                    rope(2)
                if i == 5 or i == 6:
                    kh = kf[:, i - 5, :].rearrange("p (n d) -> p n d", d=QK)[:, :, 0:NOPE]
                    r = rstd_k[:, (i - 5) * HEADS:(i - 4) * HEADS]
                    dve.tensor_tensor(kh, kh, r.unsqueeze(2).to_broadcast([P, HEADS, NOPE]), ALU.mult).then_inc(qk_ready, 1)
                if i == 7:
                    wide = [P, HALVES, HEADS, ROPE]
                    dve.tensor_tensor(kf.rearrange("p h (n d) -> p h n d", d=QK)[:, :, :, NOPE:QK],
                                      kr.unsqueeze(2).to_broadcast(wide),
                                      rstd_k.rearrange("p (h n) -> p h n", h=HALVES).unsqueeze(3).to_broadcast(wide),
                                      ALU.mult).then_inc(qk_ready, 1)
                if i >= DHEADS:
                    gate_bias("gate_a", ga, i - DHEADS)
            for i in range(1, HEADS + 3):
                if i >= 3:
                    step(dve.reciprocal(rec[(DHEADS + i - 3) % 2][:, 0:2], sums[(DHEADS + i - 3) % 2][:, 0:2]))
                if i - 1 < HEADS:
                    u = DHEADS + i - 1
                    dve.wait_ge(hS_done, u + 1)
                    if i >= 1:
                        dve.wait_ge(exp_done, u - 1)
                    step(dve.tensor_reduce(mxn[u % 2][:, 0:2], ps[:, 5, :].rearrange("p (h k) -> p h k", h=2), AX, ALU.max))
                    dve.tensor_scalar(mxn[u % 2][:, 0:2], mxn[u % 2][:, 0:2], -QK ** -0.5, None, ALU.mult).then_inc(max_ready, 1)
                if 0 <= i - 2 < HEADS:
                    u = DHEADS + i - 2
                    dve.wait_ge(hP_done, u + 1)
                    dve.wait_ge(hO_done, u - 1)
                    dve.tensor_copy(pt_sb[u % 2], ps[:, 6, :].rearrange("p (k t) -> p k t", k=2)).then_inc(hP_evac, 1)
                if 0 <= i - 3 < HEADS:
                    hd = i - 3
                    u = DHEADS + hd
                    r = rec[u % 2]
                    if hd == 0:
                        dve.wait_ge(gate_ready, 1)
                    if hd == HEADS - 1:
                        cols = slice(0, D // 2)
                        dve.wait_ge(od_ready, 1)
                        dve.wait_ge(gate_ready, 2)
                        step(dve.tensor_tensor(dq[:, :, cols], dq[:, :, cols], gb[:, :, cols], ALU.mult))
                    dve.wait_ge(hO_done, u + 1)
                    for h in range(HALVES):
                        g = ga[:, h, hd * VD:(hd + 1) * VD]
                        o = dve.scalar_tensor_tensor(g, ps[:, 7, h * VD:(h + 1) * VD], r[:, h:h + 1], g, ALU.mult, ALU.mult)
                    o.then_inc(hO_evac, 1)
                if i in (HEADS - 2, HEADS - 1):
                    dve.wait_ge(gate_bias_loaded, 16)
                    gate_bias("gate_b", gb, i - HEADS + 2)
                if i == 6:
                    dve.wait_ge(od_sums, HALVES)
                    step(dve.tensor_reduce(ss_o, sq.rearrange("p (n d) -> p n d", d=DV), AX, ALU.add))
                if i == 7:
                    roots(ss_o, rstd_o, 2 * DHEADS, DV, od_root)
            for i in range(2):
                c = slice(i * 512, (i + 1) * 512)
                dve.wait_ge(hO_evac, DHEADS + HEADS // 2 * (i + 1))
                if i:
                    dve.wait_ge(od_gated, 1)
                dve.tensor_tensor(ga[:, :, c], ga[:, :, c], dq[:, :, c], ALU.add).then_inc(merged_ready, 1)
            low_stage("merge", 0, None)

            def add_product(name):
                for h in range(HALVES):
                    half_complete(dve, name, h)
                    dve.tensor_tensor(xs[:, h, :], pset(SETS[name], h), xs[:, h, :], ALU.add).then_inc(x_ready, 1)

            add_product("out")
            for kt in (0, 1, 4, 5):
                dve.wait_ge(tr_done, 4 * TRANSPOSED.index("ffn") + kt // 2 + 1)
                dve.tensor_scalar(hT_f[:, kt, :], ps[:, kt // 2, (kt % 2) * T:(kt % 2 + 1) * T],
                                  vec[:, VEC["ffn_norm_w"] + kt:VEC["ffn_norm_w"] + kt + 1], None, ALU.mult).then_inc(router_dve, 1)
            norm(1, scaled=False, squared=True)
            work, sel, eq, cum, zero = (routing[:, i, :] for i in range(5))
            dve.wait_ge(logit_done, 1)
            lp = ps[:, 4, 0:HALVES * EXPERTS].rearrange("p (h e) -> p h e", h=HALVES)
            for h in range(HALVES):
                dve.tensor_scalar(logit[:, h, :], lp[:, h, :], rstd_x[:, h:h + 1], None, ALU.mult).then_inc(dve_step, 1)
                count[0] += 1
            dve.wait_ge(dve_step, count[0])
            step(dve.tensor_reduce(rmax, logit, AX, ALU.max))
            dve.tensor_scalar(rmax, rmax, -1.0, None, ALU.mult).then_inc(rmax_ready, 1)
            dve.tensor_scalar(xn[:, 1, :], xs[:, 1, :], rstd_x[:, 1:2], None, ALU.mult).then_inc(xn_dve, 1)
            step(dve.memset(zero, 0.0))
            dve.wait_ge(rexp_done, 1)
            step(dve.reciprocal(rinv, rsum))
            for h in range(HALVES):
                dve.tensor_scalar(aff[:, h, :], logit[:, h, :], rinv[:, h:h + 1], None, ALU.mult).then_inc(aff_ready, 1)
            dve.wait_ge(affT_done, 1)
            r0 = ps[0:EXPERTS, 5, 0:T]
            src = r0
            for k in range(CAP // 8):
                step(dve.max(top8[:, k, :], src))
                if k + 1 < CAP // 8:
                    step(dve.match_replace(work, top8[:, k, :], src, -1.0))
                    src = work
            least = top8[:, CAP // 8 - 1, 7:8]
            step(dve.tensor_scalar(sel, r0, least, None, ALU.is_gt, ALU.add, accum_out=rcount[:, 0:1]))
            step(dve.tensor_scalar(rcount[:, 1:2], rcount[:, 0:1], -1.0, float(CAP), ALU.mult, ALU.add))
            step(dve.tensor_scalar(eq, r0, least, None, ALU.is_equal))
            step(dve.tensor_tensor_scan(cum, eq, zero, 0.0, ALU.add, ALU.add))
            step(dve.scalar_tensor_tensor(eq, cum, rcount[:, 1:2], eq, ALU.is_le, ALU.mult))
            step(dve.tensor_tensor(sel, sel, eq, ALU.add))
            step(dve.tensor_tensor_scan(cum, sel, zero, 0.0, ALU.add, ALU.add))
            dve.tensor_tensor(cum, cum, sel, ALU.mult).then_inc(slot_done, 1)
            dve.wait_ge(slotT_done, 1)
            step(dve.tensor_copy(slot_t, ps[:, 6, 0:HALVES * EXPERTS].rearrange("p (h e) -> p h e", h=HALVES)))

            dve.sem_inc(hid_ready, 1)
            dve.sem_inc(moe_added, 4)
            with dve.Fori(0, EXPERTS // PAIR) as pair_i:
                for j_e in range(PAIR):
                    e = pair_i * PAIR + j_e
                    for h in range(HALVES):
                        dve.tensor_scalar(onehot[:, h, :], slot_ids[:, 0:CAP], slot_t[:, h, bass.ds(e, 1)], None,
                                          ALU.is_equal).then_inc(onehot_ready, 1)
                    dve.wait_ge(scat_done, e + 1)
                    for h in range(HALVES):
                        dve.tensor_scalar(gated[:, h, :], slot_ids[:, :], slot_t[:, h, bass.ds(e, 1)], aff[:, h, bass.ds(e, 1)],
                                          ALU.is_equal, ALU.mult).then_inc(gated_ready, 1)
                    dve.wait_ge(gather_done, e + 1)
                    w = vec[:, VEC["ffn_norm_w"]:VEC["ffn_norm_w"] + KT].unsqueeze(2).to_broadcast([P, KT, CAP])
                    dve.tensor_tensor(xe, ps[:, 1, 0:KT * CAP].rearrange("p (k s) -> p k s", k=KT), w, ALU.mult).then_inc(xe_ready, 1)
                    dve.wait_ge(silu_done, e + 1)
                    dve.wait_ge(chunk_used, EXPERT_CHUNKS * e + SLOTS + 2 * KT)
                    dve.wait_ge(hidT_done, e + 1)
                    dve.tensor_tensor(hid, hid_g, ps[:, 1, :], ALU.mult).then_inc(hid_ready, 1)
                    dve.wait_ge(e_scatter, e + 2)
                    for j in range(4):
                        xv = xs[:, :, j * DCOL:(j + 1) * DCOL]
                        dve.tensor_tensor(xv, ps[:, 4 + j, :].rearrange("p (h d) -> p h d", h=HALVES), xv, ALU.add
                                          ).then_inc(moe_added, 1)

            low_stage("mix", 0, "norm1_g_2")
            dve.wait_ge(moe_added, 4 * EXPERTS + 4)
            norm(2, scaled=False)
            for h in range(HALVES):
                dve.tensor_scalar(diag[:, h * P:(h + 1) * P], ident[:, :], rstd_x[:, h:h + 1], None, ALU.mult).then_inc(diag_ready, 1)
            step(dve.scalar_tensor_tensor(rows("q_norm_g_2"), rows("q_norm_g_2"), SHD ** -0.5, rows("k_norm_g_2"), ALU.mult, ALU.mult))
            step(dve.memset(conv[:, :, 0:CONVW - 1], 0.0))
            evac("qk2", (qk2[:, 1, :], whole))
            head_sums(5, sq.rearrange("p (n d) -> p n d", d=SHD), ss_d)
            roots(ss_d, rstd_d, 4 * SHEADS, SHD)
            v = qk2.rearrange("p h (n d) -> p (h n) d", d=SHD)
            step(dve.tensor_tensor(v, v, rstd_d.unsqueeze(2).to_broadcast([P, 4 * SHEADS, SHD]), ALU.mult))
            v = qk2.rearrange("p h (n d) -> p h n d", d=SHD)[:, :, 0:SHEADS, :]
            w = rows("q_norm_g_2").unsqueeze(1).unsqueeze(1).to_broadcast([P, HALVES, SHEADS, SHD])
            dve.tensor_tensor(v, v, w, ALU.mult).then_inc(qk2_ready, 1)
            dve.wait_ge(tile_used, done("v2"))
            for h in range(HALVES):
                dve.tensor_scalar(v2[:, h, :], pset(SETS["v2"], h, SATT), rstd_x[:, h:h + 1], None, ALU.mult).then_inc(v_ready, 1)
            dve.wait_ge(row_done, 1)
            dve.tensor_copy(root_row, ps[:, 1, 0:T]).then_inc(row_read, 1)
            dve.wait_ge(row_read, 1)

            def gating_norm():
                head_sums(6, sq[:, 0:HALVES * SGU].rearrange("p (n d) -> p n d", d=SGU // SG), ss_d[:, 0:2 * SG])
                roots(ss_d[:, 0:2 * SG], rstd_d[:, 0:2 * SG], 2 * SG, SGU // SG)
                v = cv2.rearrange("p h (n d) -> p (h n) d", d=SGU // SG)
                step(dve.tensor_tensor(v, v, rstd_d[:, 0:2 * SG].unsqueeze(2).to_broadcast([P, 2 * SG, SGU // SG]), ALU.mult))
                dve.tensor_tensor(cv2, cv2, rows("sgu_norm_g_2").unsqueeze(1).to_broadcast([P, HALVES, SGU]),
                                  ALU.mult).then_inc(cv_ready, 1)

            def gated_unit():
                dve.wait_ge(sv_done, 1)
                for g in range(SG):
                    w = SGU // SG
                    s = ps[:, 1, :].rearrange("p (h d) -> p h d", h=HALVES)[:, :, g * w:(g + 1) * w]
                    b = vec[:, VEC["sgu_b_2"] + g:VEC["sgu_b_2"] + g + 1]
                    dve.scalar_tensor_tensor(yc[:, :, g * w:(g + 1) * w], s, b, u2[:, :, g * w:(g + 1) * w], ALU.add,
                                             ALU.mult).then_inc(yc_ready, 1)

            def split_y(src, k, ready):
                step(dve.tensor_copy(yT[0][:, k:k + 1, :], src))
                dve.tensor_tensor(yT[1][:, k:k + 1, :], src, yT[0][:, k:k + 1, :].bitcast(F32), ALU.subtract).then_inc(ready, 1)

            def conv_inputs():
                r2 = root_row.unsqueeze(1).to_broadcast([P, 2, T])
                dve.wait_ge(tile_used, done("conv"))
                a_b, a_c, a_h = (ps[:, b, :].rearrange("p (c t) -> p c t", c=2) for b in range(3))
                step(dve.tensor_tensor(a_hT, a_h, r2, ALU.mult))
                step(dve.tensor_tensor(conv[:, :, CONVW - 1:], a_c, a_hT, ALU.mult))
                step(dve.tensor_tensor(a_bT, a_b, r2, ALU.mult))
                dve.sem_inc(conv_read, 1)
                step(dve.tensor_tensor(conv[:, :, CONVW - 1:], conv[:, :, CONVW - 1:], r2, ALU.mult))

            def convolution(ct):
                if ct:
                    dve.wait_ge(y_conv, ct)
                w = [vec[:, VEC["conv_w_2"] + 2 * j + ct:VEC["conv_w_2"] + 2 * j + ct + 1] for j in range(CONVW)]
                step(dve.tensor_scalar(conv_y, conv[:, ct, 0:T], w[0], None, ALU.mult))
                for j in range(1, CONVW):
                    step(dve.scalar_tensor_tensor(conv_y, conv[:, ct, j:j + T], w[j], conv_y, ALU.mult, ALU.add))
                step(dve.tensor_tensor(conv_y, conv_y, a_bT[:, ct, :], ALU.mult))
                split_y(conv_y.unsqueeze(1), ct, y_conv)

            def diagonal(buf):
                return buf.rearrange("p m (c t) -> p m c t", t=P)[:, :, 0:3:2, :]

            causal = tri[:, :].unsqueeze(1).unsqueeze(1).to_broadcast([P, 2, 2, P])
            z, suffix = ps[:, 4:6, 0:SC], ps[:, 6:8, 0:SC]
            for p in range(SHEADS // 2 + 1):
                if p == 2:
                    conv_inputs()
                if p >= 1:
                    b = lb[(p - 1) % 2]
                    dve.wait_ge(suf_done, p)
                    dve.tensor_tensor(b, suffix, b, ALU.add).then_inc(arg_ready, 1)
                    dve.wait_ge(w_exp, p)
                    dve.tensor_tensor(diagonal(b), diagonal(b), causal, ALU.mult).then_inc(w_ready, 1)
                if p < SHEADS // 2:
                    dve.wait_ge(sp_ready, p + 1)
                    if p >= 2:
                        dve.wait_ge(yb_done, p - 1)
                    step(dve.scalar_tensor_tensor(lb[p % 2], z, 0.0, spl, ALU.min, ALU.subtract))
                    if p >= 1:
                        dve.wait_ge(suf_done, p)
                    step(dve.tensor_tensor(lr, lb[p % 2], z, ALU.subtract))
                    dve.tensor_tensor(diagonal(lr), diagonal(lr), causal, ALU.mult).then_inc(lr_ready, 1)
                if 2 <= p < 4:
                    convolution(p - 2)
                if p == SHEADS // 2:
                    gating_norm()
                if p >= 1:
                    dve.wait_ge(yb_done, p)
                    split_y(ps[:, 3, 0:T].unsqueeze(1), 1 + p, y_pair)
            gated_unit()
            dve.wait_ge(ycT_hi, 1)
            dve.tensor_tensor(yT[1][:, 6:8, :], ps[:, 0, :].rearrange("p (c t) -> p c t", c=2),
                              yT[0][:, 6:8, :].bitcast(F32), ALU.subtract).then_inc(y_gate, 1)
            add_product("out2")
            dve.wait_ge(tile_used, done("proj"))
            dve.tensor_copy(pe_sb[:, 1, :], pset(SETS["proj"], 1)).then_inc(proj_out, 1)
            low_stage("ff", 4, "norm2_g_2")
            dve.wait_ge(x_ready, 4)
            norm(3, scaled=False)
            step(dve.tensor_tensor(rstd_2, rstd_x, rstd_x, ALU.mult))
            for k in range(4 * 4):
                dve.wait_ge(f_relu, k + 1)
                step(dve.tensor_tensor(f_2, f_r[k % 2], f_r[k % 2], ALU.mult))
                dve.wait_ge(f_hi, k + 1)
                lo = fT[1][:, 2 * k:2 * k + 2, :]
                dve.tensor_tensor(lo, f_2.rearrange("p (c t) -> p c t", c=2), fT[0][:, 2 * k:2 * k + 2, :].bitcast(F32),
                                  ALU.subtract).then_inc(f_ready, 1)
                dve.wait_ge(f_ready, k + 1)
            for h in range(HALVES):
                half_complete(dve, "down", h)
                dve.scalar_tensor_tensor(xs[:, h, :], pset(SETS["down"], h), rstd_2[:, h:h + 1], xs[:, h, :], ALU.mult,
                                         ALU.add).then_inc(x_ready, 1)
            low_stage("ple", 4, "norm3_g_2")
            dve.wait_ge(x_ready, 6)
            norm(4, scaled=False)
            dve.wait_ge(proj_out, 2)
            for h in range(HALVES):
                cols = slice(0, D if h == 0 else D // 2)
                dve.wait_ge(gate2_ready, h + 1)
                step(dve.tensor_tensor(gate2[:, h, cols], pe_sb[:, h, cols], gate2[:, h, cols], ALU.mult))
                dve.tensor_tensor(gate2[:, h, cols], xs[:, h, cols], gate2[:, h, cols], ALU.add).then_inc(out_ready, 1)

        @block.tensor
        def _(pe):
            def mixed(kt):
                return (y_conv, kt + 1) if kt < 2 else (y_pair, kt - 1) if kt < 6 else (y_gate, 1)

            def transpose_bank(src, base, b, halves):
                for h in halves:
                    for kt in (2 * b, 2 * b + 1):
                        m = pe.transpose(ps[:, base + b, (kt % 2) * T + h * P:(kt % 2) * T + (h + 1) * P],
                                         src[:, h, kt * P:(kt + 1) * P], ident[:, :])
                return m

            def transposes(s, src, base, ready=None):
                for h in range(HALVES):
                    if ready is not None:
                        ready(h)
                    for b in range(4):
                        m = transpose_bank(src, base, b, [h])
                        if h == HALVES - 1:
                            m.then_inc(tr_done, 1)

            def stage_ready(s, kt=KT - 1):
                pe.wait_ge(lo_ready, KT * STAGES.index(s) + kt + 1)

            def tiles(name, left, kts=None, piece=None, ready=None):
                parts = list(enumerate(pieces(name)))
                chosen = parts if piece is None else parts[piece:piece + 1]

                def high_pass(h, part):
                    for j, (c0, width) in chosen:
                        pe.matmul(pset(SETS[name], h)[:, j * 512:j * 512 + width], left[part][:, kt, h * P:(h + 1) * P],
                                  w[:, 0, c0:c0 + width], start=first and part == 0, stop=False)

                def low_pass(h):
                    for j, (c0, width) in chosen:
                        m = pe.matmul(pset(SETS[name], h)[:, j * 512:j * 512 + width], left[0][:, kt, h * P:(h + 1) * P],
                                      w[:, 1, c0:c0 + width], start=False, stop=last)
                    return m

                for kt in kts if kts is not None else range(TILES[name]):
                    n = TILE0[name] + kt
                    w = w_split[:, n % WBUFS]
                    first, last = kt == 0, kt == TILES[name] - 1
                    if ready is not None:
                        ready(kt)
                    pe.wait_ge(split_hi, n + 1)
                    if last and name in HALVES_APART:
                        pe.wait_ge(split_lo, n + 1)
                        for h in range(HALVES):
                            high_pass(h, 0)
                            high_pass(h, 1)
                            m = low_pass(h)
                            if h == 0:
                                m.then_inc(half_done, 1)
                    else:
                        for part in (0, 1):
                            for h in range(HALVES):
                                high_pass(h, part)
                        pe.wait_ge(split_lo, n + 1)
                        for h in range(HALVES):
                            m = low_pass(h)
                    if chosen[-1] == parts[-1]:
                        m.then_inc(tile_used, 1)

            def tiles_T(name, kts=None, ready=None):
                for kt in kts if kts is not None else range(TILES[name]):
                    n = TILE0[name] + kt
                    w = w_split[:, n % WBUFS]
                    first, last = kt == 0, kt == TILES[name] - 1
                    if ready is not None:
                        ready(kt)

                    def pass_T(ct, part_w, left, start, stop):
                        return pe.matmul(ps[:, SET[SETS[name]] + ct // 2, (ct % 2) * T:(ct % 2 + 1) * T],
                                         w[:, part_w, ct * P:(ct + 1) * P], left[:, kt, :], start=start, stop=stop,
                                         skip_group_check=True)

                    pe.wait_ge(split_hi, n + 1)
                    for ct in range(COLS[name] // P):
                        pass_T(ct, 0, hT_hi, first and ct % 2 == 0, False)
                        pass_T(ct, 0, hT_lo, False, False)
                    pe.wait_ge(split_lo, n + 1)
                    for ct in range(COLS[name] // P):
                        m = pass_T(ct, 1, hT_hi, False, last)
                    m.then_inc(tile_used, 1)

            hT = (hT_hi, hT_lo)

            def keep_clock(bank, n):
                for _ in range(n):
                    pe.matmul(ps[:, bank, 0:P], ident[:, :], ident[:, :], start=True, stop=True)

            def out_of_psum(name):
                pe.wait_ge(block_act, evacuated(name))
                pe.wait_ge(block_dve, evacuated(name))

            pe.wait_ge(masks_ready, 1)
            keep_clock(7, WARM_START)
            pe.wait_ge(x_loaded, 16)
            transposes("attn", xs, 0)
            pe.wait_ge(norm_w_loaded, 16)
            pe.transpose(ps[:, 4, 0:KT], vec_rows[0:KT, :], ident[0:KT, 0:KT]).then_inc(vec_done, 1)

            pe.wait_ge(vec_ready, 1)
            tiles("c", hT, ready=lambda kt: stage_ready("attn", kt))
            pe.wait_ge(vec_loaded, 16 * N_VEC)
            pe.transpose(ps[:, 0, 0:NVEC], vec_rows[:, :], ident[0:NVEC, 0:NVEC]).then_inc(vec_done, 1)
            pe.wait_ge(vec_ready, 2)
            tiles("dq", hT, range(0, 6))
            pe.wait_ge(c_norm, 4)
            out_of_psum("c")
            for j in range(2):
                for kt in range(RT):
                    for h in range(HALVES):
                        c0 = j * RANK + kt * P
                        m = pe.transpose(ps[:, 4 + j, kt * T + h * P:kt * T + (h + 1) * P], c_sb[:, h, c0:c0 + P], ident[:, :])
                m.then_inc(cT_done, 1)
            tiles("dq", hT, range(6, KT))
            pe.wait_ge(cT_lo, 2 * RT)
            tiles("uq0", [c[:, 0] for c in cT])
            out_of_psum("dq")
            tiles("uq1", [c[:, 0] for c in cT])
            out_of_psum("uq0")
            tiles("ukv0", [c[:, 1] for c in cT])
            out_of_psum("uq1")
            tiles("ukv1", [c[:, 1] for c in cT])
            out_of_psum("ukv0")
            tiles("dk", hT)
            out_of_psum("ukv1")
            tiles("dv", hT, range(0, KT - 1))

            def diff_probs(u):
                pe.wait_ge(prob_ready, 2 * u + 2)
                if u >= 1:
                    pe.wait_ge(hP_evac, u)
                for kb in range(2):
                    for h in range(HALVES):
                        m = pe.transpose(ps[:, 7, kb * T + h * P:kb * T + (h + 1) * P],
                                         diff_scores[u % 3][:, h, kb * P:(kb + 1) * P], ident[:, :])
                m.then_inc(hP_done, 1)

            def diff_output(u, transposed):
                pe.wait_ge(hP_evac, u + 1)
                pe.wait_ge(hT_evac, transposed)
                if u >= 1:
                    pe.wait_ge(hO_evac, u)
                for h in range(HALVES):
                    for kb in range(2):
                        m = pe.matmul(ps[:, 4, h * P:(h + 1) * P], pt_sb[u % 2][:, kb, h * P:(h + 1) * P],
                                      dv[:, kb, u * DV:(u + 1) * DV], start=kb == 0, stop=kb == 1)
                m.then_inc(hO_done, 1)

            def diff_transposes(u):
                if u >= 1:
                    pe.wait_ge(hT_evac, u)
                if u >= 5:
                    pe.wait_ge(hO_evac, u - 4)
                for j, buf in enumerate((dq, dk)):
                    for h in range(HALVES):
                        m = pe.transpose(ps[:, 4, j * T + h * P:j * T + (h + 1) * P], buf[:, h, u * P:(u + 1) * P], ident[:, :])
                m.then_inc(hT_done, 1)

            pe.wait_ge(dqk_ready, 2)
            out_of_psum("dk")
            diff_transposes(0)
            tiles("dv", hT, [KT - 1])
            for i in range(1, DHEADS + 1):
                u = i - 1
                pe.wait_ge(hT_evac, u + 1)
                if u >= 1:
                    pe.wait_ge(hS_read, 2 * u)
                for h in range(HALVES):
                    for mp in range(2):
                        r = slice(DQK * mp, DQK * (mp + 1))
                        m = pe.matmul(ps[:, 5 + mp, h * T:(h + 1) * T], qkT[u % 2][r, h * P:(h + 1) * P],
                                      qkT[u % 2][r, T:2 * T], start=True, stop=True)
                m.then_inc(hS_done, 1)
                if i < DHEADS:
                    diff_transposes(i)
                if i == 1:
                    out_of_psum("dv")
                tiles("gate_a", hT, [i - 1])
                if i >= 3:
                    diff_probs(i - 3)
                if i >= 4:
                    diff_output(i - 4, min(i + 1, DHEADS))
            gate_b_halves = {1: (0, 1), 2: (2, 3), 3: (4, 5), **{i: (i + 2,) for i in range(4, 2 * KT - 2)}}
            pe.wait_ge(qk_ready, 3)
            for i in range(HEADS + 3):
                if i < HEADS:
                    u = DHEADS + i
                    pe.wait_ge(hT_evac, u)
                    if i <= 3:
                        pe.wait_ge(hO_evac, DHEADS - 3 + i)
                    for j, buf in enumerate((q, kf)):
                        for h in range(HALVES):
                            m = pe.transpose(ps[0:QK, 4, j * T + h * P:j * T + (h + 1) * P], buf[:, h, i * QK:(i + 1) * QK], ident[:, :])
                    m.then_inc(hT_done, 1)
                if i == 3:
                    pe.wait_ge(hO_done, DHEADS)
                    pe.sem_inc(chunk_used, 2)
                if 0 <= i - 1 < HEADS:
                    u = DHEADS + i - 1
                    pe.wait_ge(hT_evac, u + 1)
                    pe.wait_ge(exp_done, u)
                    for h in range(HALVES):
                        m = pe.matmul(ps[:, 5, h * T:(h + 1) * T], qkT[u % 2][0:QK, h * P:(h + 1) * P],
                                      qkT[u % 2][0:QK, T:2 * T], start=True, stop=True)
                    m.then_inc(hS_done, 1)
                for k in gate_b_halves.get(i, ()):
                    pe.wait_ge(gate_in, 2)
                    tiles("gate_b", hT, [k // 2], k % 2)
                    if k == 2 * KT - 1:
                        pe.sem_inc(chunk_used, 1)
                if i < 2:
                    diff_probs(DHEADS - 2 + i)
                if 0 <= i - 2 < HEADS:
                    u = DHEADS + i - 2
                    pe.wait_ge(exp_done, u + 1)
                    pe.wait_ge(hP_evac, u)
                    for kb in range(2):
                        for h in range(HALVES):
                            m = pe.transpose(ps[:, 6, kb * T + h * P:kb * T + (h + 1) * P], scores[u % 2][:, h, kb * P:(kb + 1) * P], ident[:, :])
                    m.then_inc(hP_done, 1)
                if i < 3:
                    diff_output(DHEADS - 3 + i, DHEADS + i + 1)
                if 0 <= i - 3 < HEADS:
                    hd = i - 3
                    u = DHEADS + hd
                    pe.wait_ge(hP_evac, u + 1)
                    pe.wait_ge(hO_evac, u)
                    for h in range(HALVES):
                        for kb in range(2):
                            m = pe.matmul(ps[:, 7, h * VD:(h + 1) * VD], pt_sb[u % 2][:, kb, h * P:(h + 1) * P],
                                          v1[:, kb, hd * VD:(hd + 1) * VD], start=kb == 0, stop=kb == 1)
                    m.then_inc(hO_done, 1)

            pe.wait_ge(gate_in, 4)
            keep_clock(3, WARM_MERGE)
            for kt in range(KT):
                pe.wait_ge(merged_ready, 1 if kt < KT // 2 else 2)
                for h in range(HALVES):
                    m = pe.transpose(ps[:, kt // 2, (kt % 2) * T + h * P:(kt % 2) * T + (h + 1) * P],
                                     ga[:, h, kt * P:(kt + 1) * P], ident[:, :])
                if kt % 2:
                    m.then_inc(tr_done, 1)
            pe.wait_ge(hO_done, DHEADS + HEADS)
            pe.sem_inc(chunk_used, 4)
            pe.wait_ge(tr_done, 4 * TRANSPOSED.index("merge") + 4)
            pe.sem_inc(chunk_used, 2)
            pe.wait_ge(hO_evac, DHEADS + HEADS)
            for c in range(KT // 2):
                tiles("out", hT, [2 * c, 2 * c + 1], ready=lambda kt: stage_ready("merge", kt))
                pe.sem_inc(chunk_used, 1)
            pe.wait_ge(tile_used, done("out"))
            pe.sem_inc(chunk_used, WBUFS)
            transposes("ffn", xs, 0, ready=lambda h: pe.wait_ge(x_ready, 1 + h))
            keep_clock(7, WARM_ROUTER)
            pe.wait_ge(router_act, KT // 2)
            pe.wait_ge(router_dve, KT // 2)
            for h in range(HALVES):
                for kt in range(KT):
                    m = pe.matmul(ps[:, 4, h * EXPERTS:(h + 1) * EXPERTS], hT_f[:, kt, h * P:(h + 1) * P], router[:, kt, :],
                                  start=kt == 0, stop=kt == KT - 1)
            m.then_inc(logit_done, 1)
            keep_clock(7, WARM_SOFTMAX)
            pe.wait_ge(aff_ready, 2)
            for h in range(HALVES):
                m = pe.transpose(ps[0:EXPERTS, 5, h * P:(h + 1) * P], aff[:, h, :], ident[:, :])
            m.then_inc(affT_done, 1)
            pe.wait_ge(late_loaded, 32)
            for g in range(SG):
                m = pe.transpose(ps[:, 0, g * P:(g + 1) * P], sgu_in[:, g, :], ident[:, :])
            m.then_inc(pw_done, 1)
            for kt in range(PLE // P):
                for h in range(HALVES):
                    m = pe.transpose(ps[:, 1, kt * T + h * P:kt * T + (h + 1) * P], p_in[:, h, kt * P:(kt + 1) * P], ident[:, :])
            m.then_inc(pw_done, 1)
            keep_clock(7, WARM_CHOICE)
            pe.wait_ge(slot_done, 1)
            for h in range(HALVES):
                m = pe.transpose(ps[:, 6, h * EXPERTS:(h + 1) * EXPERTS], routing[:, 3, h * P:(h + 1) * P], ident[0:EXPERTS, 0:EXPERTS])
            m.then_inc(slotT_done, 1)
            keep_clock(7, WARM_GATHER)
            pe.wait_ge(xn_lo_ready, HALVES)
            pe.wait_ge(pw_raw, 3)

            for s in (scat_done, hidT_done, e_scatter):
                pe.sem_inc(s, 1)
            with pe.Fori(0, EXPERTS // PAIR) as pair_i:
                for j_e in range(PAIR):
                    e = pair_i * PAIR + j_e
                    def chunk_wait(k):
                            pe.wait_ge(slot_loaded[expert_slot(j_e, k)],
                                       16 * (PAIR * EXPERT_CHUNKS // SLOTS) * pair_i + expert_landed(j_e, k))

                    pe.wait_ge(onehot_ready, 2 * e + 2)
                    pe.wait_ge(hid_ready, e + 1)
                    for kt in range(KT):
                        for h in range(HALVES):
                            for part, src in enumerate((xn_hi, xn_lo)):
                                m = pe.matmul(ps[:, 1, kt * CAP:(kt + 1) * CAP], src[:, h, kt * P:(kt + 1) * P], onehot[:, h, :],
                                              start=h == 0 and part == 0, stop=h == HALVES - 1 and part == 1)
                    m.then_inc(gather_done, 1)
                    pe.wait_ge(gated_ready, 2 * e + 2)
                    pe.wait_ge(ye_ready, e + 1)
                    for h in range(HALVES):
                        m = pe.transpose(ps[:, 3, 256 + h * P:256 + (h + 1) * P], gated[:, h, :], ident[:, :])
                    m.then_inc(scat_done, 1)
                    pe.wait_ge(xe_ready, e + 1)
                    for bank in range(2):
                        for kt in range(KT):
                            chunk_wait(bank * KT + kt)
                            w = slot_buf(expert_slot(j_e, bank * KT + kt))
                            for j in range(4):
                                m = pe.matmul(ps[j * CAP:(j + 1) * CAP, bank, :], xe[:, kt, :], w[:, j * FCOL:(j + 1) * FCOL],
                                              start=kt == 0, stop=kt == KT - 1, skip_group_check=True)
                            m.then_inc(chunk_used, 1)
                    pe.wait_ge(hid_ready, e + 2)
                    for c in range(4):
                        m = pe.transpose(ps[:, 2, c * P:(c + 1) * P], hid[:, c * P:(c + 1) * P], ident[:, :])
                    m.then_inc(hidT_done, 1)
                    pe.wait_ge(scat_ready, e + 1)
                    pe.wait_ge(hidT_ready, e + 1)
                    for c in range(KT):
                        if j_e == PAIR - 1 and c >= KT - 3:
                            keep_clock(0, WARM_LAST)
                        chunk_wait(2 * KT + c)
                        w = slot_view(expert_slot(j_e, 2 * KT + c), D)
                        for k in range(2):
                            ft = 2 * c + k
                            for j in range(4):
                                m = pe.matmul(ps[j * CAP:(j + 1) * CAP, 3, 0:DCOL], hidT[:, ft % 4, (ft // 4) * CAP:(ft // 4 + 1) * CAP],
                                              w[:, k, j * DCOL:(j + 1) * DCOL], start=ft == 0, stop=ft == FF // P - 1, skip_group_check=True)
                        m.then_inc(chunk_used, 1)
                    pe.wait_ge(ye_ready, e + 2)
                    pe.wait_ge(moe_added, 4 * e + 4)
                    for h in range(HALVES):
                        for j in range(4):
                            m = pe.matmul(ps[:, 4 + j, h * DCOL:(h + 1) * DCOL], scat[j * CAP:(j + 1) * CAP, h * P:(h + 1) * P],
                                          ye[j * CAP:(j + 1) * CAP, :], start=True, stop=True)
                    m.then_inc(e_scatter, 1)

            keep_clock(0, WARM_MIX)
            for b in range(4):
                pe.wait_ge(moe_added, 4 * EXPERTS + b + 1)
                transpose_bank(xs, 0, b, range(HALVES)).then_inc(tr_done, 1)
            tiles("qk2", hT, ready=lambda kt: stage_ready("mix", kt))
            stage_ready("mix")
            tiles("v2", hT)
            pe.wait_ge(diag_ready, HALVES)
            pe.matmul(ps[:, 1, 0:T], ones[:, :], diag, start=True, stop=True).then_inc(row_done, 1)
            pe.wait_ge(qk2_ready, 1)
            out_of_psum("qk2")
            for j in range(SATT // P):
                for i in range(2):
                    for h in range(HALVES):
                        m = pe.transpose(ps[:, 4 + j, i * T + h * P:i * T + (h + 1) * P],
                                         qk2[:, h, i * SATT + j * P:i * SATT + (j + 1) * P], ident[:, :])
                m.then_inc(qkT2_done, 1)
            pe.wait_ge(v_ready, 2)
            pe.wait_ge(row_read, 1)
            pe.wait_ge(qkT2_evac, SATT // P)
            for p in range(SHEADS // 2 + 1):
                if p < SHEADS // 2:
                    if p >= 1:
                        pe.wait_ge(lr_ready, p)
                    for m in range(2):
                        r = slice(SHD * m, SHD * (m + 1))
                        pe.matmul(ps[:, 4 + m, 0:T], qkT2[r, p, T:T + P], qkT2[r, p, 0:T], start=True, stop=True)
                        last = pe.matmul(ps[:, 4 + m, T:SC], qkT2[r, p, T + P:2 * T], qkT2[r, p, P:T], start=True, stop=True)
                    last.then_inc(z_done, 1)
                if p == SHEADS // 2:
                    keep_clock(1, WARM_PAIR)
                if p >= 1:
                    pe.wait_ge(lr_ready, p)
                    if p >= 2:
                        pe.wait_ge(arg_ready, p - 1)
                    for m in range(2):
                        pe.matmul(ps[:, 6 + m, 0:SC], later[:, :], lr[:, m, :], start=True, stop=False)
                        last = pe.matmul(ps[:, 6 + m, P:T], ones[:, :], lr[:, m, T:SC], start=False, stop=True)
                    last.then_inc(suf_done, 1)
                if p < 2:
                    tiles_T("conv", range(4 * p, 4 * p + 4))
                elif p < 4:
                    if p == 2:
                        pe.wait_ge(conv_read, 1)
                    tiles("cuv", hT, range(4 * p - 8, 4 * p - 4))
                else:
                    pe.wait_ge(arg_ready, p)
                    tiles("out2", yT, range(0, 4), ready=lambda kt: pe.wait_ge(*mixed(kt)))
                if p >= 1:
                    pe.wait_ge(w_ready, p)
                    if p >= 2:
                        pe.wait_ge(y_pair, p - 1)
                    for m in range(2):
                        u = 2 * (p - 1) + m
                        r = slice(SHD * m, SHD * (m + 1))
                        w = lb[(p - 1) % 2][:, m, :]
                        pe.matmul(ps[r, 3, 0:T], v2[:, 0, u * SHD:(u + 1) * SHD], w[:, 0:T], start=True, stop=False,
                                  skip_group_check=True)
                        last = pe.matmul(ps[r, 3, P:T], v2[:, 1, u * SHD:(u + 1) * SHD], w[:, T:SC], start=False, stop=True,
                                         skip_group_check=True)
                    last.then_inc(yb_done, 1)
            pe.wait_ge(cv_ready, 1)
            pe.wait_ge(gelu_done, 4)
            for h in range(HALVES):
                for g in range(SG):
                    w = SGU // SG
                    m = pe.matmul(ps[:, 1, h * SGU + g * w:h * SGU + (g + 1) * w], wsT[:, g, :], cv2[:, h, g * w:(g + 1) * w],
                                  start=True, stop=True)
            m.then_inc(sv_done, 1)
            tiles("out2", yT, [4], ready=lambda kt: pe.wait_ge(*mixed(kt)))
            pe.wait_ge(yc_ready, SG)
            for kt in range(SGU // P):
                for h in range(HALVES):
                    m = pe.transpose(ps[:, 0, kt * T + h * P:kt * T + (h + 1) * P], yc[:, h, kt * P:(kt + 1) * P], ident[:, :])
            m.then_inc(ycT_done, 1)
            tiles("out2", yT, range(5, KT), ready=lambda kt: pe.wait_ge(*mixed(kt)))
            pe.wait_ge(pw_ready, 1)
            tiles("proj", pT)
            transposes("ff", xs, 4, ready=lambda h: pe.wait_ge(x_ready, 4))
            pe.wait_ge(proj_out, 2)
            for b in range(4):
                if b == 1:
                    stage_ready("ff")
                if b >= 2:
                    pe.wait_ge(f_relu, 4 * (b - 1))
                tiles_T(f"up{b}", ready=(lambda kt: stage_ready("ff", kt)) if b == 0 else None)
            pe.wait_ge(f_relu, 12)
            tiles("down", fT, ready=lambda kt: pe.wait_ge(f_ready, kt // 2 + 1))
            transposes("ple", xs, 4, ready=lambda h: pe.wait_ge(x_ready, 5 + h))
            tiles("gate2", hT, ready=lambda kt: stage_ready("ple", kt))


INPUTS = ["x", "positions", "attn_norm_w", "w_in", "b_gate", "mla_q_norm_w", "mla_w_uq", "mla_kv_norm_w", "mla_w_ukv",
          "mla_q_hnorm_w", "mla_k_hnorm_w", "diff_q_hnorm_w", "diff_k_hnorm_w", "diff_lambda", "diff_subln_w", "w_out",
          "ffn_norm_w", "router_w", "expert_w_gate", "expert_w_up", "expert_w_down", "p_2", "norm1_g_2", "w_in_2",
          "conv_w_2", "q_norm_g_2", "k_norm_g_2", "sgu_norm_g_2", "sgu_w_2", "sgu_b_2", "w_out_2", "norm2_g_2",
          "w_ff1_2", "w_ff2_2", "norm3_g_2", "w_ple_gate_2", "w_ple_proj_2"]


def kernel(**inputs):
    import numpy as np
    import concourse.bacc as bacc
    from concourse.bass_utils import run_bass_kernel_spmd

    nc = bacc.Bacc("TRN2", target_bir_lowering=False, num_devices=1)
    arrays, t = {}, {}
    for name in INPUTS:
        a = np.ascontiguousarray(inputs[name])
        arrays[f"in_{name}"] = a
        t[name] = nc.dram_tensor(f"in_{name}", a.shape, mybir.dt.from_np(a.dtype), kind="ExternalInput").ap()
    t["out"] = nc.dram_tensor("out_x", (1, T, D), F32, kind="ExternalOutput").ap()
    hybrid_blocks(nc, t)
    result = run_bass_kernel_spmd(nc, [arrays], core_ids=[0])
    return result.results[0]["out_x"]
```
